# Optimizing a Trainium2 kernel written in Bass

```python
import math
import jax, jax.numpy as jnp
from jax import lax
import numpy as np

D_MODEL = 1024
BATCH = 1
SEQ = 512
DEPTH = 2

HEAD_DIM = 64
N_DIFF_HEADS = 6
DIFF_QK_DIM = HEAD_DIM // 2
N_GQA_HEADS = 6
N_GQA_KV_HEADS = 2
GQA_GROUP = N_GQA_HEADS // N_GQA_KV_HEADS
N_MEM_HEADS = 4
N_MEM = 256
GRID_W = 64
Q_BLOCK = 128
ROPE_THETA = 10000.0
NORM_EPS = 1e-6

DIFF_W = N_DIFF_HEADS * HEAD_DIM
GQA_W = N_GQA_HEADS * HEAD_DIM
GQA_KV_W = N_GQA_KV_HEADS * HEAD_DIM
MEM_W = N_MEM_HEADS * HEAD_DIM
D_MIX = DIFF_W + GQA_W + MEM_W
IN_SIZES = [DIFF_W, DIFF_W, DIFF_W, DIFF_W, GQA_W, GQA_KV_W, GQA_KV_W, GQA_W, MEM_W, MEM_W]
D_IN = sum(IN_SIZES)
IN_OFFSETS = [int(v) for v in np.cumsum(IN_SIZES)[:-1]]


def rms_norm(x, g):
    xf = x.astype(jnp.float32)
    y = xf * lax.rsqrt(jnp.mean(xf * xf, axis=-1, keepdims=True) + NORM_EPS)
    return (y * g.astype(jnp.float32)).astype(x.dtype)

def rope_tables(pos, dim):
    inv = ROPE_THETA ** (-jnp.arange(0, dim, 2, dtype=jnp.float32) / dim)
    ang = pos.astype(jnp.float32)[:, None] * inv[None, :]
    return jnp.cos(ang), jnp.sin(ang)

def apply_rope(x, cos, sin):
    xf = x.astype(jnp.float32)
    half = xf.shape[-1] // 2
    x1, x2 = xf[..., :half], xf[..., half:]
    return jnp.concatenate([x1 * cos - x2 * sin, x2 * cos + x1 * sin], axis=-1).astype(x.dtype)

def apply_axial_rope(x, row_cs, col_cs):
    half = x.shape[-1] // 2
    return jnp.concatenate([apply_rope(x[..., :half], *row_cs),
                            apply_rope(x[..., half:], *col_cs)], axis=-1)

def diff_attention(q1, q2, k1, k2, v, lam):
    B, H, S, d = q1.shape
    nb = S // Q_BLOCK
    scale = d ** -0.5

    def blockify(q):
        return jnp.moveaxis(q.reshape(B, H, nb, Q_BLOCK, d), 2, 0)

    def one(qs):
        a, b = qs
        s1 = jnp.einsum('bhqd,bhkd->bhqk', a, k1).astype(jnp.float32) * scale
        s2 = jnp.einsum('bhqd,bhkd->bhqk', b, k2).astype(jnp.float32) * scale
        p = jax.nn.softmax(s1, axis=-1) - lam * jax.nn.softmax(s2, axis=-1)
        return jnp.einsum('bhqk,bhke->bhqe', p.astype(v.dtype), v)

    o = lax.map(one, (blockify(q1), blockify(q2)))
    return jnp.moveaxis(o, 0, 2).reshape(B, H, S, v.shape[-1])

def gqa_attention(q, k, v):
    B, Hk, G, S, d = q.shape
    nb = S // Q_BLOCK
    scale = d ** -0.5
    qb = jnp.moveaxis(q.reshape(B, Hk, G, nb, Q_BLOCK, d), 3, 0)

    def one(qblk):
        s = jnp.einsum('bhgqd,bhkd->bhgqk', qblk, k).astype(jnp.float32) * scale
        p = jax.nn.softmax(s, axis=-1)
        return jnp.einsum('bhgqk,bhkd->bhgqd', p.astype(v.dtype), v)

    o = lax.map(one, qb)
    return jnp.moveaxis(o, 0, 3).reshape(B, Hk, G, S, d)

def first_inputs(seed: int = 0) -> dict:
    key = jax.random.key(seed)
    ks = jax.random.split(key, 14)
    f32 = jnp.float32
    n = jax.random.normal
    return {
        "x": n(ks[0], (BATCH, SEQ, D_MODEL), f32),
        "mem": n(ks[1], (BATCH, N_MEM, D_MODEL), f32),
        "pre_norm": 1.0 + 0.02 * n(ks[2], (DEPTH, D_MODEL), f32),
        "w_in": n(ks[3], (DEPTH, D_MODEL, D_IN), f32) * D_MODEL ** -0.5,
        "diff_lambda": 0.1 * n(ks[4], (DEPTH, 4, DIFF_QK_DIM), f32),
        "diff_subln": 1.0 + 0.02 * n(ks[5], (DEPTH, HEAD_DIM), f32),
        "gqa_q_norm": 1.0 + 0.02 * n(ks[6], (DEPTH, HEAD_DIM), f32),
        "gqa_k_norm": 1.0 + 0.02 * n(ks[7], (DEPTH, HEAD_DIM), f32),
        "mem_norm": 1.0 + 0.02 * n(ks[8], (DEPTH, D_MODEL), f32),
        "w_mem_kv": n(ks[9], (DEPTH, D_MODEL, 2 * MEM_W), f32) * D_MODEL ** -0.5,
        "w_out": n(ks[10], (DEPTH, D_MIX, D_MODEL), f32) * D_MIX ** -0.5,
        "post_norm": 1.0 + 0.02 * n(ks[11], (DEPTH, D_MODEL), f32),
    }

def first_block(x, mem, pre_norm, w_in, diff_lambda, diff_subln, gqa_q_norm, gqa_k_norm,
              mem_norm, w_mem_kv, w_out, post_norm):
    B, S, _ = x.shape
    M = mem.shape[1]
    ROWS = S // GRID_W
    t = jnp.arange(S, dtype=jnp.int32)
    row = jnp.repeat(jnp.arange(ROWS, dtype=jnp.int32), GRID_W)
    col = jnp.tile(jnp.arange(GRID_W, dtype=jnp.int32), ROWS)
    lin_cs = rope_tables(t, DIFF_QK_DIM)
    row_cs = rope_tables(row, HEAD_DIM // 2)
    col_cs = rope_tables(col, HEAD_DIM // 2)

    for l in range(DEPTH):
        lambda_init = 0.8 - 0.6 * math.exp(-0.3 * l)
        h = rms_norm(x, pre_norm[l])
        proj = h @ w_in[l]
        (dq, dk, dv, dgate, gq, gk, gv, ggate, mq, mgate) = jnp.split(proj, IN_OFFSETS, axis=-1)

        dq = apply_rope(dq.reshape(B, S, N_DIFF_HEADS, 2, DIFF_QK_DIM).transpose(0, 2, 3, 1, 4), *lin_cs)
        dk = apply_rope(dk.reshape(B, S, N_DIFF_HEADS, 2, DIFF_QK_DIM).transpose(0, 2, 3, 1, 4), *lin_cs)
        dv = dv.reshape(B, S, N_DIFF_HEADS, HEAD_DIM).transpose(0, 2, 1, 3)
        lp = diff_lambda[l].astype(jnp.float32)
        lam = jnp.exp(jnp.sum(lp[0] * lp[1])) - jnp.exp(jnp.sum(lp[2] * lp[3])) + lambda_init
        oa = diff_attention(dq[:, :, 0], dq[:, :, 1], dk[:, :, 0], dk[:, :, 1], dv, lam)
        oa = rms_norm(oa, diff_subln[l]) * (1.0 - lambda_init)
        oa = oa.transpose(0, 2, 1, 3).reshape(B, S, DIFF_W) * jax.nn.silu(dgate)

        gq = rms_norm(gq.reshape(B, S, N_GQA_HEADS, HEAD_DIM).transpose(0, 2, 1, 3), gqa_q_norm[l])
        gq = apply_axial_rope(gq, row_cs, col_cs).reshape(B, N_GQA_KV_HEADS, GQA_GROUP, S, HEAD_DIM)
        gk = rms_norm(gk.reshape(B, S, N_GQA_KV_HEADS, HEAD_DIM).transpose(0, 2, 1, 3), gqa_k_norm[l])
        gk = apply_axial_rope(gk, row_cs, col_cs)
        gv = gv.reshape(B, S, N_GQA_KV_HEADS, HEAD_DIM).transpose(0, 2, 1, 3)
        ob = gqa_attention(gq, gk, gv).reshape(B, N_GQA_HEADS, S, HEAD_DIM)
        ob = ob.transpose(0, 2, 1, 3).reshape(B, S, GQA_W) * jax.nn.silu(ggate)

        mkv = rms_norm(mem, mem_norm[l]) @ w_mem_kv[l]
        mk, mv = jnp.split(mkv, 2, axis=-1)
        mk = mk.reshape(B, M, N_MEM_HEADS, HEAD_DIM).transpose(0, 2, 1, 3)
        mv = mv.reshape(B, M, N_MEM_HEADS, HEAD_DIM).transpose(0, 2, 1, 3)
        mq = mq.reshape(B, S, N_MEM_HEADS, HEAD_DIM).transpose(0, 2, 1, 3)
        sm = jnp.einsum('bhsd,bhmd->bhsm', mq, mk).astype(jnp.float32) * HEAD_DIM ** -0.5
        pm = jax.nn.softmax(sm, axis=-1)
        om = jnp.einsum('bhsm,bhmd->bhsd', pm.astype(mv.dtype), mv)
        om = om.transpose(0, 2, 1, 3).reshape(B, S, MEM_W) * jax.nn.silu(mgate)

        y = jnp.concatenate([oa, ob, om], axis=-1) @ w_out[l]
        x = x + rms_norm(y, post_norm[l])
    return x


N_MIXERS = 4
D_FF = 2816
EPS = 1e-6
S5_GROUP = 16
S5_GROUPS = D_MODEL // S5_GROUP
S5_STATE = 64
DT_MIN = 1e-3
DT_MAX = 1e-1
CONV_W = 31
GM_CHUNK = 128
GM_E = 2 * D_MODEL
GM_HEADS = 8
AT_HEADS = D_MODEL // HEAD_DIM
PATTERNS = ((128, 1), (512, 4), (2048, 16))
N_PATTERNS = len(PATTERNS)
BLOCK = 128
NUM_BUCKETS = 32
MAX_DISTANCE = 2048


def rmsnorm(x, g):
    xf = x.astype(jnp.float32)
    y = xf * lax.rsqrt(jnp.mean(xf * xf, axis=-1, keepdims=True) + EPS)
    return (y * g.astype(jnp.float32)).astype(x.dtype)

def layernorm(x, g, b):
    xf = x.astype(jnp.float32)
    mu = jnp.mean(xf, axis=-1, keepdims=True)
    var = jnp.mean(jnp.square(xf - mu), axis=-1, keepdims=True)
    y = (xf - mu) * lax.rsqrt(var + EPS)
    return (y * g.astype(jnp.float32) + b.astype(jnp.float32)).astype(x.dtype)

def swiglu(h, w1, w3, w2):
    return (jax.nn.silu(h @ w1) * (h @ w3)) @ w2

def _complex_scan_op(left, right):
    a1r, a1i, b1r, b1i = left
    a2r, a2i, b2r, b2i = right
    return (a2r * a1r - a2i * a1i,
            a2r * a1i + a2i * a1r,
            a2r * b1r - a2i * b1i + b2r,
            a2r * b1i + a2i * b1r + b2i)

def s5_mixer(h, w_in, a_re, a_im, log_dt, b_re, b_im, c_re, c_im, d_skip, w_glu, b_glu, w_out):
    bsz, seq, _ = h.shape
    u = (h @ w_in).astype(jnp.float32).reshape(bsz, seq, S5_GROUPS, S5_GROUP)
    ar = a_re.astype(jnp.float32)
    ai = a_im.astype(jnp.float32)
    dt = jnp.exp(log_dt.astype(jnp.float32))[:, None]
    mag = jnp.exp(dt * ar)
    abar_re = mag * jnp.cos(dt * ai)
    abar_im = mag * jnp.sin(dt * ai)
    den = ar * ar + ai * ai
    nr = abar_re - 1.0
    f_re = (nr * ar + abar_im * ai) / den
    f_im = (abar_im * ar - nr * ai) / den
    br = b_re.astype(jnp.float32)
    bi = b_im.astype(jnp.float32)
    bb_re = f_re[..., None] * br - f_im[..., None] * bi
    bb_im = f_re[..., None] * bi + f_im[..., None] * br
    bu_re = jnp.einsum('blgh,gph->blgp', u, bb_re)
    bu_im = jnp.einsum('blgh,gph->blgp', u, bb_im)
    elems = (jnp.broadcast_to(abar_re, bu_re.shape), jnp.broadcast_to(abar_im, bu_re.shape), bu_re, bu_im)
    _, _, st_re, st_im = lax.associative_scan(_complex_scan_op, elems, axis=1)
    y = (jnp.einsum('blgp,ghp->blgh', st_re, c_re.astype(jnp.float32))
         - jnp.einsum('blgp,ghp->blgh', st_im, c_im.astype(jnp.float32))
         + d_skip.astype(jnp.float32).reshape(S5_GROUPS, S5_GROUP) * u)
    y = jax.nn.gelu(y.reshape(bsz, seq, D_MODEL)).astype(h.dtype)
    z = y * jax.nn.sigmoid(y @ w_glu + b_glu)
    return z @ w_out

def conv_mixer(h, w_in, b_in, dw, dw_b, ln_g, ln_b, w_out, b_out):
    z = h @ w_in + b_in
    a, g = jnp.split(z, 2, axis=-1)
    z = a * jax.nn.sigmoid(g)
    z = lax.conv_general_dilated(z, dw[:, None, :].astype(z.dtype), window_strides=(1,),
                                 padding=[(CONV_W - 1, 0)],
                                 dimension_numbers=('NWC', 'WIO', 'NWC'),
                                 feature_group_count=D_MODEL) + dw_b
    z = jax.nn.silu(layernorm(z, ln_g, ln_b))
    return z @ w_out + b_out

def gmlp_mixer(h, w_in, b_in, ln_g, ln_b, w_s, b_s, w_out, b_out):
    bsz, seq, _ = h.shape
    z = jax.nn.gelu(h @ w_in + b_in)
    u, v = jnp.split(z, 2, axis=-1)
    v = layernorm(v, ln_g, ln_b)
    vc = v.reshape(bsz, seq // GM_CHUNK, GM_CHUNK, GM_HEADS, GM_E // GM_HEADS)
    causal = jnp.tril(jnp.ones((GM_CHUNK, GM_CHUNK), jnp.float32))
    s = jnp.einsum('hts,bnshc->bnthc', w_s * causal, vc) + b_s.T[None, None, :, :, None]
    s = s.reshape(bsz, seq, GM_E).astype(u.dtype)
    return (u * s) @ w_out + b_out

def t5_bucket(dist):
    max_exact = NUM_BUCKETS // 2
    distf = jnp.maximum(dist, 1).astype(jnp.float32)
    large = max_exact + (jnp.log(distf / max_exact) / math.log(MAX_DISTANCE / max_exact)
                         * (NUM_BUCKETS - max_exact)).astype(jnp.int32)
    large = jnp.minimum(large, NUM_BUCKETS - 1)
    return jnp.where(dist < max_exact, dist, large)

def _band_delta():
    return (jnp.arange(BLOCK)[:, None] + BLOCK) - jnp.arange(2 * BLOCK)[None, :]

def rel_bias_block(table, dilation):
    dist = jnp.maximum(_band_delta(), 0) * dilation
    return table.astype(jnp.float32)[t5_bucket(dist)].transpose(2, 0, 1)

def dilated_window_attention(q, k, v, bias, window, dilation):
    bsz, seq, heads, hd = q.shape
    span = BLOCK * dilation
    seq_p = -(-seq // span) * span
    n_sub = seq_p // dilation
    n_blk = n_sub // BLOCK

    def to_blocks(t):
        t = jnp.pad(t.astype(jnp.float32), ((0, 0), (0, seq_p - seq), (0, 0), (0, 0)))
        t = t.reshape(bsz, n_sub, dilation, heads, hd).transpose(0, 2, 1, 3, 4)
        return t.reshape(bsz, dilation, n_blk, BLOCK, heads, hd)

    def with_prev(t):
        prev = jnp.pad(t, ((0, 0), (0, 0), (1, 0), (0, 0), (0, 0), (0, 0)))[:, :, :-1]
        return jnp.concatenate([prev, t], axis=3)

    qb = to_blocks(q)
    kk = with_prev(to_blocks(k))
    vv = with_prev(to_blocks(v))
    logits = jnp.einsum('brnqhd,brnkhd->brnhqk', qb, kk) * (hd ** -0.5) + bias[None, None, None]
    delta = _band_delta()
    in_band = (delta >= 0) & (delta <= window // dilation)
    not_before_start = (jnp.arange(n_blk)[:, None, None] > 0) | (jnp.arange(2 * BLOCK) >= BLOCK)[None, None, :]
    mask = in_band[None] & not_before_start
    logits = jnp.where(mask[None, None, :, None], logits, -jnp.inf)
    m = jnp.max(logits, axis=-1, keepdims=True)
    p = jnp.exp(logits - m)
    den = jnp.sum(p, axis=-1)
    o = jnp.einsum('brnhqk,brnkhd->brnqhd', p, vv) / jnp.swapaxes(den, -1, -2)[..., None]
    lse = jnp.swapaxes(m[..., 0] + jnp.log(den), -1, -2)
    o = o.reshape(bsz, dilation, n_sub, heads, hd).transpose(0, 2, 1, 3, 4).reshape(bsz, seq_p, heads, hd)[:, :seq]
    lse = lse.reshape(bsz, dilation, n_sub, heads).transpose(0, 2, 1, 3).reshape(bsz, seq_p, heads)[:, :seq]
    return o, lse

def attention_mixer(h, w_qkv, w_out, rel_bias):
    bsz, seq, _ = h.shape
    qkv = (h @ w_qkv).reshape(bsz, seq, N_PATTERNS, 3, AT_HEADS, HEAD_DIM)
    outs, lses = [], []
    for g, (window, dilation) in enumerate(PATTERNS):
        bias = rel_bias_block(rel_bias[:, g * AT_HEADS:(g + 1) * AT_HEADS], dilation)
        o, lse = dilated_window_attention(qkv[:, :, g, 0], qkv[:, :, g, 1], qkv[:, :, g, 2], bias, window, dilation)
        outs.append(o)
        lses.append(lse)
    wts = jax.nn.softmax(jnp.stack(lses, axis=0), axis=0)
    o = jnp.sum(wts[..., None] * jnp.stack(outs, axis=0), axis=0)
    return o.reshape(bsz, seq, AT_HEADS * HEAD_DIM).astype(h.dtype) @ w_out

def _count(kind):
    return len(range(kind, DEPTH, N_MIXERS))

def second_inputs(seed: int = 0) -> dict:
    key = jax.random.key(seed)
    ks = iter(jax.random.split(key, 48))

    def nrm(shape, scale):
        return scale * jax.random.normal(next(ks), shape, jnp.float32)

    na, nb, nc, nd = _count(0), _count(1), _count(2), _count(3)
    D, F, G, P, HG, E = D_MODEL, D_FF, S5_GROUPS, S5_STATE, S5_GROUP, GM_E
    return {
        "x": nrm((BATCH, SEQ, D), 1.0),
        "norm_pre": 1.0 + nrm((DEPTH, 3, D), 0.05),
        "norm_post": 1.0 + nrm((DEPTH, 3, D), 0.05),
        "ffn_w1": nrm((DEPTH, 2, D, F), D ** -0.5),
        "ffn_w3": nrm((DEPTH, 2, D, F), D ** -0.5),
        "ffn_w2": nrm((DEPTH, 2, F, D), F ** -0.5),
        "rel_bias": nrm((NUM_BUCKETS, N_PATTERNS * AT_HEADS), 0.5),
        "s5_w_in": nrm((na, D, D), D ** -0.5),
        "s5_a_re": -0.5 + nrm((na, G, P), 0.01),
        "s5_a_im": jnp.pi * jnp.arange(P, dtype=jnp.float32) + nrm((na, G, P), 0.01),
        "s5_log_dt": jax.random.uniform(next(ks), (na, G), jnp.float32, math.log(DT_MIN), math.log(DT_MAX)),
        "s5_b_re": nrm((na, G, P, HG), (2 * HG) ** -0.5),
        "s5_b_im": nrm((na, G, P, HG), (2 * HG) ** -0.5),
        "s5_c_re": nrm((na, G, HG, P), (2 * P) ** -0.5),
        "s5_c_im": nrm((na, G, HG, P), (2 * P) ** -0.5),
        "s5_d": nrm((na, D), 1.0),
        "s5_w_glu": nrm((na, D, D), D ** -0.5),
        "s5_b_glu": nrm((na, D), 0.01),
        "s5_w_out": nrm((na, D, D), D ** -0.5),
        "cv_w_in": nrm((nb, D, 2 * D), D ** -0.5),
        "cv_b_in": nrm((nb, 2 * D), 0.01),
        "cv_dw": nrm((nb, CONV_W, D), CONV_W ** -0.5),
        "cv_dw_b": nrm((nb, D), 0.01),
        "cv_ln_g": 1.0 + nrm((nb, D), 0.05),
        "cv_ln_b": nrm((nb, D), 0.01),
        "cv_w_out": nrm((nb, D, D), D ** -0.5),
        "cv_b_out": nrm((nb, D), 0.01),
        "gm_w_in": nrm((nc, D, 2 * E), D ** -0.5),
        "gm_b_in": nrm((nc, 2 * E), 0.01),
        "gm_ln_g": 1.0 + nrm((nc, E), 0.05),
        "gm_ln_b": nrm((nc, E), 0.01),
        "gm_w_s": nrm((nc, GM_HEADS, GM_CHUNK, GM_CHUNK), GM_CHUNK ** -0.5),
        "gm_b_s": 1.0 + nrm((nc, GM_HEADS, GM_CHUNK), 0.01),
        "gm_w_out": nrm((nc, E, D), E ** -0.5),
        "gm_b_out": nrm((nc, D), 0.01),
        "at_w_qkv": nrm((nd, D, N_PATTERNS * 3 * AT_HEADS * HEAD_DIM), D ** -0.5),
        "at_w_out": nrm((nd, AT_HEADS * HEAD_DIM, D), (AT_HEADS * HEAD_DIM) ** -0.5),
    }

def second_block(x, norm_pre, norm_post, ffn_w1, ffn_w3, ffn_w2, rel_bias,
              s5_w_in, s5_a_re, s5_a_im, s5_log_dt, s5_b_re, s5_b_im, s5_c_re, s5_c_im,
              s5_d, s5_w_glu, s5_b_glu, s5_w_out,
              cv_w_in, cv_b_in, cv_dw, cv_dw_b, cv_ln_g, cv_ln_b, cv_w_out, cv_b_out,
              gm_w_in, gm_b_in, gm_ln_g, gm_ln_b, gm_w_s, gm_b_s, gm_w_out, gm_b_out,
              at_w_qkv, at_w_out):
    for i in range(DEPTH):
        kind, j = i % N_MIXERS, i // N_MIXERS
        h = swiglu(rmsnorm(x, norm_pre[i, 0]), ffn_w1[i, 0], ffn_w3[i, 0], ffn_w2[i, 0])
        x = x + 0.5 * rmsnorm(h, norm_post[i, 0])
        h = rmsnorm(x, norm_pre[i, 1])
        if kind == 0:
            h = s5_mixer(h, s5_w_in[j], s5_a_re[j], s5_a_im[j], s5_log_dt[j], s5_b_re[j], s5_b_im[j],
                         s5_c_re[j], s5_c_im[j], s5_d[j], s5_w_glu[j], s5_b_glu[j], s5_w_out[j])
        elif kind == 1:
            h = conv_mixer(h, cv_w_in[j], cv_b_in[j], cv_dw[j], cv_dw_b[j], cv_ln_g[j], cv_ln_b[j],
                           cv_w_out[j], cv_b_out[j])
        elif kind == 2:
            h = gmlp_mixer(h, gm_w_in[j], gm_b_in[j], gm_ln_g[j], gm_ln_b[j], gm_w_s[j], gm_b_s[j],
                           gm_w_out[j], gm_b_out[j])
        else:
            h = attention_mixer(h, at_w_qkv[j], at_w_out[j], rel_bias)
        x = x + rmsnorm(h, norm_post[i, 1])
        h = swiglu(rmsnorm(x, norm_pre[i, 2]), ffn_w1[i, 1], ffn_w3[i, 1], ffn_w2[i, 1])
        x = x + 0.5 * rmsnorm(h, norm_post[i, 2])
    return x


def setup_inputs(seed=0):
    out = dict(first_inputs(seed))
    for name, value in second_inputs(seed + 1).items():
        if name != "x":
            out[name + "_2"] = value
    return out


def reference(
    x, mem, pre_norm, w_in, diff_lambda, diff_subln, gqa_q_norm, gqa_k_norm, mem_norm, w_mem_kv,
    w_out, post_norm, norm_pre_2, norm_post_2, ffn_w1_2, ffn_w3_2, ffn_w2_2, rel_bias_2,
    s5_w_in_2, s5_a_re_2, s5_a_im_2, s5_log_dt_2, s5_b_re_2, s5_b_im_2, s5_c_re_2, s5_c_im_2,
    s5_d_2, s5_w_glu_2, s5_b_glu_2, s5_w_out_2, cv_w_in_2, cv_b_in_2, cv_dw_2, cv_dw_b_2,
    cv_ln_g_2, cv_ln_b_2, cv_w_out_2, cv_b_out_2, gm_w_in_2, gm_b_in_2, gm_ln_g_2, gm_ln_b_2,
    gm_w_s_2, gm_b_s_2, gm_w_out_2, gm_b_out_2, at_w_qkv_2, at_w_out_2,
):
    x = first_block(
        x, mem, pre_norm, w_in, diff_lambda, diff_subln, gqa_q_norm, gqa_k_norm, mem_norm,
        w_mem_kv, w_out, post_norm,
    )
    return second_block(
        x, norm_pre_2, norm_post_2, ffn_w1_2, ffn_w3_2, ffn_w2_2, rel_bias_2, s5_w_in_2,
        s5_a_re_2, s5_a_im_2, s5_log_dt_2, s5_b_re_2, s5_b_im_2, s5_c_re_2, s5_c_im_2, s5_d_2,
        s5_w_glu_2, s5_b_glu_2, s5_w_out_2, cv_w_in_2, cv_b_in_2, cv_dw_2, cv_dw_b_2, cv_ln_g_2,
        cv_ln_b_2, cv_w_out_2, cv_b_out_2, gm_w_in_2, gm_b_in_2, gm_ln_g_2, gm_ln_b_2, gm_w_s_2,
        gm_b_s_2, gm_w_out_2, gm_b_out_2, at_w_qkv_2, at_w_out_2,
    )


_drawn_inputs = setup_inputs


def setup_inputs(seed=0):
    import zlib

    import numpy as np

    out = dict(_drawn_inputs(seed))
    spreads = {}
    factors = {'gqa_q_norm': 8.0,
     'gqa_k_norm': 8.0,
     'mem_norm': 8.0,
     's5_a_re_2': 200.0,
     's5_b_glu_2': 24.809,
     'cv_b_in_2': 8.0,
     'cv_dw_b_2': 6.848,
     'cv_ln_b_2': 8.0,
     'cv_b_out_2': 7.793,
     'diff_lambda': 4.411,
     'diff_subln': 8.0,
     's5_a_im_2': 38.928,
     's5_log_dt_2': 41.472,
     's5_b_re_2': 54.216,
     's5_b_im_2': 53.84,
     's5_c_re_2': 53.992,
     's5_c_im_2': 53.744}
    for name, (base, spread) in spreads.items():
        noise = np.random.default_rng([zlib.crc32(name.encode()), seed]).standard_normal(out[name].shape)
        drawn = base * np.exp(spread * noise) if base else spread * noise
        out[name] = __import__('jax').numpy.asarray(drawn.astype(out[name].dtype))
    for name, factor in factors.items():
        out[name] = (out[name] * factor).astype(out[name].dtype)
    return out
```

```python
import math
from contextlib import ExitStack

import numpy as np
import concourse.bass as bass
from concourse import mybir

ALU = mybir.AluOpType
ACT = mybir.ActivationFunctionType
F32 = mybir.dt.float32
F32R = mybir.dt.float32r
AX = mybir.AxisListType.X

P = 128
T = 512
D = 1024
KD = D // P
FF = 2816
KF = FF // P
EPS = 1e-6
CONV_W = 31
CONV_PAD = CONV_W - 1
GROUPS, GCH, STATES = 64, 16, 64
CL = 8
NC = T // CL
GS = 8
PI2 = 2 * math.pi
PI2_A = 6.28125
PI2_B = round((PI2 - PI2_A) * 2 ** 20) / 2 ** 20
PI2_C = PI2 - PI2_A - PI2_B
TURN = 6.283185
ROUND = 1.5 * 2 ** 23
NMEM = 256
GRID_W = 64
ROPE_DIM = 32

LAMBDA0 = [0.8 - 0.6 * math.exp(-0.3 * l) for l in range(2)]

FULL = ["attn0", "attn1", "ffn0", "s5", "ffn1", "ffn2", "conv", "ffn3"]


def block_plan(stages):
    plan, sizes = {}, []
    for s in stages:
        plan[s] = len(sizes)
        if s.startswith("attn"):
            sizes += [16] * (2 + 12 + 4)
        elif s.startswith("ffn"):
            sizes += [16] * (FF // 128) + [11] * (2 * KD)
        elif s == "s5":
            sizes += [16] * 12
        elif s == "conv":
            sizes += [16] * 12
    return plan, sizes


S5_JC = CL + 1
S5_EYE = S5_JC + NC + 1
S5_SGN = S5_EYE + P + (CL - 1) * GCH
S5_SWAP = S5_SGN + 3
S5_COLS = S5_SWAP + P


def shape_tables():
    inv = (np.float32(10000.0) ** (-np.arange(0, ROPE_DIM, 2, dtype=np.float32) / np.float32(ROPE_DIM))).astype(np.float32)
    t = np.arange(T)
    p = np.arange(P)
    sign = np.where(p % ROPE_DIM < 16, -1.0, 1.0).astype(np.float32)[:, None]
    linear = t[None, :] * np.ones((P, 1), np.int64)
    axial = np.where((p % 64 < 32)[:, None], t[None, :] // GRID_W, t[None, :] % GRID_W)
    out = np.zeros((P, 4, T), np.float32)
    for n, pos in enumerate((linear, axial)):
        ang = pos.astype(np.float32) * inv[p % 16][:, None]
        out[:, 2 * n] = np.cos(ang)
        out[:, 2 * n + 1] = sign * np.sin(ang)
    perm = np.zeros((P, 2, P), np.float32)
    perm[p ^ 16, 0, p] = 1.0
    perm[:, 1] = (p[:, None] // 64 == p[None, :] // 64)
    s5 = np.zeros((P, S5_COLS), np.float32)
    s5[:, 0:CL + 1] = np.arange(CL + 1)
    s5[:, S5_JC:S5_JC + NC + 1] = CL * np.arange(NC + 1)
    s5[p, S5_EYE + p + (CL - 1) * GCH] = 1.0
    s5[:, S5_SGN] = np.where(p < 64, -1.0, 1.0)
    s5[:, S5_SGN + 1] = -s5[:, S5_SGN]
    s5[:, S5_SGN + 2] = TURN * s5[:, S5_SGN + 1]
    s5[p, S5_SWAP + (p ^ 64)] = 1.0
    return {"rope_c": out, "perm_c": perm, "s5_c": s5}


def program(nc, io, stages=FULL):
    ctx = ExitStack()
    with ctx:
        def sb(name, shape, dt=F32, stack=ctx):
            return stack.enter_context(nc.sbuf_tensor(name, shape, dt))

        def sem(name):
            return ctx.enter_context(nc.semaphore(name))

        first_block, cells = block_plan(stages)

        X = sb("X", [P, KD, T])
        rstd = sb("rstd", [P, T])
        rms = sb("rms", [P, T])
        raw = sb("raw", [P, 2, 2048])
        WH = sb("WH", [P, 2, 2048], F32R)
        WL = sb("WL", [P, 2, 2048], F32R)
        ident = sb("ident", [P, P])
        ones = sb("ones", [P, P])
        eps_c = sb("eps_c", [P, 1])
        vecT = sb("vecT", [P, 256])
        dwT = sb("dwT", [P, CONV_W * KD])
        lamb = sb("lamb", [P, 2, P])
        lamv = sb("lamv", [P, 2, 4])
        nlam = sb("nlam", [P, 2])
        headg = sb("headg", [P, 6])
        sq = sb("sq", [P, 2, T])
        ssq = sb("ssq", [P, T])
        work1 = sb("work1", [P, 2, T])
        work2 = sb("work2", [P, 2, T])

        ra = ExitStack()
        XH = sb("XH", [P, KD, T], F32R, ra)
        XL = sb("XL", [P, KD, T], F32R, ra)
        ra.close()
        ra = ExitStack()
        YA = sb("YA", [P, KD, T], F32, ra)
        ra.close()

        ra = ExitStack()
        VdH = sb("VdH", [P, 4, 384], F32R, ra)
        VdL = sb("VdL", [P, 4, 384], F32R, ra)
        VgH = sb("VgH", [P, 4, 2, P], F32R, ra)
        VgL = sb("VgL", [P, 4, 2, P], F32R, ra)
        rope = sb("rope", [P, 4, T], F32, ra)
        ra.close()

        ra = ExitStack()
        YR = sb("YR", [P, KD, CL, NC], F32, ra)
        ra.close()

        sb("region_a", [P, 2 * KD, T])

        rb = ExitStack()
        HH = sb("HH", [P, KF, T], F32R, rb)
        HL = sb("HL", [P, KF, T], F32R, rb)
        rb.close()
        rb = ExitStack()
        XN = sb("XN", [P, 4, D], F32, rb)
        vrow = sb("vrow", [P, 4, P], F32, rb)
        lamrow = sb("lamrow", [1, 2, P], F32, rb)
        rb.close()
        rb = ExitStack()
        perm = sb("perm", [P, 2, P], F32, rb)
        PR = sb("PR", [P, 24, T], F32, rb)
        gk2 = sb("gk2", [P, T], F32, rb)
        MK = sb("MK", [P, 2, NMEM], F32, rb)
        VmH = sb("VmH", [P, 2, 256], F32R, rb)
        VmL = sb("VmL", [P, 2, 256], F32R, rb)
        stats = sb("stats", [P, 4, 8], F32, rb)
        rb2 = ExitStack()
        E = sb("E", [P, 2, 2, T], F32, rb2)
        PTH = sb("PTH", [P, 4, T], F32R, rb2)
        PTL = sb("PTL", [P, 4, T], F32R, rb2)
        rb2.close()
        MEMN = sb("MEMN", [P, 2, D], F32, rb)
        MH = sb("MH", [P, KD, NMEM], F32R, rb)
        ML = sb("ML", [P, KD, NMEM], F32R, rb)
        rb.close()
        rb = ExitStack()
        ZP = sb("ZP", [P, KD, CONV_PAD + T], F32, rb)
        CV = sb("CV", [P, KD, T], F32, rb)
        SG = sb("SG", [P, 2, T], F32, rb)
        YC = sb("YC", [P, KD, T], F32, rb)
        rb.close()

        rb = ExitStack()
        UN = sb("UN", [P, KD, T], F32, rb)
        rb2 = ExitStack()
        s5c = sb("s5c", [P, S5_COLS], F32, rb2)
        sm = sb("sm", [P, 20, GROUPS], F32, rb2)
        CSJ = sb("CSJ", [P, CL + 1, GROUPS], F32, rb2)
        SNJ = sb("SNJ", [P, CL + 1, GROUPS], F32, rb2)
        B1 = sb("B1", [P, GROUPS, GCH], F32, rb2)
        B2 = sb("B2", [P, GROUPS, GCH], F32, rb2)
        C1 = sb("C1", [P, GROUPS, GCH], F32, rb2)
        C2 = sb("C2", [P, GROUPS, GCH], F32, rb2)
        Wt = sb("Wt", [P, GS, CL, GCH], F32, rb2)
        W1 = sb("W1", [P, GS, 192], F32, rb2)
        Wx = sb("Wx", [P, 4, CL, GCH], F32, rb2)
        G1 = sb("G1", [P, GS, CL, GCH], F32, rb2)
        Gx = sb("Gx", [P, 4, CL, GCH], F32, rb2)
        MT = sb("MT", [P, GS, CL, GCH], F32, rb2)
        COS = sb("COS", [P, 2, GS, NC + 1], F32, rb2)
        SIN = sb("SIN", [P, 2, GS, NC + 1], F32, rb2)
        PHA = sb("PHA", [P, GS, NC + 1], F32, rb2)
        PHN = sb("PHN", [P, GS, NC + 1], F32, rb2)
        U = sb("U", [P, 2, GS, NC], F32, rb2)
        YS = sb("YS", [P, GS, NC], F32, rb2)
        RR = sb("RR", [P, GS, NC], F32, rb2)
        KS = sb("KS", [P, GS, GCH], F32, rb2)
        rb2.close()
        Y5 = sb("Y5", [P, KD, T], F32, rb)
        rb.close()
        u_scr = nc.dram_tensor("u_scr", [KD, P, GS, NC], F32).ap()
        y_scr = nc.dram_tensor("y_scr", [KD, P, CL, NC], F32).ap()

        bank = [ctx.enter_context(nc.psum_tensor(f"bank{i}", [P, T], F32)) for i in range(8)]
        stat = bank[7]

        raw_in = [sem("raw_in0"), sem("raw_in1")]
        h_done = sem("h_done")
        l_done = sem("l_done")
        mm_done = sem("mm_done")
        acc_read = sem("acc_read")
        lam_exp = sem("lam_exp")
        perm_in = sem("perm_in")
        vec_in = sem("vec_in")
        vec_t = sem("vec_t")
        vec_ok = sem("vec_ok")
        ident_0 = sem("ident_0")
        ident_ok = sem("ident_ok")
        xn_in = sem("xn_in")
        x_tr = sem("x_tr")
        x_ok = sem("x_ok")
        o_tr = sem("o_tr")
        o_cp = sem("o_cp")
        stored = sem("stored")

        VEC_ROWS = [
            [("pre_norm", 16), ("post_norm", 16), ("mem_norm", 16), ("norm_pre_2", 48), ("s5_d_2", 8),
             ("s5_b_glu_2", 8), ("cv_dw_b_2", 8)],
            [("norm_post_2", 48), ("cv_b_in_2", 16), ("cv_ln_g_2", 8), ("cv_ln_b_2", 8), ("cv_b_out_2", 8)],
        ]
        VEC_ROW1 = sum(r for _, r in VEC_ROWS[1])
        COL = {}
        for n, group in enumerate(VEC_ROWS):
            row = 128 * n
            for name, rows in group:
                COL[name] = row
                row += rows
        HEAD_ROWS = [("diff_subln", VEC_ROW1), ("gqa_q_norm", VEC_ROW1 + 2), ("gqa_k_norm", VEC_ROW1 + 4)]
        VEC_DMAS = sum(len(g) for g in VEC_ROWS) + 2 + 6 + 1
        DW_ROWS = CONV_W * KD // 2
        VEC_N = [sum(r for _, r in VEC_ROWS[0]), VEC_ROW1 + 6]

        def col(name, k, n=0):
            c = COL[name] + KD * n + k
            return vecT[:, c:c + 1]

        ADDS = {
            "all": dict(xh=KD, xl=KD, sq_in=KD, sq_use=KD, stat_ok=1, rms_ok=1, ysq_in=KD, ysq_use=KD, ystat_ok=1,
                        yrms_ok=1, t_ok=KD, x_new=KD),
            "ffn": dict(silu=KF, hid=KF, hh=KF, hl=KF),
            "attn": dict(mem_in=16, perm_in=16, rope_in=16, mem_n=2, ml=KD, mem_t=KD, mh=KD, mrms=1, msq=2, vm_t=1, vmh=1,
                         v_t=4, vh=4, vl=4, gsq=4, gms=4, grms=4, gn=4, swapped=10, roped=10, ready=1, gate=8,
                         s=88, e=88, nb=64, p=64, pt=64, pth=64, ptl=64, pv=16, o=16, osq=3, oms=3, orms=3, on=3, og=3,
                         mixh=KD, mixl=KD),
        }
        sems = {}

        def kind(s):
            return s if s == "s5" else s.rstrip("0123")

        def shared_by(s, name):
            return "all" if name in ADDS["all"] else kind(s)

        def ss(s, name):
            key = f"{shared_by(s, name)}_{name}"
            if key not in sems:
                sems[key] = sem(key)
            return sems[key]

        def at(s, name, n):
            who = shared_by(s, name)
            before = [x for x in stages[:stages.index(s)] if who == "all" or kind(x) == who]
            return n + (len(before) * ADDS[who][name] if before else 0)

        tiles_before, first_step, n_tiles, n_steps = {}, {}, 0, 0
        for s in stages:
            tiles_before[s], first_step[s] = n_tiles, n_steps
            n_tiles += {"attn": 4 + 24 + 8, "ffn": 2 * KF + KD, "s5": 24, "conv": 24}[kind(s)]
            n_steps += {"attn": 4 + 24 + 8, "ffn": 2 * KF + 2 * KD, "s5": 24, "conv": 24}[kind(s)]

        def split_h(act, b, slot, n, used):
            act.wait_ge(raw_in[slot], (b - slot) * 8 + 16)
            if not isinstance(b, int) or b >= 2:
                act.wait_ge(mm_done, used)
            act.activation(WH[:, slot, 0:n * P], raw[:, slot, 0:n * P], ACT.Copy).then_inc(h_done, 1)

        def split_l(dve, b, slot, n):
            dve.wait_ge(h_done, b + 1)
            dve.tensor_tensor(WL[:, slot, 0:n * P], raw[:, slot, 0:n * P], WH[:, slot, 0:n * P].bitcast(F32),
                              ALU.subtract).then_inc(l_done, 1)

        def load_block(sp, b, slot, dst, src):
            if not isinstance(b, int) or b >= 2:
                sp.wait_ge(l_done, b - 1)
            sp.dma_start(dst, src).then_inc(raw_in[slot], 16)

        def raw3(slot, k):
            return raw[:, slot, 0:2048].rearrange("p (k n) -> p k n", k=k)

        def mm3(pe, out, w, h, l, start, stop):
            slot, c = w
            pe.matmul(out, WH[:, slot, c:c + P], h, start=start, stop=False)
            pe.matmul(out, WH[:, slot, c:c + P], l, start=False, stop=False)
            return pe.matmul(out, WL[:, slot, c:c + P], h, start=False, stop=stop)

        def pe_block256(pe, b, slot, j, mh, ml, n=T, arrive=None):
            pe.wait_ge(l_done, b + 1)
            for o in range(2):
                acc = bank[2 * slot + o][:, 0:n]
                if not isinstance(j, int) or j + o >= 4:
                    pe.wait_ge(acc_read, j + o - 3)
                for k in range(KD):
                    if arrive is not None and o == 0:
                        pe.wait_ge(ss(*arrive), at(*arrive, k + 1))
                    mm = mm3(pe, acc, (slot, k * 256 + o * P), mh[:, k, 0:n], ml[:, k, 0:n], k == 0, k == KD - 1)
                mm.then_inc(mm_done, 1)

        def pre_act(act, s, gain):
            for k in range(KD):
                act.wait_ge(x_tile[s], x_base[s] + k + 1)
                act.activation(XH[:, k, :], X[:, k, :], ACT.Copy, scale=gain(k)).then_inc(ss(s, "xh"), 1)
                if k >= 2:
                    act.wait_ge(ss(s, "sq_use"), at(s, "sq_use", k - 1))
                act.activation(sq[:, k % 2, :], X[:, k, :], ACT.Square).then_inc(ss(s, "sq_in"), 1)

        def rms_act(act, s, which):
            act.wait_ge(ss(s, which + "stat_ok"), at(s, which + "stat_ok", 1))
            act.activation(rms[:, :], stat[:, :], ACT.Sqrt, bias=eps_c[:, 0:1], scale=1.0 / D)\
               .then_inc(ss(s, which + "rms_ok"), 1)

        def pre_dve(dve, s, gain):
            for k in range(KD):
                dve.wait_ge(ss(s, "xh"), at(s, "xh", k + 1))
                dve.scalar_tensor_tensor(XL[:, k, :], X[:, k, :], gain(k), XH[:, k, :].bitcast(F32),
                                         ALU.mult, ALU.subtract).then_inc(ss(s, "xl"), 1)

        def sum_pool(pool, s, src_sem, use_sem):
            for k in range(KD):
                pool.wait_ge(ss(s, src_sem), at(s, src_sem, k + 1))
                if k == 0:
                    ins = pool.tensor_copy(ssq[:, :], sq[:, 0, :])
                else:
                    ins = pool.tensor_tensor(ssq[:, :], ssq[:, :], sq[:, k % 2, :], ALU.add)
                ins.then_inc(ss(s, use_sem), 1)
                pool.wait_ge(ss(s, use_sem), at(s, use_sem, k + 1))

        def stat_pe(pe, s, use_sem, ok_sem):
            pe.wait_ge(ss(s, use_sem), at(s, use_sem, KD))
            pe.matmul(stat[:, :], ones[:, :], ssq[:, :], start=True, stop=True).then_inc(ss(s, ok_sem), 1)

        def rstd_dve(dve, s, which):
            dve.wait_ge(ss(s, which + "rms_ok"), at(s, which + "rms_ok", 1))
            dve.reciprocal(rstd[:, :], rms[:, :])
            dve.drain()

        def post_dve(dve, s, Y, gain, half):
            for k in range(KD):
                if k >= 2:
                    dve.wait_ge(ss(s, "x_new"), at(s, "x_new", k - 1))
                dve.scalar_tensor_tensor(work1[:, k % 2, :], Y[:, k, :], gain(k), rstd[:, :], ALU.mult, ALU.mult)\
                   .then_inc(ss(s, "t_ok"), 1)

        def post_pool(pool, s, half):
            for k in range(KD):
                pool.wait_ge(ss(s, "t_ok"), at(s, "t_ok", k + 1))
                pool.tensor_tensor(X[:, k, :], X[:, k, :], work1[:, k % 2, :], ALU.add).then_inc(ss(s, "x_new"), 1)

        x_tile, x_base = {}, {}
        prev = None
        for s in stages:
            x_tile[s] = x_ok if prev is None else ss(prev, "x_new")
            x_base[s] = 0 if prev is None else at(prev, "x_new", 0)
            prev = s
        last_x = ss(prev, "x_new")

        def gains(s):
            if s.startswith("attn"):
                l = int(s[4])
                return (lambda k: col("pre_norm", k, l)), (lambda k: col("post_norm", k, l)), False
            n = {"ffn0": 0, "s5": 1, "ffn1": 2, "ffn2": 3, "conv": 4, "ffn3": 5}[s]
            return (lambda k: col("norm_pre_2", k, n)), (lambda k: col("norm_post_2", k, n)), s.startswith("ffn")

        NP = FF // 256

        def ffn_sp(sp, s):
            n, b0 = int(s[3]), first_block[s]
            l, j = n // 2, n % 2
            w1 = io["ffn_w1_2"][l, j].rearrange("(k p) n -> p k n", p=P)
            w3 = io["ffn_w3_2"][l, j].rearrange("(k p) n -> p k n", p=P)
            w2 = io["ffn_w2_2"][l, j].rearrange("(k p) n -> p k n", p=P)

            def pair(i):
                c = i * 256
                load_block(sp, b0 + 2 * i, 0, raw3(0, KD), w1[:, :, bass.ds(c, 256)])
                load_block(sp, b0 + 2 * i + 1, 1, raw3(1, KD), w3[:, :, bass.ds(c, 256)])

            pair(0)
            with sp.Fori(1, NP) as i:
                pair(i)
            with sp.Fori(0, KD) as o:
                for half in range(2):
                    load_block(sp, b0 + 2 * NP + 2 * o + half, half,
                               raw[:, half, 0:11 * P].rearrange("p (k n) -> p k n", k=11),
                               w2[:, 11 * half:11 * half + 11, bass.ds(o * P, P)])

        def ffn_pe(pe, s):
            b0, j0, s0 = first_block[s], tiles_before[s], first_step[s]

            def pair(i, first):
                pe_block256(pe, b0 + 2 * i, 0, j0 + 4 * i, XH, XL, arrive=(s, "xl") if first else None)
                if first:
                    stat_pe(pe, s, "sq_use", "stat_ok")
                pe_block256(pe, b0 + 2 * i + 1, 1, j0 + 4 * i + 2, XH, XL)

            pair(0, True)
            with pe.Fori(1, NP) as i:
                pair(i, False)
            b1, j1, s1 = b0 + 2 * NP, j0 + 2 * KF, s0 + 2 * KF

            def down(i, first):
                for q in range(4):
                    acc = bank[q]
                    pe.wait_ge(acc_read, j1 + 4 * i + q - 3)
                    for half in range(2):
                        pe.wait_ge(l_done, b1 + 8 * i + 2 * q + half + 1)
                        for k in range(11):
                            kk = 11 * half + k
                            if first and q == 0:
                                pe.wait_ge(ss(s, "hl"), at(s, "hl", kk + 1))
                            mm = mm3(pe, acc[:, :], (half, k * P), HH[:, kk, :], HL[:, kk, :], kk == 0, kk == KF - 1)
                        mm.then_inc(mm_done, 1)

            down(0, True)
            down(1, False)
            stat_pe(pe, s, "ysq_use", "ystat_ok")

        def ffn_act(act, s):
            b0, j0, s0 = first_block[s], tiles_before[s], first_step[s]
            pre, post, half = gains(s)
            pre_act(act, s, pre)
            split_h(act, b0 + 1, 1, 16, first_step[s])
            rms_act(act, s, "")

            def silu(i, o):
                act.wait_ge(acc_read, j0 + 4 * i + o + 1)
                if not isinstance(i, int) or i >= 1:
                    act.wait_ge(ss(s, "hid"), at(s, "hid", 2 * i + o - 1))
                act.activation(work2[:, o, :], work1[:, o, :], ACT.Silu).then_inc(ss(s, "silu"), 1)

            def hidden(i, o):
                act.wait_ge(ss(s, "hid"), at(s, "hid", 2 * i + o + 1))
                act.activation(HH[:, bass.ds(2 * i + o, 1), :], work1[:, o, :], ACT.Copy).then_inc(ss(s, "hh"), 1)

            def pair(i, nxt):
                if nxt is not None:
                    pass
                silu(i, 0)
                silu(i, 1)
                split_h(act, b0 + 2 * i + 2, 0, nxt, s0 + 4 * i + 2)
                hidden(i, 0)
                hidden(i, 1)
                split_h(act, b0 + 2 * i + 3, 1, nxt, s0 + 4 * i + 4)

            pair(0, 16)
            with act.Fori(1, NP - 1) as i:
                pair(i, 16)
            pair(NP - 1, 11)
            b1, j1, s1 = b0 + 2 * NP, j0 + 2 * KF, s0 + 2 * KF

            def square(o, slot):
                act.wait_ge(acc_read, j1 + o + 1)
                if not isinstance(o, int) or o >= 2:
                    act.wait_ge(ss(s, "ysq_use"), at(s, "ysq_use", o - 1))
                act.activation(sq[:, slot, :], YA[:, bass.ds(o, 1), :], ACT.Square).then_inc(ss(s, "ysq_in"), 1)

            def out_pair(i, last):
                for q in range(2):
                    o = 2 * i + q
                    if not last or q == 0:
                        split_h(act, b1 + 2 * o + 2, 0, 11, s1 + 2 * o + 1)
                        split_h(act, b1 + 2 * o + 3, 1, 11, s1 + 2 * o + 2)
                    elif b1 + 2 * o + 2 < len(cells):
                        split_h(act, b1 + 2 * o + 2, 0, cells[b1 + 2 * o + 2], s1 + 2 * o + 1)
                    square(o, q)

            out_pair(0, False)
            with act.Fori(1, KD // 2 - 1) as i:
                out_pair(i, False)
            out_pair(KD // 2 - 1, True)
            rms_act(act, s, "y")

        def ffn_dve(dve, s):
            b0, j0, s0 = first_block[s], tiles_before[s], first_step[s]
            pre, post, half = gains(s)
            pre_dve(dve, s, pre)
            split_l(dve, b0 + 1, 1, 16)
            rstd_dve(dve, s, "")

            def up1(i, o):
                dve.wait_ge(mm_done, s0 + 4 * i + o + 1)
                if not isinstance(i, int) or i >= 1:
                    dve.wait_ge(ss(s, "hl"), at(s, "hl", 2 * i + o - 1))
                dve.tensor_tensor(work1[:, o, :], bank[o][:, :], rstd[:, :], ALU.mult).then_inc(acc_read, 1)

            def up3(i, o):
                dve.wait_ge(mm_done, s0 + 4 * i + 2 + o + 1)
                dve.wait_ge(ss(s, "silu"), at(s, "silu", 2 * i + o + 1))
                dve.tensor_tensor(work1[:, o, :], bank[2 + o][:, :], rstd[:, :], ALU.mult).then_inc(acc_read, 1)
                dve.drain()
                dve.tensor_tensor(work1[:, o, :], work1[:, o, :], work2[:, o, :], ALU.mult).then_inc(ss(s, "hid"), 1)

            def hidden(i, o):
                dve.wait_ge(ss(s, "hh"), at(s, "hh", 2 * i + o + 1))
                dve.tensor_tensor(HL[:, bass.ds(2 * i + o, 1), :], work1[:, o, :],
                                  HH[:, bass.ds(2 * i + o, 1), :].bitcast(F32), ALU.subtract)\
                   .then_inc(ss(s, "hl"), 1)

            def pair(i, nxt):
                for o in range(2):
                    up1(i, o)
                split_l(dve, b0 + 2 * i + 2, 0, nxt)
                for o in range(2):
                    up3(i, o)
                for o in range(2):
                    hidden(i, o)
                split_l(dve, b0 + 2 * i + 3, 1, nxt)

            pair(0, 16)
            with dve.Fori(1, NP - 1) as i:
                pair(i, 16)
            pair(NP - 1, 11)
            b1, j1, s1 = b0 + 2 * NP, j0 + 2 * KF, s0 + 2 * KF

            def out_tile(o, bk, n0, n1):
                if n0:
                    split_l(dve, b1 + 2 * o + 2, 0, n0)
                if n1:
                    split_l(dve, b1 + 2 * o + 3, 1, n1)
                dve.wait_ge(mm_done, s1 + 2 * o + 2)
                dve.tensor_copy(YA[:, bass.ds(o, 1), :], bank[bk][:, :]).then_inc(acc_read, 1)

            for o in range(KD):
                b = b1 + 2 * o + 2
                if o < KD - 1:
                    out_tile(o, o % 4, 11, 11)
                else:
                    out_tile(o, o % 4, cells[b] if b < len(cells) else 0, 0)
            rstd_dve(dve, s, "y")
            post_dve(dve, s, YA, post, half)

        def ffn_pool(pool, s):
            sum_pool(pool, s, "sq_in", "sq_use")
            sum_pool(pool, s, "ysq_in", "ysq_use")
            post_pool(pool, s, True)

        def nxt(b):
            return cells[b] if b < len(cells) else 0

        def out_sp(sp, b, w):
            w3 = w.rearrange("(k p) n -> p k n", p=P)
            for i in range(4):
                load_block(sp, b + i, i % 2, raw3(i % 2, KD), w3[:, :, i * 256:(i + 1) * 256])

        def out_pe(pe, s, b, j, arrive):
            for i in range(4):
                pe_block256(pe, b + i, i % 2, j + 2 * i, XH, XL, arrive=arrive if i == 0 else None)
            stat_pe(pe, s, "ysq_use", "ystat_ok")

        def out_act(act, s, b, j, step, Y):
            for i in range(4):
                if i < 3 and nxt(b + i + 2):
                    split_h(act, b + i + 2, i % 2, nxt(b + i + 2), step + 2 * i + 2)
                for o in (2 * i, 2 * i + 1):
                    act.wait_ge(acc_read, j + o + 1)
                    if o >= 2:
                        act.wait_ge(ss(s, "ysq_use"), at(s, "ysq_use", o - 1))
                    act.activation(sq[:, o % 2, :], Y[:, o, :], ACT.Square).then_inc(ss(s, "ysq_in"), 1)
            rms_act(act, s, "y")

        def out_dve(dve, s, b, j, step, Y, gain, bias=None):
            for i in range(4):
                for o in (2 * i, 2 * i + 1):
                    dve.wait_ge(mm_done, step + o + 1)
                    acc = bank[2 * (i % 2) + o % 2]
                    if bias is None:
                        dve.tensor_copy(Y[:, o, :], acc[:, :]).then_inc(acc_read, 1)
                    else:
                        dve.tensor_scalar(Y[:, o, :], acc[:, :], bias(o), None, ALU.add).then_inc(acc_read, 1)
                if i < 3 and nxt(b + i + 2):
                    split_l(dve, b + i + 2, i % 2, nxt(b + i + 2))
            rstd_dve(dve, s, "y")
            post_dve(dve, s, Y, gain, False)

        def conv_sp(sp, s):
            b0 = first_block[s]
            w = io["cv_w_in_2"][0].rearrange("(k p) n -> p k n", p=P)
            for i in range(4):
                load_block(sp, b0 + 2 * i, 0, raw3(0, KD), w[:, :, i * 256:(i + 1) * 256])
                load_block(sp, b0 + 2 * i + 1, 1, raw3(1, KD), w[:, :, D + i * 256:D + (i + 1) * 256])
            out_sp(sp, b0 + 8, io["cv_w_out_2"][0])

        def conv_pe(pe, s):
            b0, j0 = first_block[s], tiles_before[s]
            for i in range(4):
                pe_block256(pe, b0 + 2 * i, 0, j0 + 4 * i, XH, XL, arrive=(s, "xl") if i == 0 else None)
                if i == 0:
                    stat_pe(pe, s, "sq_use", "stat_ok")
                pe_block256(pe, b0 + 2 * i + 1, 1, j0 + 4 * i + 2, XH, XL)
            pe.wait_ge(ss(s, "cvsum"), at(s, "cvsum", KD))
            pe.matmul(stat[:, :], ones[:, :], ssq[:, :], start=True, stop=True).then_inc(ss(s, "cvstat"), 1)
            pe.wait_ge(ss(s, "censum"), at(s, "censum", KD))
            pe.matmul(stat[:, :], ones[:, :], ssq[:, :], start=True, stop=True).then_inc(ss(s, "censtat"), 1)
            out_pe(pe, s, b0 + 8, j0 + 16, (s, "l2"))

        def conv_act(act, s):
            b0, j0, s0 = first_block[s], tiles_before[s], first_step[s]
            pre, post, _ = gains(s)
            pre_act(act, s, pre)
            split_h(act, b0 + 1, 1, 16, s0)
            rms_act(act, s, "")
            for i in range(4):
                split_h(act, b0 + 2 * i + 2, 0, 16, s0 + 4 * i + 2)
                for o in range(2):
                    act.wait_ge(acc_read, j0 + 4 * i + 2 + o + 1)
                    if i >= 1:
                        act.wait_ge(ss(s, "z"), at(s, "z", 2 * i + o - 1))
                    act.activation(SG[:, o, :], work2[:, o, :], ACT.Sigmoid, bias=col("cv_b_in_2", KD + 2 * i + o))\
                       .then_inc(ss(s, "sig"), 1)
                split_h(act, b0 + 2 * i + 3, 1, 16, s0 + 4 * i + 4)
            act.wait_ge(ss(s, "cvstat"), at(s, "cvstat", 1))
            act.activation(rms[:, :], stat[:, :], ACT.Copy, scale=1.0 / D).then_inc(ss(s, "mu"), 1)
            for k in range(KD):
                act.wait_ge(ss(s, "cen"), at(s, "cen", k + 1))
                if k >= 2:
                    act.wait_ge(ss(s, "censum"), at(s, "censum", k - 1))
                act.activation(sq[:, k % 2, :], CV[:, k, :], ACT.Square).then_inc(ss(s, "censq"), 1)
            act.wait_ge(ss(s, "censtat"), at(s, "censtat", 1))
            act.activation(rms[:, :], stat[:, :], ACT.Sqrt, bias=eps_c[:, 0:1], scale=1.0 / D)\
               .then_inc(ss(s, "sigma"), 1)
            for k in range(KD):
                act.wait_ge(ss(s, "nrm"), at(s, "nrm", k + 1))
                act.activation(CV[:, k, :], CV[:, k, :], ACT.Silu, bias=col("cv_ln_b_2", k), scale=col("cv_ln_g_2", k))\
                   .then_inc(ss(s, "zs"), 1)
                act.wait_ge(ss(s, "zs"), at(s, "zs", k + 1))
                act.activation(XH[:, k, :], CV[:, k, :], ACT.Copy).then_inc(ss(s, "h2"), 1)
            out_act(act, s, b0 + 8, j0 + 16, s0 + 16, YC)

        def conv_dve(dve, s):
            b0, j0, s0 = first_block[s], tiles_before[s], first_step[s]
            pre, post, _ = gains(s)
            pre_dve(dve, s, pre)
            split_l(dve, b0 + 1, 1, 16)
            rstd_dve(dve, s, "")
            for i in range(4):
                for o in range(2):
                    dve.wait_ge(mm_done, s0 + 4 * i + o + 1)
                    if i >= 1:
                        dve.wait_ge(ss(s, "z"), at(s, "z", 2 * i + o - 1))
                    dve.tensor_tensor(work1[:, o, :], bank[o][:, :], rstd[:, :], ALU.mult).then_inc(acc_read, 1)
                split_l(dve, b0 + 2 * i + 2, 0, 16)
                for o in range(2):
                    dve.wait_ge(mm_done, s0 + 4 * i + 2 + o + 1)
                    if i >= 1:
                        dve.wait_ge(ss(s, "sig"), at(s, "sig", 2 * i + o - 1))
                    dve.tensor_tensor(work2[:, o, :], bank[2 + o][:, :], rstd[:, :], ALU.mult).then_inc(acc_read, 1)
                for o in range(2):
                    dve.wait_ge(ss(s, "sig"), at(s, "sig", 2 * i + o + 1))
                    dve.wait_ge(ss(s, "zpad"), at(s, "zpad", 1))
                    dve.scalar_tensor_tensor(ZP[:, 2 * i + o, CONV_PAD:], work1[:, o, :], col("cv_b_in_2", 2 * i + o),
                                             SG[:, o, :], ALU.add, ALU.mult).then_inc(ss(s, "z"), 1)
                split_l(dve, b0 + 2 * i + 3, 1, 16)
            dve.wait_ge(ss(s, "z"), at(s, "z", KD))
            for k in range(KD):
                for t in range(CONV_W):
                    tap, src = dwT[:, t * KD + k:t * KD + k + 1], ZP[:, k, t:t + T]
                    if t == 0:
                        ins = dve.tensor_scalar(CV[:, k, :], src, tap, col("cv_dw_b_2", k), ALU.mult, ALU.add)
                    else:
                        ins = dve.scalar_tensor_tensor(CV[:, k, :], src, tap, CV[:, k, :], ALU.mult, ALU.add)
                    if t < CONV_W - 1:
                        dve.drain()
                ins.then_inc(ss(s, "cv"), 1)
            dve.wait_ge(ss(s, "mu"), at(s, "mu", 1))
            for k in range(KD):
                dve.tensor_tensor(CV[:, k, :], CV[:, k, :], rms[:, :], ALU.subtract).then_inc(ss(s, "cen"), 1)
            dve.wait_ge(ss(s, "sigma"), at(s, "sigma", 1))
            dve.reciprocal(rstd[:, :], rms[:, :])
            dve.drain()
            for k in range(KD):
                dve.tensor_tensor(CV[:, k, :], CV[:, k, :], rstd[:, :], ALU.mult).then_inc(ss(s, "nrm"), 1)
            for k in range(KD):
                dve.wait_ge(ss(s, "h2"), at(s, "h2", k + 1))
                dve.tensor_tensor(XL[:, k, :], CV[:, k, :], XH[:, k, :].bitcast(F32), ALU.subtract)\
                   .then_inc(ss(s, "l2"), 1)
            out_dve(dve, s, b0 + 8, j0 + 16, s0 + 16, YC, post, lambda o: col("cv_b_out_2", o))

        def conv_pool(pool, s):
            pool.wait_ge(x_tile[s], x_base[s] + KD)
            pool.memset(ZP[:, :, 0:CONV_PAD], 0.0).then_inc(ss(s, "zpad"), 1)
            sum_pool(pool, s, "sq_in", "sq_use")
            for k in range(KD):
                pool.wait_ge(ss(s, "cv"), at(s, "cv", k + 1))
                if k == 0:
                    pool.tensor_copy(ssq[:, :], CV[:, 0, :]).then_inc(ss(s, "cvsum"), 1)
                else:
                    pool.tensor_tensor(ssq[:, :], ssq[:, :], CV[:, k, :], ALU.add).then_inc(ss(s, "cvsum"), 1)
                pool.wait_ge(ss(s, "cvsum"), at(s, "cvsum", k + 1))
            sum_pool(pool, s, "censq", "censum")
            sum_pool(pool, s, "ysq_in", "ysq_use")
            post_pool(pool, s, True)

        DQ, DK, DV, DG, GQ, GK, GV, GG, MQ, MG = 0, 3, 6, 9, 12, 15, 16, 17, 20, 22
        ROPED = [(j, 0) for j in range(DQ, DV)] + [(j, 2) for j in range(GQ, GV)]
        GATES = list(range(DG, DG + 3)) + list(range(GG, GG + 3)) + list(range(MG, MG + 2))
        NHEAD = 16

        def head(h):
            if h < 6:
                parts = [(PR[:, DQ + h // 2, :], PR[:, DK + h // 2, :], (h % 2) * 64 + 32 * i, 32) for i in range(2)]
                c = (h // 2) * P
                return parts, (lambda m, s: (VdH, VdL)[m][:, s, c:c + P]), 4, 32 ** -0.5, DG + h // 2
            if h < 12:
                g = h - 6
                kv, row = g // 3, (g % 2) * 64
                k = PR[:, GK, :] if kv * 64 == row else gk2[:, :]
                return [(PR[:, GQ + g // 2, :], k, row, 64)], (lambda m, s: (VgH, VgL)[m][:, s, kv, :]), 4, 0.125, GG + g // 2
            g = h - 12
            c = (g // 2) * P
            return ([(PR[:, MQ + g // 2, :], MK[:, g // 2, :], (g % 2) * 64, 64)],
                    (lambda m, s: (VmH, VmL)[m][:, s, c:c + P]), 2, 0.125, MG + g // 2)

        HEADS = [head(h) for h in range(NHEAD)]
        UNITS = [(h, t) for h in range(NHEAD) for t in range(4)]
        SCORE0 = []
        for h, t in UNITS:
            SCORE0.append(SCORE0[-1] + len(HEADS[UNITS[len(SCORE0) - 1][0]][0]) if SCORE0 else 0)

        def attn_sp(sp, s):
            b0, l = first_block[s], int(s[4])
            wm = io["w_mem_kv"][l].rearrange("(k p) n -> p k n", p=P)
            wi = io["w_in"][l].rearrange("(k p) n -> p k n", p=P)
            for i in range(2):
                load_block(sp, b0 + i, i, raw3(i, KD), wm[:, :, i * 256:(i + 1) * 256])
            with sp.Fori(0, 6) as i:
                for q in range(2):
                    load_block(sp, b0 + 2 + 2 * i + q, q, raw3(q, KD), wi[:, :, bass.ds(i * 512 + q * 256, 256)])
            out_sp(sp, b0 + 14, io["w_out"][l])

        def attn_pool(pool, s):
            l = int(s[4])
            pool.wait_ge(x_tile[s], x_base[s] + KD)
            pool.dma_start(MEMN[:, :, :], io["mem"][0].rearrange("(t p) d -> p t d", p=P)).then_inc(ss(s, "mem_in"), 16)
            pool.dma_start(perm[:, :, :], io["perm_c"]).then_inc(ss(s, "perm_in"), 16)
            sum_pool(pool, s, "sq_in", "sq_use")
            pool.wait_ge(mm_done, first_step[s] + 28)
            pool.dma_start(rope[:, :, :], io["rope_c"]).then_inc(ss(s, "rope_in"), 16)
            sum_pool(pool, s, "ysq_in", "ysq_use")
            post_pool(pool, s, True)

        def attn_pe(pe, s):
            b0, j0, s0 = first_block[s], tiles_before[s], first_step[s]
            for k in range(KD):
                for t in range(2):
                    pe.wait_ge(ss(s, "mem_n"), at(s, "mem_n", t + 1))
                    if k >= 3:
                        pe.wait_ge(ss(s, "ml"), at(s, "ml", k - 2))
                    mm = pe.transpose(bank[4 + k % 3][:, t * P:(t + 1) * P], MEMN[:, t, k * P:(k + 1) * P], ident[:, :])
                mm.then_inc(ss(s, "mem_t"), 1)
            for i in range(2):
                pe_block256(pe, b0 + i, i, j0 + 2 * i, MH, ML, NMEM, arrive=(s, "ml") if i == 0 else None)

            def pair(i, first):
                pe_block256(pe, b0 + 2 + 2 * i, 0, j0 + 4 + 4 * i, XH, XL, arrive=(s, "xl") if first else None)
                if first:
                    stat_pe(pe, s, "sq_use", "stat_ok")
                pe_block256(pe, b0 + 3 + 2 * i, 1, j0 + 4 + 4 * i + 2, XH, XL)

            pair(0, True)
            with pe.Fori(1, 6) as i:
                pair(i, False)
            pe.wait_ge(acc_read, j0 + 4)
            for o in range(2):
                for t in range(2):
                    mm = pe.transpose(bank[4][:, (2 * t + o) * P:(2 * t + o + 1) * P], work2[:, o, t * P:(t + 1) * P],
                                      ident[:, :])
            mm.then_inc(ss(s, "vm_t"), 1)
            for n, j in enumerate((DV, DV + 1, DV + 2, GV)):
                pe.wait_ge(acc_read, j0 + 4 + j + 1)
                if n >= 1:
                    pe.wait_ge(ss(s, "vl"), at(s, "vl", n))
                for t in range(4):
                    mm = pe.transpose(bank[5][:, t * P:(t + 1) * P], PR[:, j, t * P:(t + 1) * P], ident[:, :])
                mm.then_inc(ss(s, "v_t"), 1)
            pe.wait_ge(ss(s, "perm_in"), at(s, "perm_in", 16))
            for n in range(4):
                pe.wait_ge(ss(s, "gsq"), at(s, "gsq", n + 1))
                pe.matmul(bank[n][:, :], perm[:, 1, :], sq[:, n % 2, :], start=True, stop=True).then_inc(ss(s, "gms"), 1)
            for n, (j, _) in enumerate(ROPED):
                if j >= GQ:
                    pe.wait_ge(ss(s, "gn"), at(s, "gn", j - GQ + 1))
                if n >= 2:
                    pe.wait_ge(ss(s, "roped"), at(s, "roped", n - 1))
                pe.matmul(bank[6 + n % 2][:, :], perm[:, 0, :], PR[:, j, :], start=True, stop=True)\
                  .then_inc(ss(s, "swapped"), 1)
            pe.wait_ge(ss(s, "ready"), at(s, "ready", 1))

            def scores(u):
                h, t = UNITS[u]
                for i, (q, k, row, n) in enumerate(HEADS[h][0]):
                    m = SCORE0[u] + i
                    keys = HEADS[h][2] * P
                    if m >= 4:
                        pe.wait_ge(ss(s, "e"), at(s, "e", m - 3))
                    pe.matmul(bank[m % 4][:, 0:keys], q[row:row + n, t * P:(t + 1) * P], k[row:row + n, 0:keys],
                              start=True, stop=True).then_inc(ss(s, "s"), 1)

            def transposes(u):
                h, t = UNITS[u]
                pe.wait_ge(ss(s, "p"), at(s, "p", u + 1))
                if u >= 2:
                    pe.wait_ge(ss(s, "ptl"), at(s, "ptl", u - 1))
                for c in range(HEADS[h][2]):
                    mm = pe.transpose(bank[4 + u % 2][:, c * P:(c + 1) * P], E[:, u % 2, 0, c * P:(c + 1) * P], ident[:, :])
                mm.then_inc(ss(s, "pt"), 1)

            def values(h):
                _, v, nk, _, _ = HEADS[h]
                pe.wait_ge(ss(s, "ptl"), at(s, "ptl", 4 * h + 4))
                if h >= 2:
                    pe.wait_ge(ss(s, "o"), at(s, "o", h - 1))
                out = bank[6 + h % 2][:, :]
                for c in range(nk):
                    pe.matmul(out, v(0, c), PTH[:, c, :], start=(c == 0), stop=False)
                    pe.matmul(out, v(0, c), PTL[:, c, :], start=False, stop=False)
                    mm = pe.matmul(out, v(1, c), PTH[:, c, :], start=False, stop=(c == nk - 1))
                mm.then_inc(ss(s, "pv"), 1)

            for u in range(len(UNITS) + 2):
                if u < len(UNITS):
                    scores(u)
                if u >= 2 and UNITS[u - 2][1] == 3:
                    values(UNITS[u - 2][0])
                if 1 <= u <= len(UNITS):
                    transposes(u - 1)
            for n in range(3):
                pe.wait_ge(ss(s, "osq"), at(s, "osq", n + 1))
                pe.matmul(bank[n][:, :], perm[:, 1, :], sq[:, n % 2, :], start=True, stop=True).then_inc(ss(s, "oms"), 1)
            out_pe(pe, s, b0 + 14, j0 + 28, (s, "mixl"))

        def attn_act(act, s):
            b0, j0, s0 = first_block[s], tiles_before[s], first_step[s]
            l = int(s[4])
            pre, post, _ = gains(s)
            split_h(act, b0 + 1, 1, 16, s0)
            for t in range(2):
                act.wait_ge(ss(s, "mem_in"), at(s, "mem_in", 16))
                act.activation(sq[:, :, :], MEMN[:, t, :].rearrange("p (a n) -> p a n", a=2), ACT.Square,
                               accum_out=stats[:, 0, t:t + 1]).then_inc(ss(s, "msq"), 1)
                act.wait_ge(ss(s, "msq"), at(s, "msq", t + 1))
            act.activation(stats[:, 1, 0:2], stats[:, 0, 0:2], ACT.Sqrt, bias=eps_c[:, 0:1], scale=1.0 / D)\
               .then_inc(ss(s, "mrms"), 1)
            for k in range(KD):
                act.wait_ge(ss(s, "mem_t"), at(s, "mem_t", k + 1))
                act.activation(MH[:, k, :], bank[4 + k % 3][:, 0:NMEM], ACT.Copy, scale=col("mem_norm", k, l))\
                   .then_inc(ss(s, "mh"), 1)
            pre_act(act, s, pre)
            split_h(act, b0 + 2, 0, 16, s0 + 2)
            split_h(act, b0 + 3, 1, 16, s0 + 4)
            rms_act(act, s, "")
            with act.Fori(0, 6) as i:
                for q in range(2):
                    split_h(act, b0 + 4 + 2 * i + q, q, 16, s0 + 4 + 4 * i + 2 * q + 2)
            act.wait_ge(ss(s, "vm_t"), at(s, "vm_t", 1))
            act.activation(VmH[:, :, :], bank[4][:, :].rearrange("p (t n) -> p t n", t=2), ACT.Copy)\
               .then_inc(ss(s, "vmh"), 1)
            for n in range(4):
                act.wait_ge(ss(s, "v_t"), at(s, "v_t", n + 1))
                b = bank[5][:, :]
                if n < 3:
                    act.activation(VdH[:, :, n * P:(n + 1) * P], b.rearrange("p (t c) -> p t c", t=4), ACT.Copy)\
                       .then_inc(ss(s, "vh"), 1)
                else:
                    for half in range(2):
                        ins = act.activation(VgH[:, :, :, 64 * half:64 * half + 64],
                                             b.rearrange("p (t g c) -> p t g c", t=4, g=2), ACT.Copy)
                    ins.then_inc(ss(s, "vh"), 1)
            for n in range(4):
                act.wait_ge(acc_read, j0 + 4 + GQ + n + 1)
                if n >= 2:
                    act.wait_ge(ss(s, "gms"), at(s, "gms", n - 1))
                act.activation(sq[:, n % 2, :], PR[:, GQ + n, :], ACT.Square).then_inc(ss(s, "gsq"), 1)
                act.wait_ge(ss(s, "gms"), at(s, "gms", n + 1))
                if n >= 2:
                    act.wait_ge(ss(s, "gn"), at(s, "gn", n - 1))
                act.activation(work2[:, n % 2, :], bank[n][:, :], ACT.Sqrt, bias=eps_c[:, 0:1], scale=1.0 / 64)\
                   .then_inc(ss(s, "grms"), 1)
            for n, j in enumerate(GATES):
                act.activation(PR[:, j, :], PR[:, j, :], ACT.Silu).then_inc(ss(s, "gate"), 1)
            n_u = len(UNITS)

            def exps(u):
                h, t = UNITS[u]
                parts, _, nk, scale, _ = HEADS[h]
                act.wait_ge(ss(s, "nb"), at(s, "nb", u + 1))
                if u >= 2:
                    act.wait_ge(ss(s, "pt"), at(s, "pt", u - 1))
                for i in range(len(parts)):
                    m = SCORE0[u] + i
                    act.activation(E[:, u % 2, i, 0:nk * P], bank[m % 4][:, 0:nk * P], ACT.Exp,
                                   bias=stats[:, 1, m % 8:m % 8 + 1], scale=scale,
                                   accum_out=stats[:, 2, m % 8:m % 8 + 1]).then_inc(ss(s, "e"), 1)

            def split_p(u):
                h, t = UNITS[u]
                nk = HEADS[h][2]
                act.wait_ge(ss(s, "pt"), at(s, "pt", u + 1))
                if h >= 1:
                    act.wait_ge(ss(s, "pv"), at(s, "pv", h))
                act.activation(PTH[:, 0:nk, t * P:(t + 1) * P],
                               bank[4 + u % 2][:, 0:nk * P].rearrange("p (c n) -> p c n", c=nk), ACT.Copy)\
                   .then_inc(ss(s, "pth"), 1)

            for u in range(n_u + 1):
                if u < n_u:
                    exps(u)
                if u >= 1:
                    split_p(u - 1)
            for n in range(3):
                act.wait_ge(ss(s, "o"), at(s, "o", 2 * n + 2))
                if n >= 2:
                    act.wait_ge(ss(s, "oms"), at(s, "oms", n - 1))
                act.activation(sq[:, n % 2, :], PR[:, DQ + n, :], ACT.Square).then_inc(ss(s, "osq"), 1)
                act.wait_ge(ss(s, "oms"), at(s, "oms", n + 1))
                if n >= 2:
                    act.wait_ge(ss(s, "on"), at(s, "on", n - 1))
                act.activation(work2[:, n % 2, :], bank[n][:, :], ACT.Sqrt, bias=eps_c[:, 0:1], scale=1.0 / 64)\
                   .then_inc(ss(s, "orms"), 1)
            for k, j in enumerate(GATES):
                if k < 3:
                    act.wait_ge(ss(s, "og"), at(s, "og", k + 1))
                else:
                    act.wait_ge(ss(s, "o"), at(s, "o", NHEAD))
                act.activation(XH[:, k, :], PR[:, j, :], ACT.Copy).then_inc(ss(s, "mixh"), 1)
            out_act(act, s, b0 + 14, j0 + 28, s0 + 28, PR)

        def attn_dve(dve, s):
            b0, j0, s0 = first_block[s], tiles_before[s], first_step[s]
            l = int(s[4])
            pre, post, _ = gains(s)
            split_l(dve, b0 + 1, 1, 16)
            dve.wait_ge(ss(s, "mrms"), at(s, "mrms", 1))
            dve.reciprocal(stats[:, 2, 0:2], stats[:, 1, 0:2])
            dve.drain()
            for t in range(2):
                dve.tensor_scalar(MEMN[:, t, :], MEMN[:, t, :], stats[:, 2, t:t + 1], None, ALU.mult)\
                   .then_inc(ss(s, "mem_n"), 1)
            for k in range(KD):
                dve.wait_ge(ss(s, "mh"), at(s, "mh", k + 1))
                dve.scalar_tensor_tensor(ML[:, k, :], bank[4 + k % 3][:, 0:NMEM], col("mem_norm", k, l),
                                         MH[:, k, :].bitcast(F32), ALU.mult, ALU.subtract).then_inc(ss(s, "ml"), 1)
            pre_dve(dve, s, pre)
            for i in range(2):
                for o in range(2):
                    dve.wait_ge(mm_done, s0 + 2 * i + o + 1)
                    dst = MK[:, o, :] if i == 0 else work2[:, o, 0:NMEM]
                    dve.tensor_copy(dst, bank[2 * i + o][:, 0:NMEM]).then_inc(acc_read, 1)
                split_l(dve, b0 + 2 + i, i, 16)
            rstd_dve(dve, s, "")
            with dve.Fori(0, 6) as i:
                for q in range(2):
                    for o in range(2):
                        j = 4 * i + 2 * q + o
                        dve.wait_ge(mm_done, s0 + 4 + j + 1)
                        dve.tensor_tensor(PR[:, bass.ds(j, 1), :], bank[2 * q + o][:, :], rstd[:, :], ALU.mult)\
                           .then_inc(acc_read, 1)
                    split_l(dve, b0 + 4 + 2 * i + q, q, 16)
            dve.wait_ge(ss(s, "vmh"), at(s, "vmh", 1))
            dve.tensor_tensor(VmL[:, :, :], bank[4][:, :].rearrange("p (t n) -> p t n", t=2), VmH[:, :, :].bitcast(F32),
                              ALU.subtract)
            for n in range(4):
                dve.wait_ge(ss(s, "vh"), at(s, "vh", n + 1))
                b = bank[5][:, :]
                if n < 3:
                    dve.tensor_tensor(VdL[:, :, n * P:(n + 1) * P], b.rearrange("p (t c) -> p t c", t=4),
                                      VdH[:, :, n * P:(n + 1) * P].bitcast(F32), ALU.subtract).then_inc(ss(s, "vl"), 1)
                else:
                    for half in range(2):
                        c = slice(64 * half, 64 * half + 64)
                        ins = dve.tensor_tensor(VgL[:, :, :, c], b.rearrange("p (t g c) -> p t g c", t=4, g=2),
                                                VgH[:, :, :, c].bitcast(F32), ALU.subtract)
                    ins.then_inc(ss(s, "vl"), 1)
            for n in range(4):
                dve.wait_ge(ss(s, "grms"), at(s, "grms", n + 1))
                dve.reciprocal(work1[:, n % 2, :], work2[:, n % 2, :])
                dve.drain()
                g = headg[:, (2 if n < 3 else 4) + l:(3 if n < 3 else 5) + l]
                dve.scalar_tensor_tensor(PR[:, GQ + n, :], PR[:, GQ + n, :], g, work1[:, n % 2, :], ALU.mult, ALU.mult)\
                   .then_inc(ss(s, "gn"), 1)
            dve.wait_ge(ss(s, "rope_in"), at(s, "rope_in", 16))
            for n, (j, tab) in enumerate(ROPED):
                if n == 0:
                    dve.wait_ge(ss(s, "gn"), at(s, "gn", 4))
                dve.wait_ge(ss(s, "swapped"), at(s, "swapped", n + 1))
                dve.tensor_tensor(PR[:, j, :], PR[:, j, :], rope[:, tab, :], ALU.mult)
                dve.tensor_tensor(work1[:, n % 2, :], bank[6 + n % 2][:, :], rope[:, tab + 1, :], ALU.mult)
                dve.drain()
                dve.tensor_tensor(PR[:, j, :], PR[:, j, :], work1[:, n % 2, :], ALU.add).then_inc(ss(s, "roped"), 1)
            dve.drain()
            dve.tensor_copy(gk2[64:128, :], PR[0:64, GK, :])
            dve.tensor_copy(gk2[0:64, :], PR[64:128, GK, :])
            dve.drain()
            dve.nop().then_inc(ss(s, "ready"), 1)

            def maxima(u):
                h, t = UNITS[u]
                parts, _, nk, scale, _ = HEADS[h]
                m, n = SCORE0[u], len(parts)
                for i in range(n):
                    c = (m + i) % 8
                    dve.wait_ge(ss(s, "s"), at(s, "s", m + i + 1))
                    dve.tensor_reduce(stats[:, 0, c:c + 1], bank[(m + i) % 4][:, 0:nk * P], AX, ALU.max)
                dve.drain()
                dve.tensor_scalar(stats[:, 1, m % 8:m % 8 + n], stats[:, 0, m % 8:m % 8 + n], -scale, None, ALU.mult)\
                   .then_inc(ss(s, "nb"), 1)

            def probs(u):
                h, t = UNITS[u]
                parts, _, nk, scale, _ = HEADS[h]
                m, n = SCORE0[u], len(parts)
                c = m % 8
                dve.wait_ge(ss(s, "e"), at(s, "e", m + n))
                dve.reciprocal(stats[:, 3, c:c + n], stats[:, 2, c:c + n])
                dve.drain()
                if n == 2:
                    dve.tensor_scalar(stats[:, 3, c + 1:c + 2], stats[:, 3, c + 1:c + 2], nlam[:, l:l + 1], None, ALU.mult)
                e0 = E[:, u % 2, 0, 0:nk * P]
                ins = dve.tensor_scalar(e0, e0, stats[:, 3, c:c + 1], None, ALU.mult)
                if n == 2:
                    dve.drain()
                    ins = dve.scalar_tensor_tensor(e0, E[:, u % 2, 1, :], stats[:, 3, c + 1:c + 2], e0, ALU.mult, ALU.add)
                ins.then_inc(ss(s, "p"), 1)

            def split_p(u):
                h, t = UNITS[u]
                nk = HEADS[h][2]
                dve.wait_ge(ss(s, "pth"), at(s, "pth", u + 1))
                dve.tensor_tensor(PTL[:, 0:nk, t * P:(t + 1) * P],
                                  bank[4 + u % 2][:, 0:nk * P].rearrange("p (c n) -> p c n", c=nk),
                                  PTH[:, 0:nk, t * P:(t + 1) * P].bitcast(F32), ALU.subtract).then_inc(ss(s, "ptl"), 1)

            def outputs(h):
                row = (h % 2) * 64
                dve.wait_ge(ss(s, "pv"), at(s, "pv", h + 1))
                acc = bank[6 + h % 2][row:row + 64, :]
                if h < 6:
                    ins = dve.tensor_copy(PR[row:row + 64, DQ + h // 2, :], acc)
                else:
                    g = PR[row:row + 64, HEADS[h][4], :]
                    ins = dve.tensor_tensor(g, acc, g, ALU.mult)
                ins.then_inc(ss(s, "o"), 1)

            dve.wait_ge(ss(s, "gate"), at(s, "gate", len(GATES)))
            for u in range(len(UNITS) + 3):
                if u < len(UNITS):
                    maxima(u)
                if 2 <= u < len(UNITS) + 2:
                    split_p(u - 2)
                if 1 <= u <= len(UNITS):
                    probs(u - 1)
                if u >= 3 and UNITS[u - 3][1] == 3:
                    outputs(UNITS[u - 3][0])
            for n in range(3):
                dve.wait_ge(ss(s, "orms"), at(s, "orms", n + 1))
                dve.reciprocal(work1[:, n % 2, :], work2[:, n % 2, :])
                dve.drain()
                dve.scalar_tensor_tensor(work1[:, n % 2, :], PR[:, DQ + n, :], headg[:, l:l + 1], work1[:, n % 2, :],
                                         ALU.mult, ALU.mult).then_inc(ss(s, "on"), 1)
                dve.wait_ge(ss(s, "on"), at(s, "on", n + 1))
                dve.tensor_tensor(PR[:, DG + n, :], PR[:, DG + n, :], work1[:, n % 2, :], ALU.mult)\
                   .then_inc(ss(s, "og"), 1)
            for k, j in enumerate(GATES):
                dve.wait_ge(ss(s, "mixh"), at(s, "mixh", k + 1))
                dve.tensor_tensor(XL[:, k, :], PR[:, j, :], XH[:, k, :].bitcast(F32), ALU.subtract)\
                   .then_inc(ss(s, "mixl"), 1)
            out_dve(dve, s, b0 + 14, j0 + 28, s0 + 28, PR, post)

        a_rows = Gx[:, :, :, :].rearrange("p a s h -> p (a s h)")[:, 0:2 * P].rearrange("p (i n) -> p i n", i=2)
        dt_row = KS[0:1, 0:GROUPS // GCH, :].rearrange("p a h -> p (a h)")
        c_rows = [x[:, :, :, :].rearrange("p g s h -> p g (s h)") for x in (G1, MT)]

        def s5_sp(sp, s):
            b0 = first_block[s]
            w = [io[n][0].rearrange("(k p) n -> p k n", p=P) for n in ("s5_w_in_2", "s5_w_glu_2")]
            for i in range(2):
                load_block(sp, b0 + i, i, raw3(i, KD), w[0][:, :, i * 256:(i + 1) * 256])
            sp.wait_ge(x_tile[s], x_base[s] + KD)
            par = ss(s, "par_in")
            sp.dma_start(s5c[:, :], io["s5_c"]).then_inc(par, 16)
            for i, n in enumerate(("s5_a_re_2", "s5_a_im_2")):
                for h in range(2):
                    sp.dma_start(a_rows[0:GROUPS, i, 64 * h:64 * h + 64], io[n][0]).then_inc(par, 16)
            sp.dma_start(dt_row, io["s5_log_dt_2"]).then_inc(par, 16)
            br, bi = (io[n][0].rearrange("g p h -> p g h") for n in ("s5_b_re_2", "s5_b_im_2"))
            for dst, src in ((B1[0:64], br), (B1[64:128], bi), (B2[0:64], bi), (B2[64:128], br)):
                sp.dma_start(dst, src).then_inc(ss(s, "b_in"), 16)
            cr, ci = (io[n][0].rearrange("g h p -> (g h) p").rearrange("(t q) p -> q t p", q=P)
                      for n in ("s5_c_re_2", "s5_c_im_2"))
            for i, pair in enumerate(((cr, ci), (ci, cr))):
                for h in range(2):
                    sp.dma_start(c_rows[i][:, :, 64 * h:64 * h + 64], pair[h]).then_inc(ss(s, "c_in"), 16)
            for i in range(2, 4):
                load_block(sp, b0 + i, i % 2, raw3(i % 2, KD), w[0][:, :, i * 256:(i + 1) * 256])
            def u_load(k):
                if k >= 2:
                    sp.wait_ge(ss(s, "ydone"), at(s, "ydone", k - 1))
                sp.dma_start(U[:, k % 2], u_scr[k]).then_inc(ss(s, "u_in"), 16)

            for k in range(KD):
                sp.wait_ge(ss(s, "us"), at(s, "us", k + 1))
                for g in range(GS):
                    sp.dma_start(u_scr[k, :, g, :].rearrange("(s h) c -> h s c", s=CL),
                                 rms[g * GCH:(g + 1) * GCH, :].rearrange("p (s c) -> p s c", s=CL))\
                      .then_inc(ss(s, "u_out"), 16)
                sp.wait_ge(ss(s, "u_out"), at(s, "u_out", 16 * GS * (k + 1)))
                if k < 2:
                    u_load(k)
                if k in (1, 3):
                    i = k // 2
                    load_block(sp, b0 + 4 + i, i, raw3(i, KD), w[1][:, :, i * 256:(i + 1) * 256])
            for k in range(KD):
                sp.wait_ge(ss(s, "ys"), at(s, "ys", k + 1))
                for t in range(CL):
                    sp.dma_start(y_scr[k, :, t, :].rearrange("(g h) c -> h g c", g=GS),
                                 YS[t * GCH:(t + 1) * GCH]).then_inc(ss(s, "y_out"), 16)
                if k + 2 < KD:
                    if True:
                        sp.wait_ge(ss(s, "u_in"), at(s, "u_in", 16 * (k + 2)))
                    u_load(k + 2)
                sp.wait_ge(ss(s, "y_out"), at(s, "y_out", 16 * CL * (k + 1)))
                if k >= 1:
                    sp.wait_ge(ss(s, "y_in"), at(s, "y_in", 16 * k))
                sp.dma_start(YR[:, k], y_scr[k]).then_inc(ss(s, "y_in"), 16)
            for i in range(2, 4):
                load_block(sp, b0 + 4 + i, i % 2, raw3(i % 2, KD), w[1][:, :, i * 256:(i + 1) * 256])
            out_sp(sp, b0 + 8, io["s5_w_out_2"][0])

        def s5_pe(pe, s):
            b0, j0, s0 = first_block[s], tiles_before[s], first_step[s]
            pe_block256(pe, b0, 0, j0, XH, XL, arrive=(s, "xl"))
            stat_pe(pe, s, "sq_use", "stat_ok")
            pe_block256(pe, b0 + 1, 1, j0 + 2, XH, XL)
            pe.wait_ge(ss(s, "par_in"), at(s, "par_in", 16 * 6))
            for i in range(2):
                pe.transpose(bank[5][:, 64 * i:64 * i + 64], a_rows[0:GROUPS, i, :], ident[0:GROUPS, 0:GROUPS])
            pe.matmul(bank[5][:, 128:192], ones[0:1, :], dt_row, start=True, stop=True)\
              .then_inc(ss(s, "par_t"), 1)
            pe.wait_ge(ss(s, "c_in"), at(s, "c_in", 16 * 4))
            for i in range(2):
                for n in (2 * i, 2 * i + 1):
                    if n >= 2:
                        pe.wait_ge(ss(s, "c_cp"), at(s, "c_cp", n - 1))
                    for t in range(4):
                        mm = pe.transpose(bank[4 + 2 * (n % 2)][:, t * P:(t + 1) * P], c_rows[n // 2][:, 4 * (n % 2) + t, :],
                                          ident[:, :])
                    mm.then_inc(ss(s, "c_t"), 1)
                pe_block256(pe, b0 + 2 + i, i, j0 + 4 + 2 * i, XH, XL)

            def to_rows(k):
                pe.wait_ge(ss(s, "wt"), at(s, "wt", k + 1))
                if k >= 1:
                    pe.wait_ge(ss(s, "mt"), at(s, "mt", k))
                for g in range(GS):
                    mm = pe.transpose(bank[4 + g // 4][:, g % 4 * P:(g % 4 + 1) * P],
                                      Wt[:, g].rearrange("p s h -> p (s h)"), ident[:, :])
                mm.then_inc(ss(s, "w_t"), 1)
                if k == 0:
                    pe.wait_ge(ss(s, "c_cp"), at(s, "c_cp", 4))
                    pe.wait_ge(ss(s, "small"), at(s, "small", 1))
                for g in range(GS):
                    mm = pe.matmul(bank[6][:, g * GCH:(g + 1) * GCH], Wt[:, g].rearrange("p s h -> p (s h)"),
                                   C1[:, k * GS + g, :], start=True, stop=True)
                mm.then_inc(ss(s, "kk"), 1)

            def toeplitz(k):
                pe.wait_ge(ss(s, "ks"), at(s, "ks", k + 1))
                pe.wait_ge(ss(s, "w1"), at(s, "w1", k + 1))
                for t in range(CL):
                    c = S5_EYE + t * GCH
                    mm = pe.matmul(bank[4 + t // 4][:, t % 4 * P:(t % 4 + 1) * P], s5c[:, c:c + P],
                                   KS[:, :, :].rearrange("p g h -> p (g h)"), start=True, stop=True)
                mm.then_inc(ss(s, "tz"), 1)

            pe.wait_ge(acc_read, j0 + 8)
            to_rows(0)
            toeplitz(0)
            for k in range(KD):
                pe.wait_ge(ss(s, "u_in"), at(s, "u_in", 16 * (k + 1)))
                pe.wait_ge(ss(s, "w1"), at(s, "w1", k + 1))
                if k >= 1:
                    pe.wait_ge(ss(s, "v"), at(s, "v", k))
                for i in range(2):
                    for g in range(GS):
                        mm = pe.matmul(bank[i][:, g * NC:(g + 1) * NC], W1[:, g, 64 * i:64 * i + P], U[:, k % 2, g, :],
                                       start=True, stop=True)
                mm.then_inc(ss(s, "s"), 1)
                if k + 1 < KD:
                    to_rows(k + 1)
                pe.wait_ge(ss(s, "z"), at(s, "z", k + 1))
                pe.matmul(bank[2][:, :], s5c[:, S5_SWAP:S5_SWAP + P], work2[:, 0, :], start=True, stop=True)\
                  .then_inc(ss(s, "zswap"), 1)
                pe.wait_ge(ss(s, "mt"), at(s, "mt", k + 1))
                pe.wait_ge(ss(s, "g1"), at(s, "g1", k + 1))
                pe.wait_ge(ss(s, "x"), at(s, "x", k + 1))
                if k >= 1:
                    pe.wait_ge(ss(s, "ys"), at(s, "ys", k))
                for g in range(GS):
                    out = bank[3][:, g * NC:(g + 1) * NC]
                    pe.matmul(out, MT[:, g].rearrange("p t h -> p (t h)"), U[:, k % 2, g, :], start=True, stop=False)
                    mm = pe.matmul(out, G1[:, g].rearrange("p t h -> p (t h)"),
                                   work2[:, 1, g * NC:(g + 1) * NC], start=False, stop=True)
                mm.then_inc(ss(s, "ydone"), 1)
                if k + 1 < KD:
                    toeplitz(k + 1)
            for i in range(4):
                pe_block256(pe, b0 + 4 + i, i % 2, j0 + 8 + 2 * i, XH, XL, arrive=(s, "gl") if i == 0 else None)
            out_pe(pe, s, b0 + 8, j0 + 16, (s, "l2"))

        def s5_act(act, s):
            b0, j0, s0 = first_block[s], tiles_before[s], first_step[s]
            pre, post, _ = gains(s)
            pre_act(act, s, pre)
            split_h(act, b0 + 1, 1, 16, s0)
            rms_act(act, s, "")
            split_h(act, b0 + 2, 0, 16, s0 + 2)
            split_h(act, b0 + 3, 1, 16, s0 + 4)
            act.wait_ge(ss(s, "par_t"), at(s, "par_t", 1))
            act.activation(sm[:, 2, :], bank[5][:, 128:192], ACT.Exp).then_inc(ss(s, "dt"), 1)
            act.wait_ge(ss(s, "m_th"), at(s, "m_th", 1))
            act.activation(sm[:, 12, :], sm[:, 3, :], ACT.Exp).then_inc(ss(s, "ex"), 1)
            act.wait_ge(ss(s, "red"), at(s, "red", 1))
            act.activation(sm[:, 13, :], sm[:, 11, :], ACT.Sin, scale=0.5).then_inc(ss(s, "half"), 1)
            act.wait_ge(ss(s, "phj"), at(s, "phj", 1))
            act.activation(CSJ[:, :, :], CSJ[:, :, :], ACT.Sin, scale=TURN)
            act.activation(SNJ[:, :, :], SNJ[:, :, :], ACT.Sin, scale=TURN).then_inc(ss(s, "sinj"), 1)

            def waves(k):
                act.wait_ge(ss(s, "ph"), at(s, "ph", k + 1))
                act.activation(COS[:, k % 2], COS[:, k % 2], ACT.Sin, scale=TURN)
                act.activation(SIN[:, k % 2], SIN[:, k % 2], ACT.Sin, scale=s5c[:, S5_SGN + 2:S5_SGN + 3])\
                   .then_inc(ss(s, "waves"), 1)

            def rows(k):
                act.wait_ge(ss(s, "w_t"), at(s, "w_t", k + 1))
                if k >= 1:
                    act.wait_ge(ss(s, "s"), at(s, "s", k))
                for b in range(2):
                    v = bank[4 + b][:, :].rearrange("p (g n) -> p g n", g=4)
                    act.activation(W1[:, 4 * b:4 * b + 4, 0:P], v, ACT.Copy)
                    ins = act.activation(W1[:, 4 * b:4 * b + 4, P:192], v[:, :, 0:64], ACT.Copy)
                ins.then_inc(ss(s, "w1"), 1)
                act.wait_ge(ss(s, "kk"), at(s, "kk", k + 1))
                if k >= 1:
                    act.wait_ge(ss(s, "tz"), at(s, "tz", k))
                act.activation(KS[:, :, :], bank[6][:, 0:P].rearrange("p (g h) -> p g h", g=GS), ACT.Copy)\
                   .then_inc(ss(s, "ks"), 1)

            def kernel_copy(k):
                act.wait_ge(ss(s, "tz"), at(s, "tz", k + 1))
                if k >= 1:
                    act.wait_ge(ss(s, "ydone"), at(s, "ydone", k))
                for b in range(2):
                    ins = act.activation(MT[:, :, 4 * b:4 * b + 4, :].rearrange("p g t h -> p t g h"),
                                         bank[4 + b][:, :].rearrange("p (t g h) -> p t g h", t=4, g=GS), ACT.Copy)
                ins.then_inc(ss(s, "mt"), 1)

            waves(0)
            rows(0)
            kernel_copy(0)
            for k in range(KD):
                if k + 1 < KD:
                    waves(k + 1)
                    rows(k + 1)
                act.wait_ge(ss(s, "ydone"), at(s, "ydone", k + 1))
                if k >= 1:
                    act.wait_ge(ss(s, "y_out"), at(s, "y_out", 16 * CL * k))
                act.activation(YS[:, :, :], bank[3][:, :].rearrange("p (g c) -> p g c", g=GS), ACT.Copy)\
                   .then_inc(ss(s, "ys"), 1)
                if k + 1 < KD:
                    kernel_copy(k + 1)
            for k in range(KD):
                act.wait_ge(ss(s, "yd"), at(s, "yd", k + 1))
                act.activation(UN[:, k, :].rearrange("p (c t) -> p c t", t=CL), YR[:, k].rearrange("p t c -> p c t"),
                               ACT.Gelu_apprx_tanh).then_inc(ss(s, "gel"), 1)
                act.wait_ge(ss(s, "gel"), at(s, "gel", k + 1))
                act.activation(XH[:, k, :], UN[:, k, :], ACT.Copy).then_inc(ss(s, "gh"), 1)
            split_h(act, b0 + 4, 0, 16, s0 + 6)
            split_h(act, b0 + 5, 1, 16, s0 + 8)
            for i in range(4):
                for o in (2 * i, 2 * i + 1):
                    act.wait_ge(mm_done, s0 + 8 + o + 1)
                    if o >= 2:
                        act.wait_ge(ss(s, "zz"), at(s, "zz", o - 1))
                    act.activation(work1[:, o % 2, :], bank[2 * (i % 2) + o % 2][:, :], ACT.Sigmoid,
                                   bias=col("s5_b_glu_2", o)).then_inc(acc_read, 1)
                split_h(act, b0 + 6 + i, i % 2, 16, s0 + 10 + 2 * i)
            for k in range(KD):
                act.wait_ge(ss(s, "zz"), at(s, "zz", k + 1))
                act.activation(XH[:, k, :], UN[:, k, :], ACT.Copy).then_inc(ss(s, "h2"), 1)
            out_act(act, s, b0 + 8, j0 + 16, s0 + 16, Y5)

        def s5_dve(dve, s):
            b0, j0, s0 = first_block[s], tiles_before[s], first_step[s]
            pre, post, _ = gains(s)
            pre_dve(dve, s, pre)
            split_l(dve, b0 + 1, 1, 16)
            rstd_dve(dve, s, "")

            def u_tile(o):
                dve.wait_ge(mm_done, s0 + o + 1)
                dve.tensor_tensor(UN[:, o, :], bank[2 * (o // 2 % 2) + o % 2][:, :], rstd[:, :], ALU.mult)\
                   .then_inc(acc_read, 1)
                dve.drain()
                if o >= 1:
                    dve.wait_ge(ss(s, "u_out"), at(s, "u_out", 16 * GS * o))
                for t in range(CL):
                    q = CL - 1 - t
                    ins = dve.tensor_copy(rms[:, q * NC:(q + 1) * NC], UN[:, o, t:T:CL])
                ins.then_inc(ss(s, "us"), 1)

            def v(i):
                return sm[:, i, :]

            def two(ins):
                dve.drain()

            def ts(out, in0, a, b, op0, op1=None):
                if op1 is None:
                    two(dve.tensor_scalar(out, in0, a, None, op0))
                else:
                    two(dve.tensor_scalar(out, in0, a, b, op0, op1))

            def tt(out, a, b, op):
                two(dve.tensor_tensor(out, a, b, op))

            def stt(out, a, c, b, op0, op1):
                two(dve.scalar_tensor_tensor(out, a, c, b, op0, op1))

            u_tile(0)
            u_tile(1)
            split_l(dve, b0 + 2, 0, 16)
            u_tile(2)
            u_tile(3)
            split_l(dve, b0 + 3, 1, 16)
            for n in range(4):
                dve.wait_ge(ss(s, "c_t"), at(s, "c_t", n + 1))
                dst = (C1, C2)[n // 2][:, 32 * (n % 2):32 * (n % 2) + 32, :].rearrange("p g h -> p (g h)")
                sgn = s5c[:, S5_SGN + 1:S5_SGN + 2] if n < 2 else -1.0
                dve.tensor_scalar(dst, bank[4 + 2 * (n % 2)][:, :], sgn, None, ALU.mult).then_inc(ss(s, "c_cp"), 1)
            AR, AI, DT, M, TH, MC, EM, T0, T1, FH, FL, RED, EX, S2, FR, FI, MAG, PW, NR, DEN = range(20)
            dve.wait_ge(ss(s, "dt"), at(s, "dt", 1))
            dve.tensor_copy(v(AR), bank[5][:, 0:64])
            dve.tensor_copy(v(AI), bank[5][:, 64:128])
            dve.drain()
            dve.tensor_tensor(v(M), v(DT), v(AR), ALU.mult)
            tt(v(TH), v(DT), v(AI), ALU.mult)
            dve.nop().then_inc(ss(s, "m_th"), 1)
            ts(v(MC), v(M), -0.5, 0.5, ALU.max, ALU.min)
            ts(v(T0), v(MC), 1.0 / 8, 1.0, ALU.mult, ALU.add)
            for n in range(7, 1, -1):
                tt(v(T0), v(T0), v(MC), ALU.mult)
                ts(v(T0), v(T0), 1.0 / n, 1.0, ALU.mult, ALU.add)
            tt(v(EM), v(T0), v(MC), ALU.mult)
            ts(v(T1), v(TH), 1 / PI2, ROUND, ALU.mult, ALU.add)
            ts(v(T1), v(T1), -ROUND, None, ALU.add)
            stt(v(RED), v(T1), -PI2_A, v(TH), ALU.mult, ALU.add)
            stt(v(RED), v(T1), -PI2_B, v(RED), ALU.mult, ALU.add)
            stt(v(RED), v(T1), -PI2_C, v(RED), ALU.mult, ALU.add)
            dve.nop().then_inc(ss(s, "red"), 1)
            ts(v(T1), v(RED), 2.0 ** 13 / PI2, ROUND, ALU.mult, ALU.add)
            ts(v(FH), v(T1), -ROUND, 2.0 ** -13, ALU.add, ALU.mult)
            stt(v(T0), v(FH), -PI2_A, v(RED), ALU.mult, ALU.add)
            stt(v(T0), v(FH), -PI2_B, v(T0), ALU.mult, ALU.add)
            stt(v(T0), v(FH), -PI2_C, v(T0), ALU.mult, ALU.add)
            ts(v(FL), v(T0), 1 / PI2, None, ALU.mult)
            J = CL + 1
            pa = work1[:, :, :].rearrange("p a n -> p (a n)")[:, 0:J * GROUPS].rearrange("p (j g) -> p j g", j=J)
            pn = work2[:, :, :].rearrange("p a n -> p (a n)")[:, 0:J * GROUPS].rearrange("p (j g) -> p j g", j=J)
            jj = s5c[:, 0:J].unsqueeze(2).to_broadcast([P, J, GROUPS])
            tt(pa, v(FH).unsqueeze(1).to_broadcast([P, J, GROUPS]), jj, ALU.mult)
            ts(pn, pa, ROUND, -ROUND, ALU.add, ALU.add)
            tt(pa, pa, pn, ALU.subtract)
            tt(pn, v(FL).unsqueeze(1).to_broadcast([P, J, GROUPS]), jj, ALU.mult)
            tt(pa, pa, pn, ALU.add)
            ts(pn, pa, ROUND, -ROUND, ALU.add, ALU.add)
            tt(SNJ[:, :, :], pa, pn, ALU.subtract)
            ts(pa, pa, 0.25, None, ALU.add)
            ts(pn, pa, ROUND, -ROUND, ALU.add, ALU.add)
            tt(CSJ[:, :, :], pa, pn, ALU.subtract)
            dve.nop().then_inc(ss(s, "phj"), 1)
            dve.wait_ge(ss(s, "ex"), at(s, "ex", 1))
            ts(v(EX), v(EX), -1.0, None, ALU.add)
            tt(v(T0), v(EM), v(EX), ALU.subtract)
            tt(v(T1), v(MC), v(M), ALU.is_equal)
            tt(v(T0), v(T0), v(T1), ALU.mult)
            tt(v(EM), v(EX), v(T0), ALU.add)
            ts(v(MAG), v(EM), 1.0, None, ALU.add)
            dve.wait_ge(ss(s, "half"), at(s, "half", 1))
            tt(v(T0), v(S2), v(S2), ALU.mult)
            dve.wait_ge(ss(s, "sinj"), at(s, "sinj", 1))
            tt(v(NR), v(EM), CSJ[:, 1, :], ALU.mult)
            stt(v(NR), v(T0), -2.0, v(NR), ALU.mult, ALU.add)
            two(dve.tensor_copy(v(PW), v(MAG)))
            for j in range(1, J):
                dve.tensor_tensor(CSJ[:, j, :], CSJ[:, j, :], v(PW), ALU.mult)
                dve.tensor_tensor(SNJ[:, j, :], SNJ[:, j, :], v(PW), ALU.mult)
                dve.drain()
                if j < CL:
                    tt(v(PW), v(PW), v(MAG), ALU.mult)
            tt(v(DEN), v(AR), v(AR), ALU.mult)
            tt(v(T0), v(AI), v(AI), ALU.mult)
            tt(v(DEN), v(DEN), v(T0), ALU.add)
            two(dve.reciprocal(v(T1), v(DEN)))
            tt(v(FR), v(NR), v(AR), ALU.mult)
            tt(v(T0), SNJ[:, 1, :], v(AI), ALU.mult)
            tt(v(FR), v(FR), v(T0), ALU.add)
            tt(v(FR), v(FR), v(T1), ALU.mult)
            tt(v(FI), SNJ[:, 1, :], v(AR), ALU.mult)
            tt(v(T0), v(NR), v(AI), ALU.mult)
            tt(v(FI), v(FI), v(T0), ALU.subtract)
            tt(v(FI), v(FI), v(T1), ALU.mult)
            dve.nop().then_inc(ss(s, "small0"), 1)
            dve.wait_ge(ss(s, "b_in"), at(s, "b_in", 64))
            ts(B2[:, :, :], B2[:, :, :], s5c[:, S5_SGN:S5_SGN + 1], None, ALU.mult)
            shape = [P, GROUPS, GCH]
            fr, fi = (v(n).unsqueeze(2).to_broadcast(shape) for n in (FR, FI))
            t1 = Wt[:, :, :, :].rearrange("p a b c -> p (a b c)").rearrange("p (g h) -> p g h", g=GROUPS)
            t2 = W1[:, :, :].rearrange("p a b -> p (a b)")[:, 0:1024].rearrange("p (g h) -> p g h", g=GROUPS)
            dve.tensor_tensor(t1, B2[:, :, :], fi, ALU.mult)
            tt(t2, B1[:, :, :], fi, ALU.mult)
            dve.tensor_tensor(B1[:, :, :], B1[:, :, :], fr, ALU.mult)
            tt(B2[:, :, :], B2[:, :, :], fr, ALU.mult)
            dve.tensor_tensor(B1[:, :, :], B1[:, :, :], t1, ALU.add)
            tt(B2[:, :, :], B2[:, :, :], t2, ALU.subtract)
            dve.nop().then_inc(ss(s, "small"), 1)

            def matrices(k):
                if k >= 1:
                    dve.wait_ge(ss(s, "kk"), at(s, "kk", k))
                for a in range(2):
                    g = k * GS + 4 * a
                    shape = [P, 4, CL, GCH]
                    er, ei = (x[:, 0:CL, g:g + 4].rearrange("p j g -> p g j").unsqueeze(3).to_broadcast(shape)
                              for x in (CSJ, SNJ))
                    b1, b2 = (x[:, g:g + 4, :].unsqueeze(2).to_broadcast(shape) for x in (B1, B2))
                    w = Wt[:, 4 * a:4 * a + 4]
                    dve.tensor_tensor(w, er, b1, ALU.mult)
                    dve.tensor_tensor(Wx[:, :, :, :], ei, b2, ALU.mult)
                    dve.drain()
                    ins = dve.tensor_tensor(w, w, Wx[:, :, :, :], ALU.add)
                    dve.drain()
                dve.nop().then_inc(ss(s, "wt"), 1)

            for o in range(4, 8):
                u_tile(o)
                if o == 4:
                    matrices(0)

            def flat(x):
                return x.rearrange("p g c -> p (g c)")

            for k in range(KD):
                cs, sn = COS[:, k % 2], SIN[:, k % 2]
                dve.wait_ge(ss(s, "waves"), at(s, "waves", k + 1))
                dve.wait_ge(ss(s, "rr"), at(s, "rr", k + 1))
                dve.wait_ge(ss(s, "s"), at(s, "s", k + 1))

                def gc(x):
                    return x.rearrange("p (g c) -> p g c", g=GS)

                if k >= 1:
                    dve.wait_ge(ss(s, "zswap"), at(s, "zswap", k))
                dve.tensor_tensor(gc(work1[:, 0, :]), gc(bank[0][:, :]), cs[:, :, 1:NC + 1], ALU.mult)
                dve.tensor_tensor(gc(work1[:, 1, :]), gc(bank[1][:, :]), sn[:, :, 1:NC + 1], ALU.mult)\
                   .then_inc(ss(s, "v"), 1)
                dve.drain()
                dve.tensor_tensor(work1[:, 0, :], work1[:, 0, :], work1[:, 1, :], ALU.add)
                dve.drain()
                dve.tensor_tensor_scan(work2[:, 0, :], flat(RR[:, :, :]), work1[:, 0, :], 0.0, ALU.mult, ALU.add)\
                   .then_inc(ss(s, "z"), 1)
                if k + 1 < KD:
                    matrices(k + 1)
                dve.wait_ge(ss(s, "zswap"), at(s, "zswap", k + 1))
                if k >= 1:
                    dve.wait_ge(ss(s, "ydone"), at(s, "ydone", k))
                x = gc(work2[:, 1, :])
                dve.memset(x[:, :, 0:1], 0.0)
                dve.tensor_tensor(x[:, :, 1:NC], gc(work2[:, 0, :])[:, :, 0:NC - 1], cs[:, :, 1:NC], ALU.mult)
                dve.tensor_tensor(gc(ssq[:, :])[:, :, 1:NC], gc(bank[2][:, :])[:, :, 0:NC - 1], sn[:, :, 1:NC], ALU.mult)
                dve.drain()
                dve.tensor_tensor(x[:, :, 1:NC], x[:, :, 1:NC], gc(ssq[:, :])[:, :, 1:NC], ALU.subtract)\
                   .then_inc(ss(s, "x"), 1)
                dve.drain()
            for k in range(KD):
                dve.wait_ge(ss(s, "y_in"), at(s, "y_in", 16 * (k + 1)))
                dve.scalar_tensor_tensor(YR[:, k], UN[:, k, :].rearrange("p (c t) -> p t c", t=CL), col("s5_d_2", k),
                                         YR[:, k], ALU.mult, ALU.add).then_inc(ss(s, "yd"), 1)
            for k in range(KD):
                dve.wait_ge(ss(s, "gh"), at(s, "gh", k + 1))
                dve.tensor_tensor(XL[:, k, :], UN[:, k, :], XH[:, k, :].bitcast(F32), ALU.subtract)\
                   .then_inc(ss(s, "gl"), 1)
            split_l(dve, b0 + 4, 0, 16)
            split_l(dve, b0 + 5, 1, 16)
            for i in range(4):
                for o in (2 * i, 2 * i + 1):
                    dve.wait_ge(acc_read, j0 + 8 + o + 1)
                    dve.tensor_tensor(UN[:, o, :], UN[:, o, :], work1[:, o % 2, :], ALU.mult).then_inc(ss(s, "zz"), 1)
                split_l(dve, b0 + 6 + i, i % 2, 16)
            for k in range(KD):
                dve.wait_ge(ss(s, "h2"), at(s, "h2", k + 1))
                dve.tensor_tensor(XL[:, k, :], UN[:, k, :], XH[:, k, :].bitcast(F32), ALU.subtract)\
                   .then_inc(ss(s, "l2"), 1)
            out_dve(dve, s, b0 + 8, j0 + 16, s0 + 16, Y5, post)

        def s5_pool(pool, s):
            sum_pool(pool, s, "sq_in", "sq_use")
            pool.wait_ge(ss(s, "small0"), at(s, "small0", 1))
            jc = s5c[:, S5_JC:S5_JC + NC + 1].unsqueeze(1).to_broadcast([P, GS, NC + 1])
            pool.memset(RR[:, :, 0:1], 0.0)

            def ph(ins):
                pool.drain()

            def phases(k):
                if k >= 2:
                    pool.wait_ge(ss(s, "x"), at(s, "x", k - 1))
                g = slice(k * GS, (k + 1) * GS)
                fh, fl = (sm[:, n, g].unsqueeze(2).to_broadcast([P, GS, NC + 1]) for n in (9, 10))
                a, n = PHA[:, :, :], PHN[:, :, :]
                ph(pool.tensor_tensor(a, fh, jc, ALU.mult))
                ph(pool.tensor_scalar(n, a, ROUND, -ROUND, ALU.add, ALU.add))
                ph(pool.tensor_tensor(a, a, n, ALU.subtract))
                ph(pool.tensor_tensor(n, fl, jc, ALU.mult))
                ph(pool.tensor_tensor(a, a, n, ALU.add))
                ph(pool.tensor_scalar(n, a, ROUND, -ROUND, ALU.add, ALU.add))
                ph(pool.tensor_tensor(SIN[:, k % 2], a, n, ALU.subtract))
                ph(pool.tensor_scalar(a, a, 0.25, None, ALU.add))
                ph(pool.tensor_scalar(n, a, ROUND, -ROUND, ALU.add, ALU.add))
                pool.tensor_tensor(COS[:, k % 2], a, n, ALU.subtract).then_inc(ss(s, "ph"), 1)
                pool.drain()

            def outmat(k):
                if k >= 1:
                    pool.wait_ge(ss(s, "ydone"), at(s, "ydone", k))
                for a in range(2):
                    g = k * GS + 4 * a
                    shape = [P, 4, CL, GCH]
                    er, ei = (x[:, 1:CL + 1, g:g + 4].rearrange("p j g -> p g j").unsqueeze(3).to_broadcast(shape)
                              for x in (CSJ, SNJ))
                    c1, c2 = (x[:, g:g + 4, :].unsqueeze(2).to_broadcast(shape) for x in (C1, C2))
                    w = G1[:, 4 * a:4 * a + 4]
                    pool.tensor_tensor(w, er, c1, ALU.mult)
                    pool.tensor_tensor(Gx[:, :, :, :], ei, c2, ALU.mult)
                    pool.drain()
                    pool.tensor_tensor(w, w, Gx[:, :, :, :], ALU.add)
                    pool.drain()
                pool.nop().then_inc(ss(s, "g1"), 1)

            def decay(k):
                if k >= 1:
                    pool.wait_ge(ss(s, "z"), at(s, "z", k))
                pool.tensor_copy(RR[:, :, 1:NC], sm[:, 17, k * GS:(k + 1) * GS].unsqueeze(2).to_broadcast([P, GS, NC - 1]))\
                    .then_inc(ss(s, "rr"), 1)
                pool.drain()

            phases(0)
            decay(0)
            pool.wait_ge(ss(s, "small"), at(s, "small", 1))
            phases(1)
            outmat(0)
            for k in range(1, KD):
                decay(k)
                if k + 1 < KD:
                    phases(k + 1)
                outmat(k)
            sum_pool(pool, s, "ysq_in", "ysq_use")
            post_pool(pool, s, True)

        STAGE = {"attn": (attn_sp, attn_pe, attn_act, attn_dve, attn_pool), "s5": (s5_sp, s5_pe, s5_act, s5_dve, s5_pool),
                 "ffn": (ffn_sp, ffn_pe, ffn_act, ffn_dve, ffn_pool),
                 "conv": (conv_sp, conv_pe, conv_act, conv_dve, conv_pool)}

        block = ctx.enter_context(nc.Block())
        x_rows = io["x"][0].rearrange("(t p) d -> p t d", p=P)
        out_rows = io["out"][0].rearrange("(t p) d -> p t d", p=P)

        @block.sync
        def _(sp):
            sp.dma_start(XN[:, :, :], x_rows).then_inc(xn_in, 16)
            for n, group in enumerate(VEC_ROWS):
                at = 0
                for name, rows in group:
                    src = io[name]
                    if len(src.shape) == 3:
                        src = src.rearrange("l n (k q) -> (l n k) q", q=P)
                    else:
                        src = src.rearrange("l (k q) -> (l k) q", q=P)
                    sp.dma_start(vrow[at:at + rows, n, :], src).then_inc(vec_in, 16)
                    at += rows
            for name, row in HEAD_ROWS:
                for h in range(2):
                    sp.dma_start(vrow[row:row + 2, 1, 64 * h:64 * h + 64], io[name]).then_inc(vec_in, 16)
            sp.dma_start(lamrow[0:1, :, :], io["diff_lambda"].rearrange("(o l) a d -> o l (a d)", o=1))\
              .then_inc(vec_in, 16)
            dw = io["cv_dw_2"].rearrange("l j (k q) -> (l j k) q", q=P)
            for n in range(2):
                sp.dma_start(vrow[0:DW_ROWS, 2 + n, :], dw[n * DW_ROWS:(n + 1) * DW_ROWS, :]).then_inc(vec_in, 16)
            for s in stages:
                STAGE[kind(s)][0](sp, s)
            sp.wait_ge(o_cp, 4 * KD)
            sp.dma_start(out_rows, XN[:, :, :]).then_inc(stored, 16)
            sp.wait_ge(stored, 16)

        @block.gpsimd
        def _(pool):
            pool.memset(ident[:, :], 0.0).then_inc(ident_0, 1)
            pool.memset(ones[:, :], 1.0)
            pool.memset(eps_c[:, :], EPS)
            pool.wait_ge(ident_0, 1)
            pool.affine_select(out=ident[:, :], in_=ident[:, :], compare_op=ALU.not_equal, fill=1.0, base=0,
                               pattern=[[-1, P]], channel_multiplier=1)
            pool.drain()
            pool.nop().then_inc(ident_ok, 1)
            for s in stages:
                STAGE[kind(s)][4](pool, s)

        @block.tensor
        def _(pe):
            pe.wait_ge(ident_ok, 1)
            pe.wait_ge(vec_in, 16 * VEC_DMAS)
            for n in range(2):
                r = VEC_N[n]
                pe.transpose(bank[n][:, 0:r], vrow[0:r, n, :], ident[0:r, 0:r]).then_inc(vec_t, 1)
            for n in range(2):
                pe.transpose(bank[6 + n][:, 0:DW_ROWS], vrow[0:DW_ROWS, 2 + n, :], ident[0:DW_ROWS, 0:DW_ROWS])\
                  .then_inc(vec_t, 1)
            pe.matmul(bank[5][:, 0:2 * P], ones[0:1, :], lamrow[0:1, :, :], start=True, stop=True).then_inc(vec_t, 1)
            pe.wait_ge(xn_in, 16)
            for k in range(KD):
                if k >= 3:
                    pe.wait_ge(x_ok, k - 2)
                for t in range(4):
                    mm = pe.transpose(bank[2 + k % 3][:, t * P:(t + 1) * P], XN[:, t, k * P:(k + 1) * P], ident[:, :])
                mm.then_inc(x_tr, 1)
            for s in stages:
                STAGE[kind(s)][1](pe, s)
            for k in range(KD):
                pe.wait_ge(last_x, at(stages[-1], "x_new", k + 1))
                for t in range(4):
                    n = k * 4 + t
                    if n >= 4:
                        pe.wait_ge(o_cp, n - 3)
                    pe.transpose(bank[n % 4][:, 0:P], X[:, k, t * P:(t + 1) * P], ident[:, :]).then_inc(o_tr, 1)

        @block.scalar
        def _(act):
            act.wait_ge(ident_ok, 1)
            act.wait_ge(vec_ok, 2)
            act.activation(lamv[:, :, 2:4], lamv[:, :, 0:2], ACT.Exp).then_inc(lam_exp, 1)
            split_h(act, 0, 0, cells[0], 0)
            for s in stages:
                STAGE[kind(s)][2](act, s)

        @block.vector
        def _(dve):
            for n in range(2):
                dve.wait_ge(vec_t, n + 1)
                dve.tensor_copy(vecT[:, 128 * n:128 * n + VEC_N[n]], bank[n][:, 0:VEC_N[n]])
            for n in range(2):
                dve.wait_ge(vec_t, 3 + n)
                dve.tensor_copy(dwT[:, n * DW_ROWS:(n + 1) * DW_ROWS], bank[6 + n][:, 0:DW_ROWS])
            dve.wait_ge(vec_t, 5)
            dve.tensor_copy(lamb[:, :, :], bank[5][:, 0:2 * P].rearrange("p (l n) -> p l n", l=2))
            dve.drain()
            for n in (0, 2, 3, 5):
                g = vecT[:, COL["norm_post_2"] + KD * n:COL["norm_post_2"] + KD * (n + 1)]
                dve.tensor_scalar(g, g, 0.5, None, ALU.mult)
            for l in range(2):
                for i in range(2):
                    dve.tensor_tensor(work1[:, 0, 64 * l + 32 * i:64 * l + 32 * i + 32], lamb[:, l, 64 * i:64 * i + 32],
                                      lamb[:, l, 64 * i + 32:64 * i + 64], ALU.mult)
            dve.drain()
            dve.tensor_reduce(lamv[:, :, 0:2], work1[:, 0, 0:P].rearrange("p (l i d) -> p l i d", l=2, i=2), AX, ALU.add)
            c1 = 128 + VEC_ROW1
            dve.tensor_copy(headg[:, :], vecT[:, c1:c1 + 6])
            dve.drain()
            for l in range(2):
                dve.tensor_scalar(headg[:, l:l + 1], headg[:, l:l + 1], 1.0 - LAMBDA0[l], None, ALU.mult)
            dve.drain()
            dve.nop().then_inc(vec_ok, 2)
            dve.wait_ge(lam_exp, 1)
            dve.tensor_tensor(nlam[:, :], lamv[:, :, 3], lamv[:, :, 2], ALU.subtract)
            dve.drain()
            for l in range(2):
                dve.tensor_scalar(nlam[:, l:l + 1], nlam[:, l:l + 1], -LAMBDA0[l], None, ALU.add)
            for k in range(KD):
                dve.wait_ge(x_tr, k + 1)
                dve.tensor_copy(X[:, k, :], bank[2 + k % 3][:, :]).then_inc(x_ok, 1)
            split_l(dve, 0, 0, cells[0])
            for s in stages:
                STAGE[kind(s)][3](dve, s)
            for k in range(KD):
                for t in range(4):
                    n = k * 4 + t
                    dve.wait_ge(o_tr, n + 1)
                    dve.tensor_copy(XN[:, t, k * P:(k + 1) * P], bank[n % 4][:, 0:P]).then_inc(o_cp, 1)


INS = ["x", "mem", "pre_norm", "w_in", "diff_lambda", "diff_subln", "gqa_q_norm", "gqa_k_norm", "mem_norm", "w_mem_kv",
       "w_out", "post_norm", "norm_pre_2", "norm_post_2", "ffn_w1_2", "ffn_w3_2", "ffn_w2_2", "s5_w_in_2", "s5_a_re_2",
       "s5_a_im_2", "s5_log_dt_2", "s5_b_re_2", "s5_b_im_2", "s5_c_re_2", "s5_c_im_2", "s5_d_2", "s5_w_glu_2",
       "s5_b_glu_2", "s5_w_out_2", "cv_w_in_2", "cv_b_in_2", "cv_dw_2", "cv_dw_b_2", "cv_ln_g_2", "cv_ln_b_2",
       "cv_w_out_2", "cv_b_out_2"]


def kernel(**inputs):
    import concourse.bacc as bacc
    from concourse.bass_utils import run_bass_kernel_spmd

    nc = bacc.Bacc("TRN2", target_bir_lowering=False, num_devices=1)
    arrays, io = {}, {}
    given = {name: np.ascontiguousarray(inputs[name]) for name in INS}
    given.update(shape_tables())
    for name, a in given.items():
        arrays[f"in_{name}_dram"] = a
        io[name] = nc.dram_tensor(f"in_{name}_dram", a.shape, mybir.dt.from_np(a.dtype), kind="ExternalInput").ap()
    io["out"] = nc.dram_tensor("out_dram", (1, T, D), F32, kind="ExternalOutput").ap()
    program(nc, io)
    r = run_bass_kernel_spmd(nc, [arrays], core_ids=[0])
    return r.results[0]["out_dram"]
```

```python
import math
from contextlib import ExitStack

import numpy as np
import concourse.bass as bass
from concourse import mybir

ALU = mybir.AluOpType
ACT = mybir.ActivationFunctionType
F32 = mybir.dt.float32
F32R = mybir.dt.float32r
AX = mybir.AxisListType.X

P = 128
T = 512
D = 1024
KD = D // P
FF = 2816
KF = FF // P
EPS = 1e-6
CONV_W = 31
CONV_PAD = CONV_W - 1
GROUPS, GCH, STATES = 64, 16, 64
CL = 8
NC = T // CL
GS = 8
PI2 = 2 * math.pi
PI2_A = 6.28125
PI2_B = round((PI2 - PI2_A) * 2 ** 20) / 2 ** 20
PI2_C = PI2 - PI2_A - PI2_B
TURN = 6.283185
ROUND = 1.5 * 2 ** 23
NMEM = 256
GRID_W = 64
ROPE_DIM = 32

LAMBDA0 = [0.8 - 0.6 * math.exp(-0.3 * l) for l in range(2)]

FULL = ["attn0", "attn1", "ffn0", "s5", "ffn1", "ffn2", "conv", "ffn3"]


def block_plan(stages):
    plan, sizes = {}, []
    for s in stages:
        plan[s] = len(sizes)
        if s.startswith("attn"):
            sizes += [16] * (2 + 12 + 4)
        elif s.startswith("ffn"):
            sizes += [16] * (FF // 128) + [11] * (2 * KD)
        elif s == "s5":
            sizes += [16] * 12
        elif s == "conv":
            sizes += [16] * 12
    return plan, sizes


S5_JC = CL + 1
S5_EYE = S5_JC + NC + 1
S5_SGN = S5_EYE + P + (CL - 1) * GCH
S5_SWAP = S5_SGN + 3
S5_COLS = S5_SWAP + P


def shape_tables():
    inv = (np.float32(10000.0) ** (-np.arange(0, ROPE_DIM, 2, dtype=np.float32) / np.float32(ROPE_DIM))).astype(np.float32)
    t = np.arange(T)
    p = np.arange(P)
    sign = np.where(p % ROPE_DIM < 16, -1.0, 1.0).astype(np.float32)[:, None]
    linear = t[None, :] * np.ones((P, 1), np.int64)
    axial = np.where((p % 64 < 32)[:, None], t[None, :] // GRID_W, t[None, :] % GRID_W)
    out = np.zeros((P, 4, T), np.float32)
    for n, pos in enumerate((linear, axial)):
        ang = pos.astype(np.float32) * inv[p % 16][:, None]
        out[:, 2 * n] = np.cos(ang)
        out[:, 2 * n + 1] = sign * np.sin(ang)
    perm = np.zeros((P, 2, P), np.float32)
    perm[p ^ 16, 0, p] = 1.0
    perm[:, 1] = (p[:, None] // 64 == p[None, :] // 64)
    s5 = np.zeros((P, S5_COLS), np.float32)
    s5[:, 0:CL + 1] = np.arange(CL + 1)
    s5[:, S5_JC:S5_JC + NC + 1] = CL * np.arange(NC + 1)
    s5[p, S5_EYE + p + (CL - 1) * GCH] = 1.0
    s5[:, S5_SGN] = np.where(p < 64, -1.0, 1.0)
    s5[:, S5_SGN + 1] = -s5[:, S5_SGN]
    s5[:, S5_SGN + 2] = TURN * s5[:, S5_SGN + 1]
    s5[p, S5_SWAP + (p ^ 64)] = 1.0
    return {"rope_c": out, "perm_c": perm, "s5_c": s5}


def program(nc, io, stages=FULL):
    ctx = ExitStack()
    with ctx:
        def sb(name, shape, dt=F32, stack=ctx):
            return stack.enter_context(nc.sbuf_tensor(name, shape, dt))

        def sem(name):
            return ctx.enter_context(nc.semaphore(name))

        first_block, cells = block_plan(stages)

        X = sb("X", [P, KD, T])
        rstd = sb("rstd", [P, T])
        rms = sb("rms", [P, T])
        rcol = sb("rcol", [P, 2, 4])
        raw = sb("raw", [P, 2, 2048])
        WH = sb("WH", [P, 2, 2048], F32R)
        WL = sb("WL", [P, 2, 2048], F32R)
        ident = sb("ident", [P, P])
        ones = sb("ones", [P, P])
        eps_c = sb("eps_c", [P, 1])
        vecT = sb("vecT", [P, 256])
        dwT = sb("dwT", [P, CONV_W * KD])
        lamb = sb("lamb", [P, 2, P])
        lamv = sb("lamv", [P, 2, 4])
        nlam = sb("nlam", [P, 2])
        headg = sb("headg", [P, 6])
        sq = sb("sq", [P, 2, T])
        ssq = sb("ssq", [P, T])
        ra = ExitStack()
        work1r = sb("work1r", [P, 2, T], F32R, ra)
        work2r = sb("work2r", [P, 2, T], F32R, ra)
        ra.close()
        work1 = sb("work1", [P, 2, T])
        work2 = sb("work2", [P, 2, T])

        ra = ExitStack()
        XH = sb("XH", [P, KD, T], F32R, ra)
        XL = sb("XL", [P, KD, T], F32R, ra)
        ra.close()
        ra = ExitStack()
        YA = sb("YA", [P, KD, T], F32, ra)
        ra.close()

        ra = ExitStack()
        VdH = sb("VdH", [P, 4, 384], F32R, ra)
        VdL = sb("VdL", [P, 4, 384], F32R, ra)
        VgH = sb("VgH", [P, 4, 2, P], F32R, ra)
        VgL = sb("VgL", [P, 4, 2, P], F32R, ra)
        ra2 = ExitStack()
        rope = sb("rope", [P, 4, T], F32, ra2)
        ra2.close()
        QK6 = sb("QK6", [P, 6, T], F32R, ra)
        ra.close()

        ra = ExitStack()
        YR = sb("YR", [P, KD, CL, NC], F32, ra)
        ra.close()

        sb("region_a", [P, 2 * KD, T])

        rb = ExitStack()
        HH = sb("HH", [P, KF, T], F32R, rb)
        HL = sb("HL", [P, KF, T], F32R, rb)
        rb.close()
        rb = ExitStack()
        XN = sb("XN", [P, 4, D], F32, rb)
        vrow = sb("vrow", [P, 4, P], F32, rb)
        lamrow = sb("lamrow", [1, 2, P], F32, rb)
        rb.close()
        rb = ExitStack()
        perm = sb("perm", [P, 2, P], F32, rb)
        rb2 = ExitStack()
        PRr = sb("PRr", [P, 24, T], F32R, rb2)
        gk2r = sb("gk2r", [P, T], F32R, rb2)
        MKr = sb("MKr", [P, 2, NMEM], F32R, rb2)
        rb2.close()
        PR = sb("PR", [P, 24, T], F32, rb)
        gk2 = sb("gk2", [P, T], F32, rb)
        MK = sb("MK", [P, 2, NMEM], F32, rb)
        VmH = sb("VmH", [P, 2, 256], F32R, rb)
        VmL = sb("VmL", [P, 2, 256], F32R, rb)
        stats = sb("stats", [P, 4, 8], F32, rb)
        rb2 = ExitStack()
        E = sb("E", [P, 6, T], F32, rb2)
        PTH = sb("PTH", [P, 4, T], F32R, rb2)
        PTL = sb("PTL", [P, 4, T], F32R, rb2)
        rb2.close()
        MEMN = sb("MEMN", [P, 2, D], F32, rb)
        MH = sb("MH", [P, KD, NMEM], F32R, rb)
        ML = sb("ML", [P, KD, NMEM], F32R, rb)
        rb.close()
        rb = ExitStack()
        ZP = sb("ZP", [P, KD, CONV_PAD + T], F32, rb)
        CV = sb("CV", [P, KD, T], F32, rb)
        SG = sb("SG", [P, 2, T], F32, rb)
        ZH = sb("ZH", [P, KD, CONV_PAD + T], F32R, rb)
        ZL = sb("ZL", [P, KD, CONV_PAD + T], F32R, rb)
        dwH = sb("dwH", [P, CONV_W * KD], F32R, rb)
        dwL = sb("dwL", [P, CONV_W * KD], F32R, rb)
        DIAGS = 30
        diag = sb("diag", [P, DIAGS, P], F32R, rb)
        YC = ZP[:, :, 0:T]
        rb.close()

        rb = ExitStack()
        UN = sb("UN", [P, KD, T], F32, rb)
        rb2 = ExitStack()
        s5c = sb("s5c", [P, S5_COLS], F32, rb2)
        sm = sb("sm", [P, 20, GROUPS], F32, rb2)
        CSJ = sb("CSJ", [P, CL + 1, GROUPS], F32, rb2)
        SNJ = sb("SNJ", [P, CL + 1, GROUPS], F32, rb2)
        B1 = sb("B1", [P, GROUPS, GCH], F32, rb2)
        B2 = sb("B2", [P, GROUPS, GCH], F32, rb2)
        C1 = sb("C1", [P, GROUPS, GCH], F32, rb2)
        C2 = sb("C2", [P, GROUPS, GCH], F32, rb2)
        Wt = sb("Wt", [P, GS, CL, GCH], F32, rb2)
        W1 = sb("W1", [P, GS, 192], F32, rb2)
        Wx = sb("Wx", [P, 4, CL, GCH], F32, rb2)
        G1 = sb("G1", [P, GS, CL, GCH], F32, rb2)
        Gx = sb("Gx", [P, 4, CL, GCH], F32, rb2)
        MT = sb("MT", [P, GS, CL, GCH], F32, rb2)
        COS = sb("COS", [P, 2, GS, NC + 1], F32, rb2)
        SIN = sb("SIN", [P, 2, GS, NC + 1], F32, rb2)
        PHA = sb("PHA", [P, GS, NC + 1], F32, rb2)
        PHN = sb("PHN", [P, GS, NC + 1], F32, rb2)
        U = sb("U", [P, 2, GS, NC], F32, rb2)
        YS = sb("YS", [P, GS, NC], F32, rb2)
        RR = sb("RR", [P, GS, NC], F32, rb2)
        KS = sb("KS", [P, GS, GCH], F32, rb2)
        rb2.close()
        Y5 = sb("Y5", [P, KD, T], F32, rb)
        rb.close()
        u_scr = nc.dram_tensor("u_scr", [KD, P, GS, NC], F32).ap()
        y_scr = nc.dram_tensor("y_scr", [KD, P, CL, NC], F32).ap()

        bank = [ctx.enter_context(nc.psum_tensor(f"bank{i}", [P, T], F32)) for i in range(8)]
        stat = bank[7]

        raw_in = [sem("raw_in0"), sem("raw_in1")]
        h_done = sem("h_done")
        l_done = sem("l_done")
        mm_done = sem("mm_done")
        acc_read = sem("acc_read")
        lam_exp = sem("lam_exp")
        perm_in = sem("perm_in")
        vec_in = sem("vec_in")
        vec_t = sem("vec_t")
        vec_ok = sem("vec_ok")
        ident_0 = sem("ident_0")
        ident_ok = sem("ident_ok")
        xn_in = sem("xn_in")
        x_tr = sem("x_tr")
        x_ok = sem("x_ok")
        o_tr = sem("o_tr")
        o_cp = sem("o_cp")
        stored = sem("stored")

        VEC_ROWS = [
            [("pre_norm", 16), ("post_norm", 16), ("mem_norm", 16), ("norm_pre_2", 48), ("s5_d_2", 8),
             ("s5_b_glu_2", 8), ("cv_dw_b_2", 8)],
            [("norm_post_2", 48), ("cv_b_in_2", 16), ("cv_ln_g_2", 8), ("cv_ln_b_2", 8), ("cv_b_out_2", 8)],
        ]
        VEC_ROW1 = sum(r for _, r in VEC_ROWS[1])
        COL = {}
        for n, group in enumerate(VEC_ROWS):
            row = 128 * n
            for name, rows in group:
                COL[name] = row
                row += rows
        HEAD_ROWS = [("diff_subln", VEC_ROW1), ("gqa_q_norm", VEC_ROW1 + 2), ("gqa_k_norm", VEC_ROW1 + 4)]
        VEC_DMAS = sum(len(g) for g in VEC_ROWS) + 2 + 6 + 1
        DW_ROWS = CONV_W * KD // 2
        VEC_N = [sum(r for _, r in VEC_ROWS[0]), VEC_ROW1 + 6]

        def col(name, k, n=0):
            c = COL[name] + KD * n + k
            return vecT[:, c:c + 1]

        ADDS = {
            "all": dict(xh=KD, xl=KD, sq_in=KD, sq_use=KD, stat_ok=1, rms_ok=1, ysq_in=KD, ysq_use=KD, ystat_ok=1,
                        yrms_ok=1, ycol_ok=1, ybc_ok=1, t_ok=KD // 2, x_even=KD // 2, x_odd=KD // 2),
            "ffn": dict(silu=KF, hid=KF, hh=KF, hl=KF),
            "attn": dict(mem_in=16, perm_in=16, rope_in=16, mem_n=2, ml=KD, mem_t=KD, mh=KD, mrms=1, msq=2, vm_t=1, vmh=1, vml=1,
                         v_t=4, vh=4, vl=4, gsq=4, gms=4, grms=4, gn=4, swapped=10, roped=10, ready=1, gate=8,
                         s=88, e=88, nb=64, p=24, rsum=64, scaled=64, qh=14, ql=14, pt=64, pth=64, ptl=64, pv=32, o=16, osq=3, oms=3, orms=3, on=3, og=3,
                         mixh=KD, mixl=KD),
        }
        sems = {}

        def kind(s):
            return s if s == "s5" else s.rstrip("0123")

        def shared_by(s, name):
            return "all" if name in ADDS["all"] else kind(s)

        def ss(s, name):
            key = f"{shared_by(s, name)}_{name}"
            if key not in sems:
                sems[key] = sem(key)
            return sems[key]

        def at(s, name, n):
            who = shared_by(s, name)
            before = [x for x in stages[:stages.index(s)] if who == "all" or kind(x) == who]
            return n + (len(before) * ADDS[who][name] if before else 0)

        tiles_before, first_step, n_tiles, n_steps = {}, {}, 0, 0
        for s in stages:
            tiles_before[s], first_step[s] = n_tiles, n_steps
            n_tiles += {"attn": 4 + 24 + 8, "ffn": 2 * KF + KD, "s5": 24, "conv": 24}[kind(s)]
            n_steps += {"attn": 4 + 24 + 8, "ffn": 2 * KF + 2 * KD, "s5": 24, "conv": 24}[kind(s)]

        def split_h(act, b, slot, n, used):
            act.wait_ge(raw_in[slot], (b - slot) * 8 + 16)
            if not isinstance(b, int) or b >= 2:
                act.wait_ge(mm_done, used)
            act.activation(WH[:, slot, 0:n * P], raw[:, slot, 0:n * P], ACT.Copy).then_inc(h_done, 1)

        def split_l(dve, b, slot, n):
            dve.wait_ge(h_done, b + 1)
            dve.tensor_tensor(WL[:, slot, 0:n * P], raw[:, slot, 0:n * P], WH[:, slot, 0:n * P].bitcast(F32),
                              ALU.subtract).then_inc(l_done, 1)

        def load_block(sp, b, slot, dst, src):
            if not isinstance(b, int) or b >= 2:
                sp.wait_ge(l_done, b - 1)
            sp.dma_start(dst, src).then_inc(raw_in[slot], 16)

        def raw3(slot, k):
            return raw[:, slot, 0:2048].rearrange("p (k n) -> p k n", k=k)

        def mm3(pe, out, w, h, l, start, stop):
            slot, c = w
            pe.matmul(out, WH[:, slot, c:c + P], h, start=start, stop=False)
            pe.matmul(out, WH[:, slot, c:c + P], l, start=False, stop=False)
            return pe.matmul(out, WL[:, slot, c:c + P], h, start=False, stop=stop)

        def pe_block256(pe, b, slot, j, mh, ml, n=T, arrive=None):
            pe.wait_ge(l_done, b + 1)
            for o in range(2):
                acc = bank[2 * slot + o][:, 0:n]
                if not isinstance(j, int) or j + o >= 4:
                    pe.wait_ge(acc_read, j + o - 3)
                for k in range(KD):
                    if arrive is not None and o == 0:
                        pe.wait_ge(ss(*arrive), at(*arrive, k + 1))
                    mm = mm3(pe, acc, (slot, k * 256 + o * P), mh[:, k, 0:n], ml[:, k, 0:n], k == 0, k == KD - 1)
                mm.then_inc(mm_done, 1)

        def before(s):
            n = stages.index(s)
            return stages[n - 1] if n else None

        def x_final(eng, s, k):
            last = before(s) if s else stages[-1]
            if last is None:
                eng.wait_ge(x_ok, k + 1)
            else:
                name = ("x_even", "x_odd")[k % 2]
                eng.wait_ge(ss(last, name), at(last, name, k // 2 + 1))

        def x_all(eng, s):
            x_final(eng, s, KD - 2)
            x_final(eng, s, KD - 1)

        def pre_act(act, s, gain, b=None):
            def lead(k):
                x_final(act, s, k)
                act.activation(XH[:, k, :], X[:, k, :], ACT.Copy, scale=gain(k)).then_inc(ss(s, "xh"), 1)

            def square(k):
                if k >= 3:
                    act.wait_ge(ss(s, "sq_use"), at(s, "sq_use", k - 1))
                act.activation(square_to(k), X[:, k, :], ACT.Square).then_inc(ss(s, "sq_in"), 1)

            for k in range(4):
                lead(k)
            square(0)
            lead(4)
            lead(5)
            square(1)
            lead(6)
            lead(7)
            square(2)
            if b is not None:
                split_h(act, b, 1, 16, first_step[s])
            for k in range(3, KD):
                square(k)

        def square_to(k):
            return ssq[:, :] if k == 0 else sq[:, k % 2, :]

        def rms_act(act, s, which):
            act.wait_ge(ss(s, which + "stat_ok"), at(s, which + "stat_ok", 1))
            act.activation(rms[:, :], stat[:, :], ACT.Sqrt, bias=eps_c[:, 0:1], scale=1.0 / D)\
               .then_inc(ss(s, which + "rms_ok"), 1)

        def low_x(dve, s, k):
            dve.wait_ge(ss(s, "xh"), at(s, "xh", k + 1))
            dve.scalar_tensor_tensor(XL[:, k, :], X[:, k, :], gains(s)[0](k), XH[:, k, :].bitcast(F32),
                                     ALU.mult, ALU.subtract).then_inc(ss(s, "xl"), 1)

        def early(s):
            return before(s) is not None and not s.startswith("attn")

        def pre_dve(dve, s, gain):
            if not early(s):
                for k in range(KD):
                    low_x(dve, s, k)

        def sum_pool(pool, s, src_sem, use_sem):
            for k in range(KD):
                pool.wait_ge(ss(s, src_sem), at(s, src_sem, k + 1))
                if k == 0:
                    ins = pool.nop()
                else:
                    ins = pool.tensor_tensor(ssq[:, :], ssq[:, :], sq[:, k % 2, :], ALU.add)
                ins.then_inc(ss(s, use_sem), 1)
                pool.wait_ge(ss(s, use_sem), at(s, use_sem, k + 1))

        def stat_pe(pe, s, use_sem, ok_sem):
            pe.wait_ge(ss(s, use_sem), at(s, use_sem, KD))
            pe.matmul(stat[:, :], ones[:, :], ssq[:, :], start=True, stop=True).then_inc(ss(s, ok_sem), 1)

        def ystat_pe(pe, s):
            pe.wait_ge(ss(s, "ysq_use"), at(s, "ysq_use", KD))
            for t in range(4):
                mm = pe.matmul(stat[:, t:t + 1], ssq[:, t * P:(t + 1) * P], ones[:, 0:1], start=True, stop=True)
            mm.then_inc(ss(s, "ystat_ok"), 1)
            pe.wait_ge(ss(s, "ycol_ok"), at(s, "ycol_ok", 1))
            for t in range(4):
                mm = pe.matmul(stat[:, t * P:(t + 1) * P], rcol[:, 1, t:t + 1].to_broadcast([P, P]), ident[:, :],
                               start=True, stop=True)
            mm.then_inc(ss(s, "ybc_ok"), 1)

        def yrms_act(act, s):
            act.wait_ge(ss(s, "ystat_ok"), at(s, "ystat_ok", 1))
            act.activation(rcol[:, 0, :], stat[:, 0:4], ACT.Sqrt, bias=eps_c[:, 0:1], scale=1.0 / D)\
               .then_inc(ss(s, "yrms_ok"), 1)

        def yrstd_dve(dve, s):
            dve.wait_ge(ss(s, "yrms_ok"), at(s, "yrms_ok", 1))
            dve.reciprocal(rcol[:, 1, :], rcol[:, 0, :]).then_inc(ss(s, "ycol_ok"), 1)
            dve.wait_ge(ss(s, "ybc_ok"), at(s, "ybc_ok", 1))

        def rstd_dve(dve, s, which):
            dve.wait_ge(ss(s, which + "rms_ok"), at(s, which + "rms_ok", 1))
            dve.reciprocal(rstd[:, :], rms[:, :])
            dve.drain()

        def post_dve(dve, s, Y, gain):
            n = stages.index(s) + 1
            after = stages[n] if n < len(stages) and early(stages[n]) else None
            for k in range(KD):
                t = (work1, work2)[k // 2 % 2][:, k % 2, :]
                if k >= 4 and k % 2 == 0:
                    dve.wait_ge(ss(s, "x_even"), at(s, "x_even", k // 2 - 1))
                ins = dve.scalar_tensor_tensor(t, Y[:, k, :], gain(k), stat[:, :], ALU.mult, ALU.mult)
                if k % 2 == 0:
                    ins.then_inc(ss(s, "t_ok"), 1)
                else:
                    dve.drain()
                    dve.tensor_tensor(X[:, k, :], X[:, k, :], t, ALU.add).then_inc(ss(s, "x_odd"), 1)
                    dve.drain()
                if after is not None and k >= 3:
                    low_x(dve, after, k - 3)
            if after is not None:
                for k in range(KD - 3, KD):
                    low_x(dve, after, k)

        def post_pool(pool, s):
            for k in range(0, KD, 2):
                pool.wait_ge(ss(s, "t_ok"), at(s, "t_ok", k // 2 + 1))
                t = (work1, work2)[k // 2 % 2][:, 0, :]
                pool.tensor_tensor(X[:, k, :], X[:, k, :], t, ALU.add).then_inc(ss(s, "x_even"), 1)

        def gains(s):
            if s.startswith("attn"):
                l = int(s[4])
                return (lambda k: col("pre_norm", k, l)), (lambda k: col("post_norm", k, l))
            n = {"ffn0": 0, "s5": 1, "ffn1": 2, "ffn2": 3, "conv": 4, "ffn3": 5}[s]
            return (lambda k: col("norm_pre_2", k, n)), (lambda k: col("norm_post_2", k, n))

        NP = FF // 256

        def ffn_sp(sp, s):
            n, b0 = int(s[3]), first_block[s]
            l, j = n // 2, n % 2
            w1 = io["ffn_w1_2"][l, j].rearrange("(k p) n -> p k n", p=P)
            w3 = io["ffn_w3_2"][l, j].rearrange("(k p) n -> p k n", p=P)
            w2 = io["ffn_w2_2"][l, j].rearrange("(k p) n -> p k n", p=P)

            def pair(i):
                c = i * 256
                load_block(sp, b0 + 2 * i, 0, raw3(0, KD), w1[:, :, bass.ds(c, 256)])
                load_block(sp, b0 + 2 * i + 1, 1, raw3(1, KD), w3[:, :, bass.ds(c, 256)])

            pair(0)
            with sp.Fori(1, NP) as i:
                pair(i)
            with sp.Fori(0, KD) as o:
                for half in range(2):
                    load_block(sp, b0 + 2 * NP + 2 * o + half, half,
                               raw[:, half, 0:11 * P].rearrange("p (k n) -> p k n", k=11),
                               w2[:, 11 * half:11 * half + 11, bass.ds(o * P, P)])

        def ffn_pe(pe, s):
            b0, j0, s0 = first_block[s], tiles_before[s], first_step[s]

            def pair(i, first):
                pe_block256(pe, b0 + 2 * i, 0, j0 + 4 * i, XH, XL, arrive=(s, "xl") if first else None)
                if first:
                    stat_pe(pe, s, "sq_use", "stat_ok")
                pe_block256(pe, b0 + 2 * i + 1, 1, j0 + 4 * i + 2, XH, XL)

            pair(0, True)
            with pe.Fori(1, NP) as i:
                pair(i, False)
            b1, j1, s1 = b0 + 2 * NP, j0 + 2 * KF, s0 + 2 * KF

            def down(i, first):
                for q in range(4):
                    acc = bank[q]
                    pe.wait_ge(acc_read, j1 + 4 * i + q - 3)
                    for half in range(2):
                        pe.wait_ge(l_done, b1 + 8 * i + 2 * q + half + 1)
                        for k in range(11):
                            kk = 11 * half + k
                            if first and q == 0:
                                pe.wait_ge(ss(s, "hl"), at(s, "hl", kk + 1))
                            mm = mm3(pe, acc[:, :], (half, k * P), HH[:, kk, :], HL[:, kk, :], kk == 0, kk == KF - 1)
                        mm.then_inc(mm_done, 1)

            down(0, True)
            down(1, False)
            ystat_pe(pe, s)

        def ffn_act(act, s):
            b0, j0, s0 = first_block[s], tiles_before[s], first_step[s]
            pre, post = gains(s)
            pre_act(act, s, pre, b0 + 1)
            rms_act(act, s, "")

            def silu(i, o):
                act.wait_ge(acc_read, j0 + 4 * i + o + 1)
                if not isinstance(i, int) or i >= 1:
                    act.wait_ge(ss(s, "hid"), at(s, "hid", 2 * i + o - 1))
                act.activation(work2[:, o, :], work1[:, o, :], ACT.Silu).then_inc(ss(s, "silu"), 1)

            def hidden(i, o):
                act.wait_ge(ss(s, "hid"), at(s, "hid", 2 * i + o + 1))
                act.activation(HH[:, bass.ds(2 * i + o, 1), :], work1[:, o, :], ACT.Copy).then_inc(ss(s, "hh"), 1)

            def pair(i, nxt):
                silu(i, 0)
                silu(i, 1)
                split_h(act, b0 + 2 * i + 2, 0, nxt, s0 + 4 * i + 2)
                hidden(i, 0)
                hidden(i, 1)
                split_h(act, b0 + 2 * i + 3, 1, nxt, s0 + 4 * i + 4)

            pair(0, 16)
            with act.Fori(1, NP - 1) as i:
                pair(i, 16)
            pair(NP - 1, 11)
            b1, j1, s1 = b0 + 2 * NP, j0 + 2 * KF, s0 + 2 * KF

            def square(o, slot):
                act.wait_ge(acc_read, j1 + o + 1)
                if not isinstance(o, int) or o >= 2:
                    act.wait_ge(ss(s, "ysq_use"), at(s, "ysq_use", o - 1))
                dst = sq[:, slot, :] if not isinstance(o, int) else square_to(o)
                act.activation(dst, YA[:, bass.ds(o, 1), :], ACT.Square).then_inc(ss(s, "ysq_in"), 1)

            def out_pair(i, last):
                for q in range(2):
                    o = 2 * i + q
                    if not last or q == 0:
                        split_h(act, b1 + 2 * o + 2, 0, 11, s1 + 2 * o + 1)
                        split_h(act, b1 + 2 * o + 3, 1, 11, s1 + 2 * o + 2)
                    elif b1 + 2 * o + 2 < len(cells):
                        split_h(act, b1 + 2 * o + 2, 0, cells[b1 + 2 * o + 2], s1 + 2 * o + 1)
                    square(o, q)

            out_pair(0, False)
            with act.Fori(1, KD // 2 - 1) as i:
                out_pair(i, False)
            out_pair(KD // 2 - 1, True)
            yrms_act(act, s)

        def ffn_dve(dve, s):
            b0, j0, s0 = first_block[s], tiles_before[s], first_step[s]
            pre, post = gains(s)
            pre_dve(dve, s, pre)
            split_l(dve, b0 + 1, 1, 16)
            rstd_dve(dve, s, "")

            def up1(i, o):
                dve.wait_ge(mm_done, s0 + 4 * i + o + 1)
                if not isinstance(i, int) or i >= 1:
                    dve.wait_ge(ss(s, "hl"), at(s, "hl", 2 * i + o - 1))
                dve.tensor_tensor(work1[:, o, :], bank[o][:, :], rstd[:, :], ALU.mult).then_inc(acc_read, 1)

            def up3(i, o):
                dve.wait_ge(mm_done, s0 + 4 * i + 2 + o + 1)
                dve.wait_ge(ss(s, "silu"), at(s, "silu", 2 * i + o + 1))
                dve.tensor_tensor(work1[:, o, :], bank[2 + o][:, :], rstd[:, :], ALU.mult).then_inc(acc_read, 1)
                dve.drain()
                dve.tensor_tensor(work1[:, o, :], work1[:, o, :], work2[:, o, :], ALU.mult).then_inc(ss(s, "hid"), 1)

            def hidden(i, o):
                dve.wait_ge(ss(s, "hh"), at(s, "hh", 2 * i + o + 1))
                dve.tensor_tensor(HL[:, bass.ds(2 * i + o, 1), :], work1[:, o, :],
                                  HH[:, bass.ds(2 * i + o, 1), :].bitcast(F32), ALU.subtract)\
                   .then_inc(ss(s, "hl"), 1)

            def pair(i, nxt):
                for o in range(2):
                    up1(i, o)
                split_l(dve, b0 + 2 * i + 2, 0, nxt)
                for o in range(2):
                    up3(i, o)
                for o in range(2):
                    hidden(i, o)
                split_l(dve, b0 + 2 * i + 3, 1, nxt)

            pair(0, 16)
            with dve.Fori(1, NP - 1) as i:
                pair(i, 16)
            pair(NP - 1, 11)
            b1, j1, s1 = b0 + 2 * NP, j0 + 2 * KF, s0 + 2 * KF

            def out_tile(o, bk, n0, n1):
                if n0:
                    split_l(dve, b1 + 2 * o + 2, 0, n0)
                if n1:
                    split_l(dve, b1 + 2 * o + 3, 1, n1)
                dve.wait_ge(mm_done, s1 + 2 * o + 2)
                dve.tensor_copy(YA[:, bass.ds(o, 1), :], bank[bk][:, :]).then_inc(acc_read, 1)

            for o in range(KD):
                b = b1 + 2 * o + 2
                if o < KD - 1:
                    out_tile(o, o % 4, 11, 11)
                else:
                    out_tile(o, o % 4, cells[b] if b < len(cells) else 0, 0)
            yrstd_dve(dve, s)
            post_dve(dve, s, YA, post)

        def ffn_pool(pool, s):
            sum_pool(pool, s, "sq_in", "sq_use")
            sum_pool(pool, s, "ysq_in", "ysq_use")
            post_pool(pool, s)

        def nxt(b):
            return cells[b] if b < len(cells) else 0

        def out_sp(sp, b, w):
            w3 = w.rearrange("(k p) n -> p k n", p=P)
            for i in range(4):
                load_block(sp, b + i, i % 2, raw3(i % 2, KD), w3[:, :, i * 256:(i + 1) * 256])

        def out_pe(pe, s, b, j, arrive):
            for i in range(4):
                pe_block256(pe, b + i, i % 2, j + 2 * i, XH, XL, arrive=arrive if i == 0 else None)
            ystat_pe(pe, s)

        def out_act(act, s, b, j, step, Y):
            for i in range(4):
                if i < 3 and nxt(b + i + 2):
                    split_h(act, b + i + 2, i % 2, nxt(b + i + 2), step + 2 * i + 2)
                for o in (2 * i, 2 * i + 1):
                    act.wait_ge(acc_read, j + o + 1)
                    if o >= 2:
                        act.wait_ge(ss(s, "ysq_use"), at(s, "ysq_use", o - 1))
                    act.activation(square_to(o), Y[:, o, :], ACT.Square).then_inc(ss(s, "ysq_in"), 1)
            yrms_act(act, s)

        def out_dve(dve, s, b, j, step, Y, gain, bias=None):
            for i in range(4):
                for o in (2 * i, 2 * i + 1):
                    dve.wait_ge(mm_done, step + o + 1)
                    acc = bank[2 * (i % 2) + o % 2]
                    if bias is None:
                        dve.tensor_copy(Y[:, o, :], acc[:, :]).then_inc(acc_read, 1)
                    else:
                        dve.tensor_scalar(Y[:, o, :], acc[:, :], bias(o), None, ALU.add).then_inc(acc_read, 1)
                if i < 3 and nxt(b + i + 2):
                    split_l(dve, b + i + 2, i % 2, nxt(b + i + 2))
            yrstd_dve(dve, s)
            post_dve(dve, s, Y, gain)

        def conv_sp(sp, s):
            b0 = first_block[s]
            w = io["cv_w_in_2"][0].rearrange("(k p) n -> p k n", p=P)
            for i in range(4):
                load_block(sp, b0 + 2 * i, 0, raw3(0, KD), w[:, :, i * 256:(i + 1) * 256])
                load_block(sp, b0 + 2 * i + 1, 1, raw3(1, KD), w[:, :, D + i * 256:D + (i + 1) * 256])
            out_sp(sp, b0 + 8, io["cv_w_out_2"][0])

        def share(k):
            return 17 if k >= KD - 2 else 14

        TAPS_P = [sum(share(k) for k in range(n)) for n in range(KD + 1)]

        def taps_pe(pe, s, k):
            n, acc = share(k), bank[4 + k % 3][:, :]
            pe.wait_ge(ss(s, "zl"), at(s, "zl", k + 1))
            if k >= 3:
                pe.wait_ge(ss(s, "cv"), at(s, "cv", k - 2))
            for t in range(n):
                d = 2 * (TAPS_P[k] + t)
                pe.wait_ge(ss(s, "diag"), at(s, "diag", d + 2))
                high, low = diag[:, d % DIAGS, :], diag[:, (d + 1) % DIAGS, :]
                pe.matmul(acc, high, ZH[:, k, t:t + T], start=(t == 0), stop=False)
                pe.matmul(acc, high, ZL[:, k, t:t + T], start=False, stop=False)
                pe.matmul(acc, low, ZH[:, k, t:t + T], start=False, stop=(t == n - 1)).then_inc(ss(s, "ptap"), 1)

        def taps_dve(dve, k, t0, t1):
            for t in range(t0, t1):
                dve.scalar_tensor_tensor(CV[:, k, :], ZP[:, k, t:t + T], dwT[:, t * KD + k:t * KD + k + 1],
                                         CV[:, k, :], ALU.mult, ALU.add)
                dve.drain()

        def conv_pe(pe, s):
            b0, j0 = first_block[s], tiles_before[s]
            for i in range(4):
                pe_block256(pe, b0 + 2 * i, 0, j0 + 4 * i, XH, XL, arrive=(s, "xl") if i == 0 else None)
                if i == 0:
                    stat_pe(pe, s, "sq_use", "stat_ok")
                pe_block256(pe, b0 + 2 * i + 1, 1, j0 + 4 * i + 2, XH, XL)
                if i >= 1:
                    taps_pe(pe, s, 2 * i - 2)
                    taps_pe(pe, s, 2 * i - 1)
            taps_pe(pe, s, KD - 2)
            taps_pe(pe, s, KD - 1)
            pe.wait_ge(ss(s, "cvsum"), at(s, "cvsum", KD))
            pe.matmul(stat[:, :], ones[:, :], ssq[:, :], start=True, stop=True).then_inc(ss(s, "cvstat"), 1)
            pe.wait_ge(ss(s, "censum"), at(s, "censum", KD))
            pe.matmul(stat[:, :], ones[:, :], ssq[:, :], start=True, stop=True).then_inc(ss(s, "censtat"), 1)
            out_pe(pe, s, b0 + 8, j0 + 16, (s, "l2"))

        def conv_act(act, s):
            b0, j0, s0 = first_block[s], tiles_before[s], first_step[s]
            pre, post = gains(s)
            pre_act(act, s, pre, b0 + 1)
            rms_act(act, s, "")
            act.activation(dwH[:, :], dwT[:, :], ACT.Copy).then_inc(ss(s, "dwh"), 1)
            act.wait_ge(ss(s, "dwl"), at(s, "dwl", 1))

            for i in range(4):
                split_h(act, b0 + 2 * i + 2, 0, 16, s0 + 4 * i + 2)
                for o in range(2):
                    act.wait_ge(acc_read, j0 + 4 * i + 2 + o + 1)
                    if i >= 1:
                        act.wait_ge(ss(s, "z"), at(s, "z", 2 * i + o - 1))
                    act.activation(SG[:, o, :], work2[:, o, :], ACT.Sigmoid, bias=col("cv_b_in_2", KD + 2 * i + o))\
                       .then_inc(ss(s, "sig"), 1)
                split_h(act, b0 + 2 * i + 3, 1, 16, s0 + 4 * i + 4)
                for k in (2 * i, 2 * i + 1):
                    act.wait_ge(ss(s, "z"), at(s, "z", k + 1))
                    act.activation(ZH[:, k, :], ZP[:, k, :], ACT.Copy).then_inc(ss(s, "zh"), 1)
                    last = CONV_W - 1
                    act.activation(CV[:, k, :], ZP[:, k, last:last + T], ACT.Identity, bias=col("cv_dw_b_2", k),
                                   scale=dwT[:, last * KD + k:last * KD + k + 1]).then_inc(ss(s, "cva"), 1)
                for k in (2 * i, 2 * i + 1):
                    for t in range(share(k)):
                        n = TAPS_P[k] + t
                        if 2 * n >= DIAGS:
                            act.wait_ge(ss(s, "ptap"), at(s, "ptap", n - DIAGS // 2 + 1))
                        for m, part in enumerate((dwH, dwL)):
                            act.activation(diag[:, (2 * n + m) % DIAGS, :], ident[:, :], ACT.Copy,
                                           scale=part[:, t * KD + k:t * KD + k + 1].bitcast(F32))\
                               .then_inc(ss(s, "diag"), 1)
            act.wait_ge(ss(s, "cvstat"), at(s, "cvstat", 1))
            act.activation(rms[:, :], stat[:, :], ACT.Copy, scale=1.0 / D).then_inc(ss(s, "mu"), 1)
            for k in range(KD):
                act.wait_ge(ss(s, "cen"), at(s, "cen", k + 1))
                if k >= 2:
                    act.wait_ge(ss(s, "censum"), at(s, "censum", k - 1))
                act.activation(square_to(k), CV[:, k, :], ACT.Square).then_inc(ss(s, "censq"), 1)
            act.wait_ge(ss(s, "censtat"), at(s, "censtat", 1))
            act.activation(rms[:, :], stat[:, :], ACT.Sqrt, bias=eps_c[:, 0:1], scale=1.0 / D)\
               .then_inc(ss(s, "sigma"), 1)
            for k in range(KD):
                act.wait_ge(ss(s, "nrm"), at(s, "nrm", k + 1))
                act.activation(CV[:, k, :], CV[:, k, :], ACT.Silu, bias=col("cv_ln_b_2", k), scale=col("cv_ln_g_2", k))\
                   .then_inc(ss(s, "zs"), 1)
                act.wait_ge(ss(s, "zs"), at(s, "zs", k + 1))
                act.activation(XH[:, k, :], CV[:, k, :], ACT.Copy).then_inc(ss(s, "h2"), 1)
            out_act(act, s, b0 + 8, j0 + 16, s0 + 16, YC)

        def conv_dve(dve, s):
            b0, j0, s0 = first_block[s], tiles_before[s], first_step[s]
            pre, post = gains(s)
            pre_dve(dve, s, pre)
            split_l(dve, b0 + 1, 1, 16)
            rstd_dve(dve, s, "")
            dve.wait_ge(ss(s, "dwh"), at(s, "dwh", 1))
            dve.tensor_tensor(dwL[:, :], dwT[:, :], dwH[:, :].bitcast(F32), ALU.subtract).then_inc(ss(s, "dwl"), 1)

            def taps(k):
                dve.wait_ge(ss(s, "cva"), at(s, "cva", k + 1))
                taps_dve(dve, k, share(k), CONV_W - 1)

            def merge(k):
                dve.wait_ge(ss(s, "ptap"), at(s, "ptap", TAPS_P[k + 1]))
                dve.tensor_tensor(CV[:, k, :], CV[:, k, :], bank[4 + k % 3][:, :], ALU.add).then_inc(ss(s, "cv"), 1)

            for i in range(4):
                for o in range(2):
                    dve.wait_ge(mm_done, s0 + 4 * i + o + 1)
                    if i >= 1:
                        dve.wait_ge(ss(s, "z"), at(s, "z", 2 * i + o - 1))
                    dve.tensor_tensor(work1[:, o, :], bank[o][:, :], rstd[:, :], ALU.mult).then_inc(acc_read, 1)
                split_l(dve, b0 + 2 * i + 2, 0, 16)
                for o in range(2):
                    dve.wait_ge(mm_done, s0 + 4 * i + 2 + o + 1)
                    if i >= 1:
                        dve.wait_ge(ss(s, "sig"), at(s, "sig", 2 * i + o - 1))
                    dve.tensor_tensor(work2[:, o, :], bank[2 + o][:, :], rstd[:, :], ALU.mult).then_inc(acc_read, 1)
                for o in range(2):
                    dve.wait_ge(ss(s, "sig"), at(s, "sig", 2 * i + o + 1))
                    dve.wait_ge(ss(s, "zpad"), at(s, "zpad", 1))
                    dve.scalar_tensor_tensor(ZP[:, 2 * i + o, CONV_PAD:], work1[:, o, :], col("cv_b_in_2", 2 * i + o),
                                             SG[:, o, :], ALU.add, ALU.mult).then_inc(ss(s, "z"), 1)
                split_l(dve, b0 + 2 * i + 3, 1, 16)
                if i >= 1:
                    merge(2 * i - 2)
                    merge(2 * i - 1)
                taps(2 * i)
                taps(2 * i + 1)
            merge(KD - 2)
            merge(KD - 1)
            dve.wait_ge(ss(s, "mu"), at(s, "mu", 1))
            for k in range(KD):
                dve.tensor_tensor(CV[:, k, :], CV[:, k, :], rms[:, :], ALU.subtract).then_inc(ss(s, "cen"), 1)
            dve.wait_ge(ss(s, "sigma"), at(s, "sigma", 1))
            dve.reciprocal(rstd[:, :], rms[:, :])
            dve.drain()
            for k in range(KD):
                dve.tensor_tensor(CV[:, k, :], CV[:, k, :], rstd[:, :], ALU.mult).then_inc(ss(s, "nrm"), 1)
            for k in range(KD):
                dve.wait_ge(ss(s, "h2"), at(s, "h2", k + 1))
                dve.tensor_tensor(XL[:, k, :], CV[:, k, :], XH[:, k, :].bitcast(F32), ALU.subtract)\
                   .then_inc(ss(s, "l2"), 1)
            out_dve(dve, s, b0 + 8, j0 + 16, s0 + 16, YC, post, lambda o: col("cv_b_out_2", o))

        def conv_pool(pool, s):
            x_all(pool, s)
            pool.memset(ZP[:, :, 0:CONV_PAD], 0.0).then_inc(ss(s, "zpad"), 1)
            sum_pool(pool, s, "sq_in", "sq_use")
            for k in range(KD + 3):
                if k < KD:
                    pool.wait_ge(ss(s, "zh"), at(s, "zh", k + 1))
                    pool.tensor_tensor(ZL[:, k, :], ZP[:, k, :], ZH[:, k, :].bitcast(F32), ALU.subtract)\
                        .then_inc(ss(s, "zl"), 1)
                if k >= 3:
                    pool.wait_ge(ss(s, "cv"), at(s, "cv", k - 2))
                    if k == 3:
                        ins = pool.tensor_copy(ssq[:, :], CV[:, 0, :])
                    else:
                        ins = pool.tensor_tensor(ssq[:, :], ssq[:, :], CV[:, k - 3, :], ALU.add)
                    ins.then_inc(ss(s, "cvsum"), 1)
                    pool.wait_ge(ss(s, "cvsum"), at(s, "cvsum", k - 2))
            sum_pool(pool, s, "censq", "censum")
            sum_pool(pool, s, "ysq_in", "ysq_use")
            post_pool(pool, s)

        DQ, DK, DV, DG, GQ, GK, GV, GG, MQ, MG = 0, 3, 6, 9, 12, 15, 16, 17, 20, 22
        ROPED = [(j, 0) for j in range(DQ, DV)] + [(j, 2) for j in range(GQ, GV)]
        GATES = list(range(DG, DG + 3)) + list(range(GG, GG + 3)) + list(range(MG, MG + 2))
        NHEAD = 16

        def rest(j):
            return PRr[:, j, :]

        SPLIT = [(DQ, rest(DV)), (DQ + 1, rest(DV + 1)), (DQ + 2, rest(DV + 2)), (DK, rest(GV)), (DK + 1, QK6[:, 4, :]),
                 (DK + 2, QK6[:, 5, :]), (GQ, QK6[:, 0, :]), (GQ + 1, QK6[:, 1, :]), (GQ + 2, QK6[:, 2, :]),
                 (GK, QK6[:, 3, :])]
        SPLIT = [(PR[:, j, :], lead, rest(j), j) for j, lead in SPLIT]
        SPLIT += [(gk2[:, :], work2r[:, 1, :], gk2r[:, :], "gk2"),
                  (PR[:, MQ, :], work1r[:, 0, :], rest(MQ), MQ),
                  (PR[:, MQ + 1, :], work1r[:, 1, :], rest(MQ + 1), MQ + 1),
                  (MK[:, :, :].rearrange("p a n -> p (a n)"), work2r[:, 0, :],
                   MKr[:, :, :].rearrange("p a n -> p (a n)"), "MK")]
        QK = {name: (lead, low) for _, lead, low, name in SPLIT}

        def head(h):
            if h < 6:
                parts = [(DQ + h // 2, DK + h // 2, 0, (h % 2) * 64 + 32 * i, 32) for i in range(2)]
                c = (h // 2) * P
                return parts, (lambda m, s: (VdH, VdL)[m][:, s, c:c + P]), 4, 32 ** -0.5, DG + h // 2
            if h < 12:
                g = h - 6
                kv, row = g // 3, (g % 2) * 64
                return ([(GQ + g // 2, GK if kv * 64 == row else "gk2", 0, row, 64)],
                        (lambda m, s: (VgH, VgL)[m][:, s, kv, :]), 4, 0.125, GG + g // 2)
            g = h - 12
            c = (g // 2) * P
            return ([(MQ + g // 2, "MK", (g // 2) * NMEM, (g % 2) * 64, 64)],
                    (lambda m, s: (VmH, VmL)[m][:, s, c:c + P]), 2, 0.125, MG + g // 2)

        HEADS = [head(h) for h in range(NHEAD)]
        UNITS = [(h, t) for h in range(NHEAD) for t in range(4)]
        SCORES = [u for u, (h, t) in enumerate(UNITS) for _ in HEADS[h][0]]
        SCORE0 = [SCORES.index(u) for u in range(len(UNITS))]
        DIFF_UNITS = sum(len(HEADS[h][0]) == 2 for h, t in UNITS)
        LAG_T = 3
        LAG_S = 4
        LAG_V = 6

        def attn_sp(sp, s):
            b0, l = first_block[s], int(s[4])
            wm = io["w_mem_kv"][l].rearrange("(k p) n -> p k n", p=P)
            wi = io["w_in"][l].rearrange("(k p) n -> p k n", p=P)
            for i in range(2):
                load_block(sp, b0 + i, i, raw3(i, KD), wm[:, :, i * 256:(i + 1) * 256])
            with sp.Fori(0, 6) as i:
                for q in range(2):
                    load_block(sp, b0 + 2 + 2 * i + q, q, raw3(q, KD), wi[:, :, bass.ds(i * 512 + q * 256, 256)])
            out_sp(sp, b0 + 14, io["w_out"][l])

        def attn_pool(pool, s):
            l = int(s[4])
            x_all(pool, s)
            pool.dma_start(MEMN[:, :, :], io["mem"][0].rearrange("(t p) d -> p t d", p=P)).then_inc(ss(s, "mem_in"), 16)
            pool.dma_start(perm[:, :, :], io["perm_c"]).then_inc(ss(s, "perm_in"), 16)
            sum_pool(pool, s, "sq_in", "sq_use")
            pool.wait_ge(mm_done, first_step[s] + 28)
            pool.dma_start(rope[:, :, :], io["rope_c"]).then_inc(ss(s, "rope_in"), 16)

            for n, (x, lead, low, _) in enumerate(SPLIT):
                if n == 9:
                    pool.wait_ge(ss(s, "ready"), at(s, "ready", 1))
                pool.wait_ge(ss(s, "qh"), at(s, "qh", n + 1))
                pool.tensor_tensor(low, x, lead.bitcast(F32), ALU.subtract).then_inc(ss(s, "ql"), 1)
            sum_pool(pool, s, "ysq_in", "ysq_use")
            post_pool(pool, s)

        def attn_pe(pe, s):
            b0, j0, s0 = first_block[s], tiles_before[s], first_step[s]
            for k in range(KD):
                for t in range(2):
                    pe.wait_ge(ss(s, "mem_n"), at(s, "mem_n", t + 1))
                    if k >= 3:
                        pe.wait_ge(ss(s, "ml"), at(s, "ml", k - 2))
                    mm = pe.transpose(bank[4 + k % 3][:, t * P:(t + 1) * P], MEMN[:, t, k * P:(k + 1) * P], ident[:, :])
                mm.then_inc(ss(s, "mem_t"), 1)
            for i in range(2):
                pe_block256(pe, b0 + i, i, j0 + 2 * i, MH, ML, NMEM, arrive=(s, "ml") if i == 0 else None)

            def block(i, q, first=False):
                pe_block256(pe, b0 + 2 + 2 * i + q, q, j0 + 4 + 4 * i + 2 * q, XH, XL,
                            arrive=(s, "xl") if first else None)

            def head_squares(n):
                pe.wait_ge(ss(s, "gsq"), at(s, "gsq", n + 1))
                if n >= 2:
                    pe.wait_ge(ss(s, "grms"), at(s, "grms", n - 1))
                pe.matmul(bank[5 + n % 2][:, :], perm[:, 1, :], sq[:, n % 2, :], start=True, stop=True)\
                  .then_inc(ss(s, "gms"), 1)

            block(0, 0, True)
            stat_pe(pe, s, "sq_use", "stat_ok")
            block(0, 1)
            with pe.Fori(1, 4) as i:
                block(i, 0)
                block(i, 1)
            block(4, 0)
            for o in range(2):
                for t in range(2):
                    mm = pe.transpose(bank[4][:, (2 * t + o) * P:(2 * t + o + 1) * P], work2[:, o, t * P:(t + 1) * P],
                                      ident[:, :])
            mm.then_inc(ss(s, "vm_t"), 1)
            pe.wait_ge(ss(s, "perm_in"), at(s, "perm_in", 16))
            block(4, 1)
            head_squares(0)
            block(5, 0)
            head_squares(1)
            head_squares(2)
            block(5, 1)
            head_squares(3)
            pe.wait_ge(ss(s, "vml"), at(s, "vml", 1))
            for n, j in enumerate((DV, DV + 1, DV + 2, GV)):
                pe.wait_ge(acc_read, j0 + 4 + j + 1)
                if n == 1:
                    pe.wait_ge(ss(s, "grms"), at(s, "grms", 4))
                if n >= 2:
                    pe.wait_ge(ss(s, "vl"), at(s, "vl", n - 1))
                for t in range(4):
                    mm = pe.transpose(bank[4 + n % 2][:, t * P:(t + 1) * P], PR[:, j, t * P:(t + 1) * P], ident[:, :])
                mm.then_inc(ss(s, "v_t"), 1)
            for n, (j, _) in enumerate(ROPED):
                if j >= GQ:
                    pe.wait_ge(ss(s, "gn"), at(s, "gn", j - GQ + 1))
                if n >= 2:
                    pe.wait_ge(ss(s, "roped"), at(s, "roped", n - 1))
                pe.matmul(bank[6 + n % 2][:, :], perm[:, 0, :], PR[:, j, :], start=True, stop=True)\
                  .then_inc(ss(s, "swapped"), 1)
            def scores(u):
                h, t = UNITS[u]
                if t == 0:
                    pe.wait_ge(ss(s, "ql"), at(s, "ql", 6 if h < 6 else 11 if h < 12 else 14))
                for i, (q, k, k0, row, n) in enumerate(HEADS[h][0]):
                    m = SCORE0[u] + i
                    keys = HEADS[h][2] * P
                    (qh, ql), (kh, kl) = [[x[row:row + n, c:c + w] for x in QK[name]]
                                          for name, c, w in ((q, t * P, P), (k, k0, keys))]
                    acc = bank[m % 4][:, 0:keys]
                    if m >= 4:
                        pe.wait_ge(ss(s, "e"), at(s, "e", m - 3))
                    pe.matmul(acc, qh, kh, start=True, stop=False)
                    pe.matmul(acc, qh, kl, start=False, stop=False)
                    pe.matmul(acc, ql, kh, start=False, stop=True).then_inc(ss(s, "s"), 1)

            def transposes(u):
                h, t = UNITS[u]
                if u < DIFF_UNITS:
                    pe.wait_ge(ss(s, "p"), at(s, "p", u + 1))
                else:
                    pe.wait_ge(ss(s, "scaled"), at(s, "scaled", u + 1))
                if u >= 2:
                    pe.wait_ge(ss(s, "ptl"), at(s, "ptl", u - 1))
                for c in range(HEADS[h][2]):
                    mm = pe.transpose(bank[4 + u % 2][:, c * P:(c + 1) * P], E[:, SCORE0[u] % 6, c * P:(c + 1) * P],
                                      ident[:, :])
                mm.then_inc(ss(s, "pt"), 1)

            def values(h, half):
                _, v, nk, _, _ = HEADS[h]
                pe.wait_ge(ss(s, "ptl"), at(s, "ptl", 4 * h + 2 * half + 2))
                if h >= 2 and half == 0:
                    pe.wait_ge(ss(s, "o"), at(s, "o", h - 1))
                cols = slice(256 * half, 256 * half + 256)
                out = bank[6 + h % 2][:, cols]
                for c in range(nk):
                    pe.matmul(out, v(0, c), PTH[:, c, cols], start=(c == 0), stop=False)
                    pe.matmul(out, v(0, c), PTL[:, c, cols], start=False, stop=False)
                    mm = pe.matmul(out, v(1, c), PTH[:, c, cols], start=False, stop=(c == nk - 1))
                mm.then_inc(ss(s, "pv"), 1)

            for u in range(len(UNITS) + LAG_V):
                if u < len(UNITS):
                    scores(u)
                if u >= LAG_V and (u - LAG_V) % 2 == 1:
                    values(UNITS[u - LAG_V][0], UNITS[u - LAG_V][1] // 2)
                if LAG_T <= u < len(UNITS) + LAG_T:
                    transposes(u - LAG_T)
            for n in range(3):
                pe.wait_ge(ss(s, "osq"), at(s, "osq", n + 1))
                pe.matmul(bank[n][:, :], perm[:, 1, :], sq[:, n % 2, :], start=True, stop=True).then_inc(ss(s, "oms"), 1)
            out_pe(pe, s, b0 + 14, j0 + 28, (s, "mixl"))

        def attn_act(act, s):
            b0, j0, s0 = first_block[s], tiles_before[s], first_step[s]
            l = int(s[4])
            pre, post = gains(s)
            split_h(act, b0 + 1, 1, 16, s0)
            for t in range(2):
                act.wait_ge(ss(s, "mem_in"), at(s, "mem_in", 16))
                act.activation(sq[:, :, :], MEMN[:, t, :].rearrange("p (a n) -> p a n", a=2), ACT.Square,
                               accum_out=stats[:, 0, t:t + 1]).then_inc(ss(s, "msq"), 1)
                act.wait_ge(ss(s, "msq"), at(s, "msq", t + 1))
            act.activation(stats[:, 1, 0:2], stats[:, 0, 0:2], ACT.Sqrt, bias=eps_c[:, 0:1], scale=1.0 / D)\
               .then_inc(ss(s, "mrms"), 1)
            for k in range(KD):
                act.wait_ge(ss(s, "mem_t"), at(s, "mem_t", k + 1))
                act.activation(MH[:, k, :], bank[4 + k % 3][:, 0:NMEM], ACT.Copy, scale=col("mem_norm", k, l))\
                   .then_inc(ss(s, "mh"), 1)
            pre_act(act, s, pre)
            split_h(act, b0 + 2, 0, 16, s0 + 2)
            split_h(act, b0 + 3, 1, 16, s0 + 4)
            rms_act(act, s, "")
            def lead(i, q):
                split_h(act, b0 + 4 + 2 * i + q, q, 16, s0 + 4 + 4 * i + 2 * q + 2)

            def head_square(n):
                act.wait_ge(acc_read, j0 + 4 + GQ + n + 1)
                if n >= 2:
                    act.wait_ge(ss(s, "gms"), at(s, "gms", n - 1))
                act.activation(sq[:, n % 2, :], PR[:, GQ + n, :], ACT.Square).then_inc(ss(s, "gsq"), 1)

            def head_rms(n):
                act.wait_ge(ss(s, "gms"), at(s, "gms", n + 1))
                if n >= 2:
                    act.wait_ge(ss(s, "gn"), at(s, "gn", n - 1))
                act.activation(work2[:, n % 2, :], bank[5 + n % 2][:, :], ACT.Sqrt, bias=eps_c[:, 0:1], scale=1.0 / 64)\
                   .then_inc(ss(s, "grms"), 1)

            with act.Fori(0, 4) as i:
                for q in range(2):
                    lead(i, q)
            lead(4, 0)
            head_square(0)
            head_square(1)
            act.wait_ge(ss(s, "vm_t"), at(s, "vm_t", 1))
            act.activation(VmH[:, :, :], bank[4][:, :].rearrange("p (t n) -> p t n", t=2), ACT.Copy)\
               .then_inc(ss(s, "vmh"), 1)
            lead(4, 1)
            head_rms(0)
            head_square(2)
            lead(5, 0)
            head_rms(1)
            head_square(3)
            head_rms(2)
            lead(5, 1)
            head_rms(3)
            for n in range(4):
                act.wait_ge(ss(s, "v_t"), at(s, "v_t", n + 1))
                b = bank[4 + n % 2][:, :]
                if n < 3:
                    act.activation(VdH[:, :, n * P:(n + 1) * P], b.rearrange("p (t c) -> p t c", t=4), ACT.Copy)\
                       .then_inc(ss(s, "vh"), 1)
                else:
                    for half in range(2):
                        ins = act.activation(VgH[:, :, :, 64 * half:64 * half + 64],
                                             b.rearrange("p (t g c) -> p t g c", t=4, g=2), ACT.Copy)
                    ins.then_inc(ss(s, "vh"), 1)
            act.wait_ge(acc_read, j0 + 4 + 24)
            for n, j in enumerate(GATES):
                act.activation(PR[:, j, :], PR[:, j, :], ACT.Silu).then_inc(ss(s, "gate"), 1)
            for n, (x, high, _, _) in enumerate(SPLIT):
                if n < 6:
                    act.wait_ge(ss(s, "roped"), at(s, "roped", n + 1))
                elif n == 6:
                    act.wait_ge(ss(s, "roped"), at(s, "roped", 10))
                elif n == 10:
                    act.wait_ge(ss(s, "ready"), at(s, "ready", 1))
                act.activation(high, x, ACT.Copy).then_inc(ss(s, "qh"), 1)
            n_u = len(UNITS)

            def scale_first(u):
                m, nk = SCORE0[u], HEADS[UNITS[u][0]][2]
                act.wait_ge(ss(s, "rsum"), at(s, "rsum", u + 1))
                e = E[:, m % 6, 0:nk * P]
                act.activation(e, e, ACT.Copy, scale=stats[:, 3, m % 8:m % 8 + 1]).then_inc(ss(s, "scaled"), 1)

            def exps(u):
                h, t = UNITS[u]
                parts, _, nk, scale, _ = HEADS[h]
                act.wait_ge(ss(s, "nb"), at(s, "nb", u + 1))
                last = SCORE0[u] + len(parts) - 1
                if last >= 6:
                    act.wait_ge(ss(s, "pt"), at(s, "pt", SCORES[last - 6] + 1))
                for i in range(len(parts)):
                    m = SCORE0[u] + i
                    act.activation(E[:, m % 6, 0:nk * P], bank[m % 4][:, 0:nk * P], ACT.Exp,
                                   bias=stats[:, 1, m % 8:m % 8 + 1], scale=scale,
                                   accum_out=stats[:, 2, m % 8:m % 8 + 1]).then_inc(ss(s, "e"), 1)

            def split_p(u):
                h, t = UNITS[u]
                nk = HEADS[h][2]
                act.wait_ge(ss(s, "pt"), at(s, "pt", u + 1))
                if h >= 1:
                    act.wait_ge(ss(s, "pv"), at(s, "pv", 2 * h - 1 + t // 2))
                act.activation(PTH[:, 0:nk, t * P:(t + 1) * P],
                               bank[4 + u % 2][:, 0:nk * P].rearrange("p (c n) -> p c n", c=nk), ACT.Copy)\
                   .then_inc(ss(s, "pth"), 1)

            for u in range(n_u + LAG_S):
                if u >= LAG_S:
                    split_p(u - LAG_S)
                if u < n_u:
                    exps(u)
                if 1 <= u <= n_u:
                    scale_first(u - 1)
            for n in range(3):
                act.wait_ge(ss(s, "o"), at(s, "o", 2 * n + 2))
                if n >= 2:
                    act.wait_ge(ss(s, "oms"), at(s, "oms", n - 1))
                act.activation(sq[:, n % 2, :], PR[:, DQ + n, :], ACT.Square).then_inc(ss(s, "osq"), 1)
                act.wait_ge(ss(s, "oms"), at(s, "oms", n + 1))
                if n >= 2:
                    act.wait_ge(ss(s, "on"), at(s, "on", n - 1))
                act.activation(work2[:, n % 2, :], bank[n][:, :], ACT.Sqrt, bias=eps_c[:, 0:1], scale=1.0 / 64)\
                   .then_inc(ss(s, "orms"), 1)
            for k, j in enumerate(GATES):
                if k < 3:
                    act.wait_ge(ss(s, "og"), at(s, "og", k + 1))
                else:
                    act.wait_ge(ss(s, "o"), at(s, "o", NHEAD))
                act.activation(XH[:, k, :], PR[:, j, :], ACT.Copy).then_inc(ss(s, "mixh"), 1)
            out_act(act, s, b0 + 14, j0 + 28, s0 + 28, PR)

        def attn_dve(dve, s):
            b0, j0, s0 = first_block[s], tiles_before[s], first_step[s]
            l = int(s[4])
            pre, post = gains(s)
            split_l(dve, b0 + 1, 1, 16)
            dve.wait_ge(ss(s, "mrms"), at(s, "mrms", 1))
            dve.reciprocal(stats[:, 2, 0:2], stats[:, 1, 0:2])
            dve.drain()
            for t in range(2):
                dve.tensor_scalar(MEMN[:, t, :], MEMN[:, t, :], stats[:, 2, t:t + 1], None, ALU.mult)\
                   .then_inc(ss(s, "mem_n"), 1)
            for k in range(KD):
                dve.wait_ge(ss(s, "mh"), at(s, "mh", k + 1))
                dve.scalar_tensor_tensor(ML[:, k, :], bank[4 + k % 3][:, 0:NMEM], col("mem_norm", k, l),
                                         MH[:, k, :].bitcast(F32), ALU.mult, ALU.subtract).then_inc(ss(s, "ml"), 1)
            pre_dve(dve, s, pre)
            for i in range(2):
                for o in range(2):
                    dve.wait_ge(mm_done, s0 + 2 * i + o + 1)
                    dst = MK[:, o, :] if i == 0 else work2[:, o, 0:NMEM]
                    dve.tensor_copy(dst, bank[2 * i + o][:, 0:NMEM]).then_inc(acc_read, 1)
                split_l(dve, b0 + 2 + i, i, 16)
            rstd_dve(dve, s, "")
            def tiles(i, q):
                for o in range(2):
                    j = 4 * i + 2 * q + o
                    dve.wait_ge(mm_done, s0 + 4 + j + 1)
                    dve.tensor_tensor(PR[:, bass.ds(j, 1), :], bank[2 * q + o][:, :], rstd[:, :], ALU.mult)\
                       .then_inc(acc_read, 1)
                split_l(dve, b0 + 4 + 2 * i + q, q, 16)

            def head_norm(n):
                dve.wait_ge(ss(s, "grms"), at(s, "grms", n + 1))
                dve.reciprocal(work1[:, n % 2, :], work2[:, n % 2, :])
                dve.drain()
                g = headg[:, (2 if n < 3 else 4) + l:(3 if n < 3 else 5) + l]
                dve.scalar_tensor_tensor(PR[:, GQ + n, :], PR[:, GQ + n, :], g, work1[:, n % 2, :], ALU.mult, ALU.mult)\
                   .then_inc(ss(s, "gn"), 1)

            with dve.Fori(0, 4) as i:
                for q in range(2):
                    tiles(i, q)
            tiles(4, 0)
            dve.wait_ge(ss(s, "vmh"), at(s, "vmh", 1))
            dve.tensor_tensor(VmL[:, :, :], bank[4][:, :].rearrange("p (t n) -> p t n", t=2), VmH[:, :, :].bitcast(F32),
                              ALU.subtract).then_inc(ss(s, "vml"), 1)
            tiles(4, 1)
            head_norm(0)
            tiles(5, 0)
            head_norm(1)
            head_norm(2)
            tiles(5, 1)
            head_norm(3)
            for n in range(4):
                dve.wait_ge(ss(s, "vh"), at(s, "vh", n + 1))
                b = bank[4 + n % 2][:, :]
                if n < 3:
                    dve.tensor_tensor(VdL[:, :, n * P:(n + 1) * P], b.rearrange("p (t c) -> p t c", t=4),
                                      VdH[:, :, n * P:(n + 1) * P].bitcast(F32), ALU.subtract).then_inc(ss(s, "vl"), 1)
                else:
                    for half in range(2):
                        c = slice(64 * half, 64 * half + 64)
                        ins = dve.tensor_tensor(VgL[:, :, :, c], b.rearrange("p (t g c) -> p t g c", t=4, g=2),
                                                VgH[:, :, :, c].bitcast(F32), ALU.subtract)
                    ins.then_inc(ss(s, "vl"), 1)
            dve.wait_ge(ss(s, "rope_in"), at(s, "rope_in", 16))
            for n, (j, tab) in enumerate(ROPED):
                if n == 0:
                    dve.wait_ge(ss(s, "gn"), at(s, "gn", 4))
                dve.wait_ge(ss(s, "swapped"), at(s, "swapped", n + 1))
                dve.tensor_tensor(PR[:, j, :], PR[:, j, :], rope[:, tab, :], ALU.mult)
                dve.tensor_tensor(work1[:, n % 2, :], bank[6 + n % 2][:, :], rope[:, tab + 1, :], ALU.mult)
                dve.drain()
                dve.tensor_tensor(PR[:, j, :], PR[:, j, :], work1[:, n % 2, :], ALU.add).then_inc(ss(s, "roped"), 1)
            dve.drain()
            dve.tensor_copy(gk2[64:128, :], PR[0:64, GK, :])
            dve.tensor_copy(gk2[0:64, :], PR[64:128, GK, :])
            dve.drain()
            dve.nop().then_inc(ss(s, "ready"), 1)

            def maxima(u):
                h, t = UNITS[u]
                parts, _, nk, scale, _ = HEADS[h]
                m, n = SCORE0[u], len(parts)
                for i in range(n):
                    c = (m + i) % 8
                    dve.wait_ge(ss(s, "s"), at(s, "s", m + i + 1))
                    dve.tensor_reduce(stats[:, 0, c:c + 1], bank[(m + i) % 4][:, 0:nk * P], AX, ALU.max)
                dve.drain()
                dve.tensor_scalar(stats[:, 1, m % 8:m % 8 + n], stats[:, 0, m % 8:m % 8 + n], -scale, None, ALU.mult)\
                   .then_inc(ss(s, "nb"), 1)

            def split_p(u):
                h, t = UNITS[u]
                nk = HEADS[h][2]
                dve.wait_ge(ss(s, "pth"), at(s, "pth", u + 1))
                dve.tensor_tensor(PTL[:, 0:nk, t * P:(t + 1) * P],
                                  bank[4 + u % 2][:, 0:nk * P].rearrange("p (c n) -> p c n", c=nk),
                                  PTH[:, 0:nk, t * P:(t + 1) * P].bitcast(F32), ALU.subtract).then_inc(ss(s, "ptl"), 1)

            def sums(u):
                n, c = len(HEADS[UNITS[u][0]][0]), SCORE0[u] % 8
                dve.wait_ge(ss(s, "e"), at(s, "e", SCORE0[u] + n))
                ins = dve.reciprocal(stats[:, 3, c:c + n], stats[:, 2, c:c + n])
                if n == 2:
                    dve.drain()
                    ins = dve.tensor_scalar(stats[:, 3, c + 1:c + 2], stats[:, 3, c + 1:c + 2], nlam[:, l:l + 1], None,
                                            ALU.mult)
                ins.then_inc(ss(s, "rsum"), 1)

            def combine(u):
                m = SCORE0[u]
                dve.wait_ge(ss(s, "scaled"), at(s, "scaled", u + 1))
                dve.scalar_tensor_tensor(E[:, m % 6, :], E[:, (m + 1) % 6, :], stats[:, 3, (m + 1) % 8:(m + 1) % 8 + 1],
                                         E[:, m % 6, :], ALU.mult, ALU.add).then_inc(ss(s, "p"), 1)

            def outputs(h):
                row = (h % 2) * 64
                dve.wait_ge(ss(s, "pv"), at(s, "pv", 2 * h + 2))
                acc = bank[6 + h % 2][row:row + 64, :]
                if h < 6:
                    ins = dve.tensor_copy(PR[row:row + 64, DQ + h // 2, :], acc)
                else:
                    g = PR[row:row + 64, HEADS[h][4], :]
                    ins = dve.tensor_tensor(g, acc, g, ALU.mult)
                ins.then_inc(ss(s, "o"), 1)

            dve.wait_ge(ss(s, "gate"), at(s, "gate", len(GATES)))
            for u in range(len(UNITS) + LAG_V + 1):
                if u < len(UNITS):
                    maxima(u)
                if 2 <= u < DIFF_UNITS + 2:
                    combine(u - 2)
                if LAG_S <= u < len(UNITS) + LAG_S:
                    split_p(u - LAG_S)
                if 1 <= u <= len(UNITS):
                    sums(u - 1)
                if u > LAG_V and UNITS[u - LAG_V - 1][1] == 3:
                    outputs(UNITS[u - LAG_V - 1][0])
            for n in range(3):
                dve.wait_ge(ss(s, "orms"), at(s, "orms", n + 1))
                dve.reciprocal(work1[:, n % 2, :], work2[:, n % 2, :])
                dve.drain()
                dve.scalar_tensor_tensor(work1[:, n % 2, :], PR[:, DQ + n, :], headg[:, l:l + 1], work1[:, n % 2, :],
                                         ALU.mult, ALU.mult).then_inc(ss(s, "on"), 1)
                dve.wait_ge(ss(s, "on"), at(s, "on", n + 1))
                dve.tensor_tensor(PR[:, DG + n, :], PR[:, DG + n, :], work1[:, n % 2, :], ALU.mult)\
                   .then_inc(ss(s, "og"), 1)
            for k, j in enumerate(GATES):
                dve.wait_ge(ss(s, "mixh"), at(s, "mixh", k + 1))
                dve.tensor_tensor(XL[:, k, :], PR[:, j, :], XH[:, k, :].bitcast(F32), ALU.subtract)\
                   .then_inc(ss(s, "mixl"), 1)
            out_dve(dve, s, b0 + 14, j0 + 28, s0 + 28, PR, post)

        a_rows = Gx[:, :, :, :].rearrange("p a s h -> p (a s h)")[:, 0:2 * P].rearrange("p (i n) -> p i n", i=2)
        dt_row = KS[0:1, 0:GROUPS // GCH, :].rearrange("p a h -> p (a h)")
        c_rows = [x[:, :, :, :].rearrange("p g s h -> p g (s h)") for x in (G1, MT)]

        def s5_sp(sp, s):
            b0 = first_block[s]
            w = [io[n][0].rearrange("(k p) n -> p k n", p=P) for n in ("s5_w_in_2", "s5_w_glu_2")]
            for i in range(2):
                load_block(sp, b0 + i, i, raw3(i, KD), w[0][:, :, i * 256:(i + 1) * 256])
            x_all(sp, s)
            par = ss(s, "par_in")
            sp.dma_start(s5c[:, :], io["s5_c"]).then_inc(par, 16)
            for i, n in enumerate(("s5_a_re_2", "s5_a_im_2")):
                for h in range(2):
                    sp.dma_start(a_rows[0:GROUPS, i, 64 * h:64 * h + 64], io[n][0]).then_inc(par, 16)
            sp.dma_start(dt_row, io["s5_log_dt_2"]).then_inc(par, 16)
            br, bi = (io[n][0].rearrange("g p h -> p g h") for n in ("s5_b_re_2", "s5_b_im_2"))
            for dst, src in ((B1[0:64], br), (B1[64:128], bi), (B2[0:64], bi), (B2[64:128], br)):
                sp.dma_start(dst, src).then_inc(ss(s, "b_in"), 16)
            cr, ci = (io[n][0].rearrange("g h p -> (g h) p").rearrange("(t q) p -> q t p", q=P)
                      for n in ("s5_c_re_2", "s5_c_im_2"))
            for i, pair in enumerate(((cr, ci), (ci, cr))):
                for h in range(2):
                    sp.dma_start(c_rows[i][:, :, 64 * h:64 * h + 64], pair[h]).then_inc(ss(s, "c_in"), 16)
            for i in range(2, 4):
                load_block(sp, b0 + i, i % 2, raw3(i % 2, KD), w[0][:, :, i * 256:(i + 1) * 256])
            def u_load(k):
                if k >= 2:
                    sp.wait_ge(ss(s, "ydone"), at(s, "ydone", k - 1))
                sp.dma_start(U[:, k % 2], u_scr[k]).then_inc(ss(s, "u_in"), 16)

            for k in range(KD):
                sp.wait_ge(ss(s, "us"), at(s, "us", k + 1))
                for g in range(GS):
                    sp.dma_start(u_scr[k, :, g, :].rearrange("(s h) c -> h s c", s=CL),
                                 rms[g * GCH:(g + 1) * GCH, :].rearrange("p (s c) -> p s c", s=CL))\
                      .then_inc(ss(s, "u_out"), 16)
                sp.wait_ge(ss(s, "u_out"), at(s, "u_out", 16 * GS * (k + 1)))
                if k < 2:
                    u_load(k)
                if k in (1, 3):
                    i = k // 2
                    load_block(sp, b0 + 4 + i, i, raw3(i, KD), w[1][:, :, i * 256:(i + 1) * 256])
            for k in range(KD):
                sp.wait_ge(ss(s, "ys"), at(s, "ys", k + 1))
                for t in range(CL):
                    sp.dma_start(y_scr[k, :, t, :].rearrange("(g h) c -> h g c", g=GS),
                                 YS[t * GCH:(t + 1) * GCH]).then_inc(ss(s, "y_out"), 16)
                if k + 2 < KD:
                    sp.wait_ge(ss(s, "u_in"), at(s, "u_in", 16 * (k + 2)))
                    u_load(k + 2)
                sp.wait_ge(ss(s, "y_out"), at(s, "y_out", 16 * CL * (k + 1)))
                if k >= 1:
                    sp.wait_ge(ss(s, "y_in"), at(s, "y_in", 16 * k))
                sp.dma_start(YR[:, k], y_scr[k]).then_inc(ss(s, "y_in"), 16)
            for i in range(2, 4):
                load_block(sp, b0 + 4 + i, i % 2, raw3(i % 2, KD), w[1][:, :, i * 256:(i + 1) * 256])
            out_sp(sp, b0 + 8, io["s5_w_out_2"][0])

        def s5_pe(pe, s):
            b0, j0, s0 = first_block[s], tiles_before[s], first_step[s]
            pe_block256(pe, b0, 0, j0, XH, XL, arrive=(s, "xl"))
            stat_pe(pe, s, "sq_use", "stat_ok")
            pe_block256(pe, b0 + 1, 1, j0 + 2, XH, XL)
            pe.wait_ge(ss(s, "par_in"), at(s, "par_in", 16 * 6))
            for i in range(2):
                pe.transpose(bank[5][:, 64 * i:64 * i + 64], a_rows[0:GROUPS, i, :], ident[0:GROUPS, 0:GROUPS])
            pe.matmul(bank[5][:, 128:192], ones[0:1, :], dt_row, start=True, stop=True)\
              .then_inc(ss(s, "par_t"), 1)
            pe.wait_ge(ss(s, "c_in"), at(s, "c_in", 16 * 4))
            for i in range(2):
                for n in (2 * i, 2 * i + 1):
                    if n >= 2:
                        pe.wait_ge(ss(s, "c_cp"), at(s, "c_cp", n - 1))
                    for t in range(4):
                        mm = pe.transpose(bank[4 + 2 * (n % 2)][:, t * P:(t + 1) * P], c_rows[n // 2][:, 4 * (n % 2) + t, :],
                                          ident[:, :])
                    mm.then_inc(ss(s, "c_t"), 1)
                pe_block256(pe, b0 + 2 + i, i, j0 + 4 + 2 * i, XH, XL)

            def to_rows(k):
                pe.wait_ge(ss(s, "wt"), at(s, "wt", k + 1))
                if k >= 1:
                    pe.wait_ge(ss(s, "mt"), at(s, "mt", k))
                for g in range(GS):
                    mm = pe.transpose(bank[4 + g // 4][:, g % 4 * P:(g % 4 + 1) * P],
                                      Wt[:, g].rearrange("p s h -> p (s h)"), ident[:, :])
                mm.then_inc(ss(s, "w_t"), 1)
                if k == 0:
                    pe.wait_ge(ss(s, "c_cp"), at(s, "c_cp", 4))
                    pe.wait_ge(ss(s, "small"), at(s, "small", 1))
                for g in range(GS):
                    mm = pe.matmul(bank[6][:, g * GCH:(g + 1) * GCH], Wt[:, g].rearrange("p s h -> p (s h)"),
                                   C1[:, k * GS + g, :], start=True, stop=True)
                mm.then_inc(ss(s, "kk"), 1)

            def toeplitz(k):
                pe.wait_ge(ss(s, "ks"), at(s, "ks", k + 1))
                pe.wait_ge(ss(s, "w1"), at(s, "w1", k + 1))
                for t in range(CL):
                    c = S5_EYE + t * GCH
                    mm = pe.matmul(bank[4 + t // 4][:, t % 4 * P:(t % 4 + 1) * P], s5c[:, c:c + P],
                                   KS[:, :, :].rearrange("p g h -> p (g h)"), start=True, stop=True)
                mm.then_inc(ss(s, "tz"), 1)

            def inputs(k):
                pe.wait_ge(ss(s, "u_in"), at(s, "u_in", 16 * (k + 1)))
                pe.wait_ge(ss(s, "w1"), at(s, "w1", k + 1))
                if k >= 1:
                    pe.wait_ge(ss(s, "v"), at(s, "v", k))
                for i in range(2):
                    for g in range(GS):
                        mm = pe.matmul(bank[i][:, g * NC:(g + 1) * NC], W1[:, g, 64 * i:64 * i + P], U[:, k % 2, g, :],
                                       start=True, stop=True)
                mm.then_inc(ss(s, "s"), 1)

            to_rows(0)
            toeplitz(0)
            pe.wait_ge(acc_read, j0 + 8)
            inputs(0)
            for k in range(KD):
                if k + 1 < KD:
                    to_rows(k + 1)
                pe.wait_ge(ss(s, "z"), at(s, "z", k + 1))
                pe.matmul(bank[2][:, :], s5c[:, S5_SWAP:S5_SWAP + P], work2[:, 0, :], start=True, stop=True)\
                  .then_inc(ss(s, "zswap"), 1)
                if k + 1 < KD:
                    toeplitz(k + 1)
                    inputs(k + 1)
                pe.wait_ge(ss(s, "mt"), at(s, "mt", k + 1))
                pe.wait_ge(ss(s, "g1"), at(s, "g1", k + 1))
                pe.wait_ge(ss(s, "x"), at(s, "x", k + 1))
                if k >= 1:
                    pe.wait_ge(ss(s, "ys"), at(s, "ys", k))
                for g in range(GS):
                    out = bank[3][:, g * NC:(g + 1) * NC]
                    pe.matmul(out, MT[:, g].rearrange("p t h -> p (t h)"), U[:, k % 2, g, :], start=True, stop=False)
                    mm = pe.matmul(out, G1[:, g].rearrange("p t h -> p (t h)"),
                                   work2[:, 1, g * NC:(g + 1) * NC], start=False, stop=True)
                mm.then_inc(ss(s, "ydone"), 1)
            for i in range(4):
                pe_block256(pe, b0 + 4 + i, i % 2, j0 + 8 + 2 * i, XH, XL, arrive=(s, "gl") if i == 0 else None)
            out_pe(pe, s, b0 + 8, j0 + 16, (s, "l2"))

        def s5_act(act, s):
            b0, j0, s0 = first_block[s], tiles_before[s], first_step[s]
            pre, post = gains(s)
            pre_act(act, s, pre, b0 + 1)
            rms_act(act, s, "")
            split_h(act, b0 + 2, 0, 16, s0 + 2)
            split_h(act, b0 + 3, 1, 16, s0 + 4)
            act.wait_ge(ss(s, "par_t"), at(s, "par_t", 1))
            act.activation(sm[:, 2, :], bank[5][:, 128:192], ACT.Exp).then_inc(ss(s, "dt"), 1)
            act.wait_ge(ss(s, "m_th"), at(s, "m_th", 1))
            act.activation(sm[:, 12, :], sm[:, 3, :], ACT.Exp).then_inc(ss(s, "ex"), 1)
            act.wait_ge(ss(s, "red"), at(s, "red", 1))
            act.activation(sm[:, 13, :], sm[:, 11, :], ACT.Sin, scale=0.5).then_inc(ss(s, "half"), 1)
            act.wait_ge(ss(s, "phj"), at(s, "phj", 1))
            act.activation(CSJ[:, :, :], CSJ[:, :, :], ACT.Sin, scale=TURN)
            act.activation(SNJ[:, :, :], SNJ[:, :, :], ACT.Sin, scale=TURN).then_inc(ss(s, "sinj"), 1)

            def waves(k):
                act.wait_ge(ss(s, "ph"), at(s, "ph", k + 1))
                act.activation(COS[:, k % 2], COS[:, k % 2], ACT.Sin, scale=TURN)
                act.activation(SIN[:, k % 2], SIN[:, k % 2], ACT.Sin, scale=s5c[:, S5_SGN + 2:S5_SGN + 3])\
                   .then_inc(ss(s, "waves"), 1)

            def rows(k):
                act.wait_ge(ss(s, "w_t"), at(s, "w_t", k + 1))
                if k >= 1:
                    act.wait_ge(ss(s, "s"), at(s, "s", k))
                for b in range(2):
                    v = bank[4 + b][:, :].rearrange("p (g n) -> p g n", g=4)
                    act.activation(W1[:, 4 * b:4 * b + 4, 0:P], v, ACT.Copy)
                    ins = act.activation(W1[:, 4 * b:4 * b + 4, P:192], v[:, :, 0:64], ACT.Copy)
                ins.then_inc(ss(s, "w1"), 1)
                act.wait_ge(ss(s, "kk"), at(s, "kk", k + 1))
                if k >= 1:
                    act.wait_ge(ss(s, "tz"), at(s, "tz", k))
                act.activation(KS[:, :, :], bank[6][:, 0:P].rearrange("p (g h) -> p g h", g=GS), ACT.Copy)\
                   .then_inc(ss(s, "ks"), 1)

            def kernel_copy(k):
                act.wait_ge(ss(s, "tz"), at(s, "tz", k + 1))
                if k >= 1:
                    act.wait_ge(ss(s, "ydone"), at(s, "ydone", k))
                for b in range(2):
                    ins = act.activation(MT[:, :, 4 * b:4 * b + 4, :].rearrange("p g t h -> p t g h"),
                                         bank[4 + b][:, :].rearrange("p (t g h) -> p t g h", t=4, g=GS), ACT.Copy)
                ins.then_inc(ss(s, "mt"), 1)

            waves(0)
            rows(0)
            kernel_copy(0)
            waves(1)
            for k in range(KD):
                if k + 1 < KD:
                    rows(k + 1)
                if k + 2 < KD:
                    waves(k + 2)
                act.wait_ge(ss(s, "ydone"), at(s, "ydone", k + 1))
                if k >= 1:
                    act.wait_ge(ss(s, "y_out"), at(s, "y_out", 16 * CL * k))
                act.activation(YS[:, :, :], bank[3][:, :].rearrange("p (g c) -> p g c", g=GS), ACT.Copy)\
                   .then_inc(ss(s, "ys"), 1)
                if k + 1 < KD:
                    kernel_copy(k + 1)
            for k in range(KD):
                act.wait_ge(ss(s, "yd"), at(s, "yd", k + 1))
                act.activation(UN[:, k, :].rearrange("p (c t) -> p c t", t=CL), YR[:, k].rearrange("p t c -> p c t"),
                               ACT.Gelu_apprx_tanh).then_inc(ss(s, "gel"), 1)
                act.wait_ge(ss(s, "gel"), at(s, "gel", k + 1))
                act.activation(XH[:, k, :], UN[:, k, :], ACT.Copy).then_inc(ss(s, "gh"), 1)
            split_h(act, b0 + 4, 0, 16, s0 + 6)
            split_h(act, b0 + 5, 1, 16, s0 + 8)
            for i in range(4):
                for o in (2 * i, 2 * i + 1):
                    act.wait_ge(mm_done, s0 + 8 + o + 1)
                    if o >= 2:
                        act.wait_ge(ss(s, "zz"), at(s, "zz", o - 1))
                    act.activation(work1[:, o % 2, :], bank[2 * (i % 2) + o % 2][:, :], ACT.Sigmoid,
                                   bias=col("s5_b_glu_2", o)).then_inc(acc_read, 1)
                split_h(act, b0 + 6 + i, i % 2, 16, s0 + 10 + 2 * i)
            for k in range(KD):
                act.wait_ge(ss(s, "zz"), at(s, "zz", k + 1))
                act.activation(XH[:, k, :], UN[:, k, :], ACT.Copy).then_inc(ss(s, "h2"), 1)
            out_act(act, s, b0 + 8, j0 + 16, s0 + 16, Y5)

        def phases(eng, s, k):
            jc = s5c[:, S5_JC:S5_JC + NC + 1].unsqueeze(1).to_broadcast([P, GS, NC + 1])
            g = slice(k * GS, (k + 1) * GS)
            fh, fl = (sm[:, n, g].unsqueeze(2).to_broadcast([P, GS, NC + 1]) for n in (9, 10))
            a, n = PHA[:, :, :], PHN[:, :, :]
            eng.tensor_tensor(a, fh, jc, ALU.mult)
            eng.drain()
            eng.tensor_scalar(n, a, ROUND, -ROUND, ALU.add, ALU.add)
            eng.drain()
            eng.tensor_tensor(a, a, n, ALU.subtract)
            eng.tensor_tensor(SIN[:, k % 2], fl, jc, ALU.mult)
            eng.drain()
            eng.tensor_tensor(a, a, SIN[:, k % 2], ALU.add)
            eng.drain()
            eng.tensor_scalar(n, a, ROUND, -ROUND, ALU.add, ALU.add)
            eng.tensor_scalar(COS[:, k % 2], a, 0.25, None, ALU.add)
            eng.drain()
            eng.tensor_tensor(SIN[:, k % 2], a, n, ALU.subtract)
            eng.drain()
            eng.tensor_scalar(a, COS[:, k % 2], ROUND, -ROUND, ALU.add, ALU.add)
            eng.drain()
            eng.tensor_tensor(COS[:, k % 2], COS[:, k % 2], a, ALU.subtract).then_inc(ss(s, "ph"), 1)
            eng.drain()

        def s5_dve(dve, s):
            b0, j0, s0 = first_block[s], tiles_before[s], first_step[s]
            pre, post = gains(s)
            pre_dve(dve, s, pre)
            split_l(dve, b0 + 1, 1, 16)
            rstd_dve(dve, s, "")

            def u_tile(o):
                dve.wait_ge(mm_done, s0 + o + 1)
                dve.tensor_tensor(UN[:, o, :], bank[2 * (o // 2 % 2) + o % 2][:, :], rstd[:, :], ALU.mult)\
                   .then_inc(acc_read, 1)
                dve.drain()
                if o >= 1:
                    dve.wait_ge(ss(s, "u_out"), at(s, "u_out", 16 * GS * o))
                for t in range(CL):
                    q = CL - 1 - t
                    ins = dve.tensor_copy(rms[:, q * NC:(q + 1) * NC], UN[:, o, t:T:CL])
                ins.then_inc(ss(s, "us"), 1)

            def v(i):
                return sm[:, i, :]

            def two(ins):
                dve.drain()

            def ts(out, in0, a, b, op0, op1=None):
                if op1 is None:
                    two(dve.tensor_scalar(out, in0, a, None, op0))
                else:
                    two(dve.tensor_scalar(out, in0, a, b, op0, op1))

            def tt(out, a, b, op):
                two(dve.tensor_tensor(out, a, b, op))

            def stt(out, a, c, b, op0, op1):
                two(dve.scalar_tensor_tensor(out, a, c, b, op0, op1))

            u_tile(0)
            u_tile(1)
            split_l(dve, b0 + 2, 0, 16)
            u_tile(2)
            u_tile(3)
            split_l(dve, b0 + 3, 1, 16)
            for n in range(4):
                dve.wait_ge(ss(s, "c_t"), at(s, "c_t", n + 1))
                dst = (C1, C2)[n // 2][:, 32 * (n % 2):32 * (n % 2) + 32, :].rearrange("p g h -> p (g h)")
                sgn = s5c[:, S5_SGN + 1:S5_SGN + 2] if n < 2 else -1.0
                dve.tensor_scalar(dst, bank[4 + 2 * (n % 2)][:, :], sgn, None, ALU.mult).then_inc(ss(s, "c_cp"), 1)
            AR, AI, DT, M, TH, MC, EM, T0, T1, FH, FL, RED, EX, S2, FR, FI, MAG, PW, NR, DEN = range(20)
            dve.wait_ge(ss(s, "dt"), at(s, "dt", 1))
            dve.tensor_copy(v(AR), bank[5][:, 0:64])
            dve.tensor_copy(v(AI), bank[5][:, 64:128])
            dve.drain()
            dve.tensor_tensor(v(M), v(DT), v(AR), ALU.mult)
            tt(v(TH), v(DT), v(AI), ALU.mult)
            dve.nop().then_inc(ss(s, "m_th"), 1)
            ts(v(MC), v(M), -0.5, 0.5, ALU.max, ALU.min)
            ts(v(T0), v(MC), 1.0 / 8, 1.0, ALU.mult, ALU.add)
            for n in range(7, 1, -1):
                tt(v(T0), v(T0), v(MC), ALU.mult)
                ts(v(T0), v(T0), 1.0 / n, 1.0, ALU.mult, ALU.add)
            tt(v(EM), v(T0), v(MC), ALU.mult)
            ts(v(T1), v(TH), 1 / PI2, ROUND, ALU.mult, ALU.add)
            ts(v(T1), v(T1), -ROUND, None, ALU.add)
            stt(v(RED), v(T1), -PI2_A, v(TH), ALU.mult, ALU.add)
            stt(v(RED), v(T1), -PI2_B, v(RED), ALU.mult, ALU.add)
            stt(v(RED), v(T1), -PI2_C, v(RED), ALU.mult, ALU.add)
            dve.nop().then_inc(ss(s, "red"), 1)
            ts(v(T1), v(RED), 2.0 ** 13 / PI2, ROUND, ALU.mult, ALU.add)
            ts(v(FH), v(T1), -ROUND, 2.0 ** -13, ALU.add, ALU.mult)
            stt(v(T0), v(FH), -PI2_A, v(RED), ALU.mult, ALU.add)
            stt(v(T0), v(FH), -PI2_B, v(T0), ALU.mult, ALU.add)
            stt(v(T0), v(FH), -PI2_C, v(T0), ALU.mult, ALU.add)
            ts(v(FL), v(T0), 1 / PI2, None, ALU.mult)
            dve.nop().then_inc(ss(s, "frac"), 1)
            J = CL + 1
            pa = work1[:, :, :].rearrange("p a n -> p (a n)")[:, 0:J * GROUPS].rearrange("p (j g) -> p j g", j=J)
            pn = work2[:, :, :].rearrange("p a n -> p (a n)")[:, 0:J * GROUPS].rearrange("p (j g) -> p j g", j=J)
            jj = s5c[:, 0:J].unsqueeze(2).to_broadcast([P, J, GROUPS])
            tt(pa, v(FH).unsqueeze(1).to_broadcast([P, J, GROUPS]), jj, ALU.mult)
            ts(pn, pa, ROUND, -ROUND, ALU.add, ALU.add)
            tt(pa, pa, pn, ALU.subtract)
            tt(pn, v(FL).unsqueeze(1).to_broadcast([P, J, GROUPS]), jj, ALU.mult)
            tt(pa, pa, pn, ALU.add)
            ts(pn, pa, ROUND, -ROUND, ALU.add, ALU.add)
            tt(SNJ[:, :, :], pa, pn, ALU.subtract)
            ts(pa, pa, 0.25, None, ALU.add)
            ts(pn, pa, ROUND, -ROUND, ALU.add, ALU.add)
            tt(CSJ[:, :, :], pa, pn, ALU.subtract)
            dve.nop().then_inc(ss(s, "phj"), 1)
            u_tile(4)
            dve.wait_ge(ss(s, "ex"), at(s, "ex", 1))
            ts(v(EX), v(EX), -1.0, None, ALU.add)
            tt(v(T0), v(EM), v(EX), ALU.subtract)
            tt(v(T1), v(MC), v(M), ALU.is_equal)
            tt(v(T0), v(T0), v(T1), ALU.mult)
            tt(v(EM), v(EX), v(T0), ALU.add)
            ts(v(MAG), v(EM), 1.0, None, ALU.add)
            dve.wait_ge(ss(s, "half"), at(s, "half", 1))
            tt(v(T0), v(S2), v(S2), ALU.mult)
            dve.wait_ge(ss(s, "sinj"), at(s, "sinj", 1))
            tt(v(NR), v(EM), CSJ[:, 1, :], ALU.mult)
            stt(v(NR), v(T0), -2.0, v(NR), ALU.mult, ALU.add)
            two(dve.tensor_copy(v(PW), v(MAG)))
            for j in range(1, J):
                dve.tensor_tensor(CSJ[:, j, :], CSJ[:, j, :], v(PW), ALU.mult)
                dve.tensor_tensor(SNJ[:, j, :], SNJ[:, j, :], v(PW), ALU.mult)
                dve.drain()
                if j < CL:
                    tt(v(PW), v(PW), v(MAG), ALU.mult)
            tt(v(DEN), v(AR), v(AR), ALU.mult)
            tt(v(T0), v(AI), v(AI), ALU.mult)
            tt(v(DEN), v(DEN), v(T0), ALU.add)
            two(dve.reciprocal(v(T1), v(DEN)))
            tt(v(FR), v(NR), v(AR), ALU.mult)
            tt(v(T0), SNJ[:, 1, :], v(AI), ALU.mult)
            tt(v(FR), v(FR), v(T0), ALU.add)
            tt(v(FR), v(FR), v(T1), ALU.mult)
            tt(v(FI), SNJ[:, 1, :], v(AR), ALU.mult)
            tt(v(T0), v(NR), v(AI), ALU.mult)
            tt(v(FI), v(FI), v(T0), ALU.subtract)
            tt(v(FI), v(FI), v(T1), ALU.mult)
            dve.nop().then_inc(ss(s, "small0"), 1)
            u_tile(5)
            dve.wait_ge(ss(s, "b_in"), at(s, "b_in", 64))
            ts(B2[:, :, :], B2[:, :, :], s5c[:, S5_SGN:S5_SGN + 1], None, ALU.mult)
            shape = [P, GROUPS, GCH]
            fr, fi = (v(n).unsqueeze(2).to_broadcast(shape) for n in (FR, FI))
            t1 = Wt[:, :, :, :].rearrange("p a b c -> p (a b c)").rearrange("p (g h) -> p g h", g=GROUPS)
            t2 = W1[:, :, :].rearrange("p a b -> p (a b)")[:, 0:1024].rearrange("p (g h) -> p g h", g=GROUPS)
            dve.tensor_tensor(t1, B2[:, :, :], fi, ALU.mult)
            tt(t2, B1[:, :, :], fi, ALU.mult)
            dve.tensor_tensor(B1[:, :, :], B1[:, :, :], fr, ALU.mult)
            tt(B2[:, :, :], B2[:, :, :], fr, ALU.mult)
            dve.tensor_tensor(B1[:, :, :], B1[:, :, :], t1, ALU.add)
            tt(B2[:, :, :], B2[:, :, :], t2, ALU.subtract)
            dve.nop().then_inc(ss(s, "small"), 1)

            def matrices(k):
                if k >= 1:
                    dve.wait_ge(ss(s, "kk"), at(s, "kk", k))
                for a in range(2):
                    g = k * GS + 4 * a
                    shape = [P, 4, CL, GCH]
                    er, ei = (x[:, 0:CL, g:g + 4].rearrange("p j g -> p g j").unsqueeze(3).to_broadcast(shape)
                              for x in (CSJ, SNJ))
                    b1, b2 = (x[:, g:g + 4, :].unsqueeze(2).to_broadcast(shape) for x in (B1, B2))
                    w = Wt[:, 4 * a:4 * a + 4]
                    dve.tensor_tensor(w, er, b1, ALU.mult)
                    dve.tensor_tensor(Wx[:, :, :, :], ei, b2, ALU.mult)
                    dve.drain()
                    ins = dve.tensor_tensor(w, w, Wx[:, :, :, :], ALU.add)
                    dve.drain()
                dve.nop().then_inc(ss(s, "wt"), 1)

            matrices(0)
            u_tile(6)
            matrices(1)
            u_tile(7)

            def flat(x):
                return x.rearrange("p g c -> p (g c)")

            for k in range(KD):
                cs, sn = COS[:, k % 2], SIN[:, k % 2]
                dve.wait_ge(ss(s, "waves"), at(s, "waves", k + 1))
                dve.wait_ge(ss(s, "rr"), at(s, "rr", k + 1))
                dve.wait_ge(ss(s, "s"), at(s, "s", k + 1))

                def gc(x):
                    return x.rearrange("p (g c) -> p g c", g=GS)

                if k >= 1:
                    dve.wait_ge(ss(s, "zswap"), at(s, "zswap", k))
                dve.tensor_tensor(gc(work1[:, 0, :]), gc(bank[0][:, :]), cs[:, :, 1:NC + 1], ALU.mult)
                dve.tensor_tensor(gc(work1[:, 1, :]), gc(bank[1][:, :]), sn[:, :, 1:NC + 1], ALU.mult)\
                   .then_inc(ss(s, "v"), 1)
                dve.drain()
                dve.tensor_tensor(work1[:, 0, :], work1[:, 0, :], work1[:, 1, :], ALU.add)
                dve.drain()
                dve.tensor_tensor_scan(work2[:, 0, :], flat(RR[:, :, :]), work1[:, 0, :], 0.0, ALU.mult, ALU.add)\
                   .then_inc(ss(s, "z"), 1)
                dve.wait_ge(ss(s, "zswap"), at(s, "zswap", k + 1))
                if k >= 1:
                    dve.wait_ge(ss(s, "ydone"), at(s, "ydone", k))
                x = gc(work2[:, 1, :])
                dve.memset(x[:, :, 0:1], 0.0)
                dve.tensor_tensor(x[:, :, 1:NC], gc(work2[:, 0, :])[:, :, 0:NC - 1], cs[:, :, 1:NC], ALU.mult)
                dve.tensor_tensor(gc(ssq[:, :])[:, :, 1:NC], gc(bank[2][:, :])[:, :, 0:NC - 1], sn[:, :, 1:NC], ALU.mult)
                dve.drain()
                dve.tensor_tensor(x[:, :, 1:NC], x[:, :, 1:NC], gc(ssq[:, :])[:, :, 1:NC], ALU.subtract)\
                   .then_inc(ss(s, "x"), 1)
                dve.drain()
                if k + 2 < KD:
                    if k == 0:
                        dve.wait_ge(ss(s, "ph"), at(s, "ph", 2))
                    phases(dve, s, k + 2)
                    matrices(k + 2)
            for k in range(KD):
                dve.wait_ge(ss(s, "y_in"), at(s, "y_in", 16 * (k + 1)))
                dve.scalar_tensor_tensor(YR[:, k], UN[:, k, :].rearrange("p (c t) -> p t c", t=CL), col("s5_d_2", k),
                                         YR[:, k], ALU.mult, ALU.add).then_inc(ss(s, "yd"), 1)
            for k in range(KD):
                dve.wait_ge(ss(s, "gh"), at(s, "gh", k + 1))
                dve.tensor_tensor(XL[:, k, :], UN[:, k, :], XH[:, k, :].bitcast(F32), ALU.subtract)\
                   .then_inc(ss(s, "gl"), 1)
            split_l(dve, b0 + 4, 0, 16)
            split_l(dve, b0 + 5, 1, 16)
            for i in range(4):
                for o in (2 * i, 2 * i + 1):
                    dve.wait_ge(acc_read, j0 + 8 + o + 1)
                    dve.tensor_tensor(UN[:, o, :], UN[:, o, :], work1[:, o % 2, :], ALU.mult).then_inc(ss(s, "zz"), 1)
                split_l(dve, b0 + 6 + i, i % 2, 16)
            for k in range(KD):
                dve.wait_ge(ss(s, "h2"), at(s, "h2", k + 1))
                dve.tensor_tensor(XL[:, k, :], UN[:, k, :], XH[:, k, :].bitcast(F32), ALU.subtract)\
                   .then_inc(ss(s, "l2"), 1)
            out_dve(dve, s, b0 + 8, j0 + 16, s0 + 16, Y5, post)

        def s5_pool(pool, s):
            sum_pool(pool, s, "sq_in", "sq_use")
            pool.wait_ge(ss(s, "frac"), at(s, "frac", 1))
            pool.memset(RR[:, :, 0:1], 0.0)

            def outmat(k):
                if k >= 1:
                    pool.wait_ge(ss(s, "ydone"), at(s, "ydone", k))
                for a in range(2):
                    g = k * GS + 4 * a
                    shape = [P, 4, CL, GCH]
                    er, ei = (x[:, 1:CL + 1, g:g + 4].rearrange("p j g -> p g j").unsqueeze(3).to_broadcast(shape)
                              for x in (CSJ, SNJ))
                    c1, c2 = (x[:, g:g + 4, :].unsqueeze(2).to_broadcast(shape) for x in (C1, C2))
                    w = G1[:, 4 * a:4 * a + 4]
                    pool.tensor_tensor(w, er, c1, ALU.mult)
                    pool.tensor_tensor(Gx[:, :, :, :], ei, c2, ALU.mult)
                    pool.drain()
                    pool.tensor_tensor(w, w, Gx[:, :, :, :], ALU.add)
                    pool.drain()
                pool.nop().then_inc(ss(s, "g1"), 1)

            def decay(k):
                if k >= 1:
                    pool.wait_ge(ss(s, "z"), at(s, "z", k))
                pool.tensor_copy(RR[:, :, 1:NC], sm[:, 17, k * GS:(k + 1) * GS].unsqueeze(2).to_broadcast([P, GS, NC - 1]))\
                    .then_inc(ss(s, "rr"), 1)
                pool.drain()

            phases(pool, s, 0)
            pool.wait_ge(ss(s, "small0"), at(s, "small0", 1))
            decay(0)
            pool.wait_ge(ss(s, "small"), at(s, "small", 1))
            outmat(0)
            phases(pool, s, 1)
            for k in range(1, KD):
                decay(k)
                outmat(k)
            sum_pool(pool, s, "ysq_in", "ysq_use")
            post_pool(pool, s)

        STAGE = {"attn": (attn_sp, attn_pe, attn_act, attn_dve, attn_pool), "s5": (s5_sp, s5_pe, s5_act, s5_dve, s5_pool),
                 "ffn": (ffn_sp, ffn_pe, ffn_act, ffn_dve, ffn_pool),
                 "conv": (conv_sp, conv_pe, conv_act, conv_dve, conv_pool)}

        block = ctx.enter_context(nc.Block())
        x_rows = io["x"][0].rearrange("(t p) d -> p t d", p=P)
        out_rows = io["out"][0].rearrange("(t p) d -> p t d", p=P)

        @block.sync
        def _(sp):
            sp.dma_start(XN[:, :, :], x_rows).then_inc(xn_in, 16)
            for n, group in enumerate(VEC_ROWS):
                at = 0
                for name, rows in group:
                    src = io[name]
                    if len(src.shape) == 3:
                        src = src.rearrange("l n (k q) -> (l n k) q", q=P)
                    else:
                        src = src.rearrange("l (k q) -> (l k) q", q=P)
                    sp.dma_start(vrow[at:at + rows, n, :], src).then_inc(vec_in, 16)
                    at += rows
            for name, row in HEAD_ROWS:
                for h in range(2):
                    sp.dma_start(vrow[row:row + 2, 1, 64 * h:64 * h + 64], io[name]).then_inc(vec_in, 16)
            sp.dma_start(lamrow[0:1, :, :], io["diff_lambda"].rearrange("(o l) a d -> o l (a d)", o=1))\
              .then_inc(vec_in, 16)
            dw = io["cv_dw_2"].rearrange("l j (k q) -> (l j k) q", q=P)
            for n in range(2):
                sp.dma_start(vrow[0:DW_ROWS, 2 + n, :], dw[n * DW_ROWS:(n + 1) * DW_ROWS, :]).then_inc(vec_in, 16)
            for s in stages:
                STAGE[kind(s)][0](sp, s)
            sp.wait_ge(o_cp, 4 * KD)
            sp.dma_start(out_rows, XN[:, :, :]).then_inc(stored, 16)
            sp.wait_ge(stored, 16)

        @block.gpsimd
        def _(pool):
            pool.memset(ident[:, :], 0.0).then_inc(ident_0, 1)
            pool.memset(ones[:, :], 1.0)
            pool.memset(eps_c[:, :], EPS)
            pool.wait_ge(ident_0, 1)
            pool.affine_select(out=ident[:, :], in_=ident[:, :], compare_op=ALU.not_equal, fill=1.0, base=0,
                               pattern=[[-1, P]], channel_multiplier=1)
            pool.drain()
            pool.nop().then_inc(ident_ok, 1)
            for s in stages:
                STAGE[kind(s)][4](pool, s)

        @block.tensor
        def _(pe):
            pe.wait_ge(ident_ok, 1)
            pe.wait_ge(vec_in, 16 * VEC_DMAS)
            for n in range(2):
                r = VEC_N[n]
                pe.transpose(bank[n][:, 0:r], vrow[0:r, n, :], ident[0:r, 0:r]).then_inc(vec_t, 1)
            for n in range(2):
                pe.transpose(bank[6 + n][:, 0:DW_ROWS], vrow[0:DW_ROWS, 2 + n, :], ident[0:DW_ROWS, 0:DW_ROWS])\
                  .then_inc(vec_t, 1)
            pe.matmul(bank[5][:, 0:2 * P], ones[0:1, :], lamrow[0:1, :, :], start=True, stop=True).then_inc(vec_t, 1)
            pe.wait_ge(xn_in, 16)
            for k in range(KD):
                if k >= 3:
                    pe.wait_ge(x_ok, k - 2)
                for t in range(4):
                    mm = pe.transpose(bank[2 + k % 3][:, t * P:(t + 1) * P], XN[:, t, k * P:(k + 1) * P], ident[:, :])
                mm.then_inc(x_tr, 1)
            for s in stages:
                STAGE[kind(s)][1](pe, s)
            for k in range(KD):
                x_final(pe, None, k)
                for t in range(4):
                    n = k * 4 + t
                    if n >= 4:
                        pe.wait_ge(o_cp, n - 3)
                    pe.transpose(bank[n % 4][:, 0:P], X[:, k, t * P:(t + 1) * P], ident[:, :]).then_inc(o_tr, 1)

        @block.scalar
        def _(act):
            act.wait_ge(ident_ok, 1)
            act.wait_ge(vec_ok, 2)
            act.activation(lamv[:, :, 2:4], lamv[:, :, 0:2], ACT.Exp).then_inc(lam_exp, 1)
            split_h(act, 0, 0, cells[0], 0)
            for s in stages:
                STAGE[kind(s)][2](act, s)

        @block.vector
        def _(dve):
            for n in range(2):
                dve.wait_ge(vec_t, n + 1)
                dve.tensor_copy(vecT[:, 128 * n:128 * n + VEC_N[n]], bank[n][:, 0:VEC_N[n]])
            for n in range(2):
                dve.wait_ge(vec_t, 3 + n)
                dve.tensor_copy(dwT[:, n * DW_ROWS:(n + 1) * DW_ROWS], bank[6 + n][:, 0:DW_ROWS])
            dve.wait_ge(vec_t, 5)
            dve.tensor_copy(lamb[:, :, :], bank[5][:, 0:2 * P].rearrange("p (l n) -> p l n", l=2))
            dve.drain()
            for n in (0, 2, 3, 5):
                g = vecT[:, COL["norm_post_2"] + KD * n:COL["norm_post_2"] + KD * (n + 1)]
                dve.tensor_scalar(g, g, 0.5, None, ALU.mult)
            for l in range(2):
                for i in range(2):
                    dve.tensor_tensor(work1[:, 0, 64 * l + 32 * i:64 * l + 32 * i + 32], lamb[:, l, 64 * i:64 * i + 32],
                                      lamb[:, l, 64 * i + 32:64 * i + 64], ALU.mult)
            dve.drain()
            dve.tensor_reduce(lamv[:, :, 0:2], work1[:, 0, 0:P].rearrange("p (l i d) -> p l i d", l=2, i=2), AX, ALU.add)
            c1 = 128 + VEC_ROW1
            dve.tensor_copy(headg[:, :], vecT[:, c1:c1 + 6])
            dve.drain()
            for l in range(2):
                dve.tensor_scalar(headg[:, l:l + 1], headg[:, l:l + 1], 1.0 - LAMBDA0[l], None, ALU.mult)
            dve.drain()
            dve.nop().then_inc(vec_ok, 2)
            dve.wait_ge(lam_exp, 1)
            dve.tensor_tensor(nlam[:, :], lamv[:, :, 3], lamv[:, :, 2], ALU.subtract)
            dve.drain()
            for l in range(2):
                dve.tensor_scalar(nlam[:, l:l + 1], nlam[:, l:l + 1], -LAMBDA0[l], None, ALU.add)
            for k in range(KD):
                dve.wait_ge(x_tr, k + 1)
                dve.tensor_copy(X[:, k, :], bank[2 + k % 3][:, :]).then_inc(x_ok, 1)
            split_l(dve, 0, 0, cells[0])
            for s in stages:
                STAGE[kind(s)][3](dve, s)
            for k in range(KD):
                for t in range(4):
                    n = k * 4 + t
                    dve.wait_ge(o_tr, n + 1)
                    dve.tensor_copy(XN[:, t, k * P:(k + 1) * P], bank[n % 4][:, 0:P]).then_inc(o_cp, 1)


INS = ["x", "mem", "pre_norm", "w_in", "diff_lambda", "diff_subln", "gqa_q_norm", "gqa_k_norm", "mem_norm", "w_mem_kv",
       "w_out", "post_norm", "norm_pre_2", "norm_post_2", "ffn_w1_2", "ffn_w3_2", "ffn_w2_2", "s5_w_in_2", "s5_a_re_2",
       "s5_a_im_2", "s5_log_dt_2", "s5_b_re_2", "s5_b_im_2", "s5_c_re_2", "s5_c_im_2", "s5_d_2", "s5_w_glu_2",
       "s5_b_glu_2", "s5_w_out_2", "cv_w_in_2", "cv_b_in_2", "cv_dw_2", "cv_dw_b_2", "cv_ln_g_2", "cv_ln_b_2",
       "cv_w_out_2", "cv_b_out_2"]


def kernel(**inputs):
    import concourse.bacc as bacc
    from concourse.bass_utils import run_bass_kernel_spmd

    nc = bacc.Bacc("TRN2", target_bir_lowering=False, num_devices=1)
    arrays, io = {}, {}
    given = {name: np.ascontiguousarray(inputs[name]) for name in INS}
    given.update(shape_tables())
    for name, a in given.items():
        arrays[f"in_{name}_dram"] = a
        io[name] = nc.dram_tensor(f"in_{name}_dram", a.shape, mybir.dt.from_np(a.dtype), kind="ExternalInput").ap()
    io["out"] = nc.dram_tensor("out_dram", (1, T, D), F32, kind="ExternalOutput").ap()
    program(nc, io)
    r = run_bass_kernel_spmd(nc, [arrays], core_ids=[0])
    return r.results[0]["out_dram"]
```
